# Optimizing a Trainium2 kernel written in Bass

```python
import math
import jax, jax.numpy as jnp
from jax import lax
import numpy as np

D_MODEL = 2048
BATCH = 1
SEQ = 256
DEPTH = 1

D_MIX = D_MODEL
D_SSM = D_MIX // 2
SSM_GROUP = 16
N_SSM_GROUPS = D_SSM // SSM_GROUP
SSM_STATE = 64
DT_MIN = 1e-3
DT_MAX = 1e-1

N_HEADS = 16
N_KV = 4
GQA_R = N_HEADS // N_KV
HEAD_DIM = (D_MIX - D_SSM) // N_HEADS
CMP_BLOCK = 32
CMP_STRIDE = 16
CMP_HIDDEN = 128
SEL_BLOCK = 64
SEL_TOP = 16
WINDOW = 512
Q_BLOCK = 128
SEL_RATIO = SEL_BLOCK // CMP_STRIDE
CMP_RATIO = CMP_BLOCK // CMP_STRIDE
FORCED_SCORE = 1e4

N_BUCKETS = 32
RPB_MAX_EXACT = 16
RPB_MAX_DIST = 1024

D_FF = ((8 * D_MODEL // 3 + 255) // 256) * 256
NORM_EPS = 1e-6

IN_SIZES = [D_SSM, N_HEADS * HEAD_DIM] + [N_KV * HEAD_DIM] * 6 + [3 * N_HEADS]
IN_COLS = int(sum(IN_SIZES))
IN_SPLITS = [int(v) for v in np.cumsum(IN_SIZES)[:-1]]

kernel_name = "hymba_s5_nsa_hybrid_trunk"

def rms_norm(x, g):
    xf = x.astype(jnp.float32)
    y = xf * lax.rsqrt(jnp.mean(xf * xf, axis=-1, keepdims=True) + NORM_EPS)
    return (y * g.astype(jnp.float32)).astype(x.dtype)

def masked_softmax(logits, mask):
    logits = jnp.where(mask, logits.astype(jnp.float32), -jnp.inf)
    m = jnp.max(logits, axis=-1, keepdims=True)
    m = jnp.where(jnp.isfinite(m), m, 0.0)
    e = jnp.exp(logits - m)
    return e / jnp.maximum(jnp.sum(e, axis=-1, keepdims=True), 1e-30)

def rel_bucket(dist):
    n = jnp.maximum(dist, 0)
    nf = jnp.maximum(n, 1).astype(jnp.float32)
    large = RPB_MAX_EXACT + (jnp.log(nf / RPB_MAX_EXACT) / math.log(RPB_MAX_DIST / RPB_MAX_EXACT)
                             * (N_BUCKETS - RPB_MAX_EXACT)).astype(jnp.int32)
    large = jnp.minimum(large, N_BUCKETS - 1)
    return jnp.where(n < RPB_MAX_EXACT, n, large)

def _complex_linear_combine(e1, e2):
    a1r, a1i, b1r, b1i = e1
    a2r, a2i, b2r, b2i = e2
    return (a2r * a1r - a2i * a1i,
            a2r * a1i + a2i * a1r,
            a2r * b1r - a2i * b1i + b2r,
            a2r * b1i + a2i * b1r + b2i)

def s5_glu(u, a_re, a_im, log_dt, b_re, b_im, c_re, c_im, d, w_glu, b_glu):
    B_, L_ = u.shape[:2]
    ug = u.astype(jnp.float32).reshape(B_, L_, N_SSM_GROUPS, SSM_GROUP)
    lam_re = jnp.minimum(a_re.astype(jnp.float32), -1e-4)
    lam_im = a_im.astype(jnp.float32)
    dt = jnp.exp(log_dt.astype(jnp.float32))[:, None]
    mag = jnp.exp(lam_re * dt)
    ab_re = mag * jnp.cos(lam_im * dt)
    ab_im = mag * jnp.sin(lam_im * dt)
    nr, ni = ab_re - 1.0, ab_im
    den = lam_re * lam_re + lam_im * lam_im
    f_re = (nr * lam_re + ni * lam_im) / den
    f_im = (ni * lam_re - nr * lam_im) / den
    br, bi = b_re.astype(jnp.float32), b_im.astype(jnp.float32)
    bb_re = f_re[..., None] * br - f_im[..., None] * bi
    bb_im = f_re[..., None] * bi + f_im[..., None] * br
    bu_re = jnp.einsum('blgh,gph->blgp', ug, bb_re)
    bu_im = jnp.einsum('blgh,gph->blgp', ug, bb_im)
    a_b_re = jnp.broadcast_to(ab_re, bu_re.shape)
    a_b_im = jnp.broadcast_to(ab_im, bu_im.shape)
    _, _, x_re, x_im = lax.associative_scan(_complex_linear_combine,
                                            (a_b_re, a_b_im, bu_re, bu_im), axis=1)
    y = (jnp.einsum('blgp,ghp->blgh', x_re, c_re.astype(jnp.float32))
         - jnp.einsum('blgp,ghp->blgh', x_im, c_im.astype(jnp.float32))
         + d.astype(jnp.float32).reshape(N_SSM_GROUPS, SSM_GROUP) * ug)
    y = jax.nn.gelu(y.reshape(B_, L_, D_SSM))
    ab = y @ w_glu.astype(jnp.float32) + b_glu.astype(jnp.float32)
    a, b = jnp.split(ab, 2, axis=-1)
    return (a * jax.nn.sigmoid(b)).astype(u.dtype)

def compress(k, pos, w1, w2):
    B_, L_ = k.shape[:2]
    c = k.reshape(B_, L_ // CMP_STRIDE, CMP_STRIDE, N_KV, HEAD_DIM)
    blocks = jnp.concatenate([c[:, :-1], c[:, 1:]], axis=2)
    blocks = blocks + pos[None, None, :, None, :]
    n_cmp = blocks.shape[1]
    flat = blocks.transpose(0, 1, 3, 2, 4).reshape(B_, n_cmp, N_KV, CMP_BLOCK * HEAD_DIM)
    return jax.nn.gelu(flat @ w1) @ w2

def nsa_mixer(q, kc, vc, ks, vs, kw, vw, gates,
              pos_k, w1_k, w2_k, pos_v, w1_v, w2_v, rpb_table):
    B_, L_ = q.shape[:2]
    n_qb = L_ // Q_BLOCK
    n_sel = L_ // SEL_BLOCK
    top = min(SEL_TOP, n_sel)
    kv_shape = (B_, L_, N_KV, HEAD_DIM)
    q = q.reshape(B_, L_, N_KV, GQA_R, HEAD_DIM) * (HEAD_DIM ** -0.5)
    gates = jax.nn.sigmoid(gates.astype(jnp.float32)).reshape(B_, L_, N_KV, GQA_R, 3)

    k_cmp = compress(kc.reshape(kv_shape), pos_k, w1_k, w2_k)
    v_cmp = compress(vc.reshape(kv_shape), pos_v, w1_v, w2_v)
    n_cmp = k_cmp.shape[1]
    cmp_end = jnp.arange(n_cmp) * CMP_STRIDE + (CMP_BLOCK - 1)

    k_sel_blk = ks.reshape(B_, n_sel, SEL_BLOCK, N_KV, HEAD_DIM).transpose(0, 3, 1, 2, 4)
    v_sel_blk = vs.reshape(B_, n_sel, SEL_BLOCK, N_KV, HEAD_DIM).transpose(0, 3, 1, 2, 4)
    pad_w = ((0, 0), (WINDOW, 0), (0, 0), (0, 0))
    k_win = jnp.pad(kw.reshape(kv_shape), pad_w)
    v_win = jnp.pad(vw.reshape(kv_shape), pad_w)

    table_gr = rpb_table.astype(jnp.float32).reshape(N_BUCKETS, N_KV, GQA_R)
    table_g = table_gr.transpose(1, 0, 2)

    qi = jnp.arange(Q_BLOCK)
    kj = jnp.arange(Q_BLOCK + WINDOW)
    win_dist = qi[:, None] + WINDOW - kj[None, :]
    win_rel_mask = (win_dist >= 0) & (win_dist < WINDOW)
    win_bias = table_gr[rel_bucket(win_dist)].transpose(2, 3, 0, 1)

    bidx = jnp.arange(B_)[:, None, None, None]
    gidx = jnp.arange(N_KV)[None, :, None, None]
    blk_ids = jnp.arange(n_sel)
    s_max = SEL_RATIO + CMP_RATIO - 2
    coefs = {}
    for m in range(SEL_RATIO):
        for n in range(CMP_RATIO):
            coefs[m + n] = coefs.get(m + n, 0) + 1
    span = SEL_RATIO * (n_sel - 1) + 1

    def block(j):
        t = j * Q_BLOCK + qi
        qb = lax.dynamic_slice_in_dim(q, j * Q_BLOCK, Q_BLOCK, axis=1)
        gb = lax.dynamic_slice_in_dim(gates, j * Q_BLOCK, Q_BLOCK, axis=1)

        cdist = t[:, None] - cmp_end[None, :]
        c_bias = table_gr[rel_bucket(cdist)].transpose(2, 3, 0, 1)
        c_logits = jnp.einsum('bqgrd,bngd->bgrqn', qb, k_cmp).astype(jnp.float32) + c_bias
        p_cmp = masked_softmax(c_logits, cdist >= 0)
        o_cmp = jnp.einsum('bgrqn,bngd->bqgrd', p_cmp.astype(v_cmp.dtype), v_cmp)

        imp = jnp.pad(p_cmp.sum(axis=2), ((0, 0), (0, 0), (0, 0), (s_max, SEL_RATIO)))
        p_slc = jnp.zeros(imp.shape[:-1] + (n_sel,), jnp.float32)
        for s, cnt in coefs.items():
            p_slc = p_slc + cnt * imp[..., s_max - s: s_max - s + span: SEL_RATIO]
        cur = t // SEL_BLOCK
        valid = blk_ids[None, :] * SEL_BLOCK <= t[:, None]
        forced = ((blk_ids[None, :] == 0) | (blk_ids[None, :] == cur[:, None])
                  | (blk_ids[None, :] == cur[:, None] - 1))
        score = jnp.where(valid, jnp.where(forced, FORCED_SCORE, p_slc), -1.0)
        top_score, idx = lax.top_k(score, top)
        ksel = k_sel_blk[bidx, gidx, idx].reshape(B_, N_KV, Q_BLOCK, top * SEL_BLOCK, HEAD_DIM)
        vsel = v_sel_blk[bidx, gidx, idx].reshape(B_, N_KV, Q_BLOCK, top * SEL_BLOCK, HEAD_DIM)
        spos = (idx[..., None] * SEL_BLOCK + jnp.arange(SEL_BLOCK)).reshape(B_, N_KV, Q_BLOCK, -1)
        sdist = t[None, None, :, None] - spos
        s_valid = jnp.repeat(top_score >= 0.0, SEL_BLOCK, axis=-1) & (sdist >= 0)
        s_bias = table_g[gidx, rel_bucket(sdist)].transpose(0, 1, 4, 2, 3)
        s_logits = jnp.einsum('bqgrd,bgqkd->bgrqk', qb, ksel).astype(jnp.float32) + s_bias
        p_sel = masked_softmax(s_logits, s_valid[:, :, None])
        o_sel = jnp.einsum('bgrqk,bgqkd->bqgrd', p_sel.astype(vsel.dtype), vsel)

        kwb = lax.dynamic_slice_in_dim(k_win, j * Q_BLOCK, Q_BLOCK + WINDOW, axis=1)
        vwb = lax.dynamic_slice_in_dim(v_win, j * Q_BLOCK, Q_BLOCK + WINDOW, axis=1)
        w_mask = win_rel_mask & (kj[None, :] >= WINDOW - j * Q_BLOCK)
        w_logits = jnp.einsum('bqgrd,bkgd->bgrqk', qb, kwb).astype(jnp.float32) + win_bias
        p_win = masked_softmax(w_logits, w_mask)
        o_win = jnp.einsum('bgrqk,bkgd->bqgrd', p_win.astype(vwb.dtype), vwb)

        out = gb[..., 0:1] * o_cmp + gb[..., 1:2] * o_sel + gb[..., 2:3] * o_win
        return out.reshape(B_, Q_BLOCK, N_HEADS * HEAD_DIM).astype(q.dtype)

    out = lax.map(block, jnp.arange(n_qb))
    return out.transpose(1, 0, 2, 3).reshape(B_, L_, N_HEADS * HEAD_DIM)

def swiglu(h, w_gate, w_up, w_down):
    return (jax.nn.silu(h @ w_gate) * (h @ w_up)) @ w_down

def setup_inputs(seed: int = 0) -> dict:
    key = jax.random.key(seed)
    ks = jax.random.split(key, 32)
    f32 = jnp.float32

    def nrm(k, shape, scale):
        return jax.random.normal(k, shape, f32) * scale

    G, P, H16 = N_SSM_GROUPS, SSM_STATE, SSM_GROUP
    n_idx = jnp.arange(P, dtype=f32)
    return {
        "x": nrm(ks[0], (BATCH, SEQ, D_MODEL), 1.0),
        "rpb_table": nrm(ks[1], (N_BUCKETS, N_HEADS), 0.5),
        "attn_norm": 1.0 + nrm(ks[2], (DEPTH, D_MODEL), 0.01),
        "ffn_norm": 1.0 + nrm(ks[3], (DEPTH, D_MODEL), 0.01),
        "final_norm": 1.0 + nrm(ks[4], (D_MODEL,), 0.01),
        "w_in": nrm(ks[5], (DEPTH, D_MODEL, IN_COLS), D_MODEL ** -0.5),
        "ssm_a_re": -0.5 + nrm(ks[6], (DEPTH, G, P), 0.01),
        "ssm_a_im": math.pi * n_idx[None, None, :] + nrm(ks[7], (DEPTH, G, P), 0.01),
        "ssm_log_dt": jax.random.uniform(ks[8], (DEPTH, G), f32, math.log(DT_MIN), math.log(DT_MAX)),
        "ssm_b_re": nrm(ks[9], (DEPTH, G, P, H16), (2 * H16) ** -0.5),
        "ssm_b_im": nrm(ks[10], (DEPTH, G, P, H16), (2 * H16) ** -0.5),
        "ssm_c_re": nrm(ks[11], (DEPTH, G, H16, P), 0.5),
        "ssm_c_im": nrm(ks[12], (DEPTH, G, H16, P), 0.5),
        "ssm_d": nrm(ks[13], (DEPTH, D_SSM), 1.0),
        "w_glu": nrm(ks[14], (DEPTH, D_SSM, 2 * D_SSM), D_SSM ** -0.5),
        "b_glu": nrm(ks[15], (DEPTH, 2 * D_SSM), 0.01),
        "cmp_pos_k": nrm(ks[16], (DEPTH, CMP_BLOCK, HEAD_DIM), 0.02),
        "cmp_w1_k": nrm(ks[17], (DEPTH, CMP_BLOCK * HEAD_DIM, CMP_HIDDEN), (CMP_BLOCK * HEAD_DIM) ** -0.5),
        "cmp_w2_k": nrm(ks[18], (DEPTH, CMP_HIDDEN, HEAD_DIM), CMP_HIDDEN ** -0.5),
        "cmp_pos_v": nrm(ks[19], (DEPTH, CMP_BLOCK, HEAD_DIM), 0.02),
        "cmp_w1_v": nrm(ks[20], (DEPTH, CMP_BLOCK * HEAD_DIM, CMP_HIDDEN), (CMP_BLOCK * HEAD_DIM) ** -0.5),
        "cmp_w2_v": nrm(ks[21], (DEPTH, CMP_HIDDEN, HEAD_DIM), CMP_HIDDEN ** -0.5),
        "w_out": nrm(ks[22], (DEPTH, D_MIX, D_MODEL), D_MIX ** -0.5),
        "w_ffn_gate": nrm(ks[23], (DEPTH, D_MODEL, D_FF), D_MODEL ** -0.5),
        "w_ffn_up": nrm(ks[24], (DEPTH, D_MODEL, D_FF), D_MODEL ** -0.5),
        "w_ffn_down": nrm(ks[25], (DEPTH, D_FF, D_MODEL), D_FF ** -0.5),
    }

def reference(x, rpb_table, attn_norm, ffn_norm, final_norm, w_in,
              ssm_a_re, ssm_a_im, ssm_log_dt, ssm_b_re, ssm_b_im, ssm_c_re, ssm_c_im, ssm_d,
              w_glu, b_glu, cmp_pos_k, cmp_w1_k, cmp_w2_k, cmp_pos_v, cmp_w1_v, cmp_w2_v,
              w_out, w_ffn_gate, w_ffn_up, w_ffn_down):
    for l in range(DEPTH):
        h = rms_norm(x, attn_norm[l])
        proj = h @ w_in[l]
        u, q, kc, vc, ks_, vs_, kw, vw, gates = jnp.split(proj, IN_SPLITS, axis=-1)
        y_ssm = s5_glu(u, ssm_a_re[l], ssm_a_im[l], ssm_log_dt[l], ssm_b_re[l], ssm_b_im[l],
                       ssm_c_re[l], ssm_c_im[l], ssm_d[l], w_glu[l], b_glu[l])
        y_nsa = nsa_mixer(q, kc, vc, ks_, vs_, kw, vw, gates,
                          cmp_pos_k[l], cmp_w1_k[l], cmp_w2_k[l],
                          cmp_pos_v[l], cmp_w1_v[l], cmp_w2_v[l], rpb_table)
        x = x + jnp.concatenate([y_ssm, y_nsa], axis=-1) @ w_out[l]
        h = rms_norm(x, ffn_norm[l])
        x = x + swiglu(h, w_ffn_gate[l], w_ffn_up[l], w_ffn_down[l])
    return rms_norm(x, final_norm)


_drawn_inputs = setup_inputs


def setup_inputs(seed=0):
    import zlib

    import numpy as np

    out = dict(_drawn_inputs(seed))
    spreads = {}
    factors = {'attn_norm': 8.0,
     'ffn_norm': 33.295,
     'final_norm': 32.787,
     'ssm_a_re': 64.0,
     'b_glu': 39.38,
     'cmp_pos_k': 8.0,
     'cmp_pos_v': 42.283}
    for name, (base, spread) in spreads.items():
        noise = np.random.default_rng([zlib.crc32(name.encode()), seed]).standard_normal(out[name].shape)
        drawn = base * np.exp(spread * noise) if base else spread * noise
        out[name] = __import__('jax').numpy.asarray(drawn.astype(out[name].dtype))
    for name, factor in factors.items():
        out[name] = (out[name] * factor).astype(out[name].dtype)
    return out
```

```python
from contextlib import ExitStack

import numpy as np

import concourse.bass as bass
from concourse import mybir

F32 = mybir.dt.float32
F32R = mybir.dt.float32r
ACT = mybir.ActivationFunctionType
ALU = mybir.AluOpType
AX_X = mybir.AxisListType.X
ds = bass.ds

P = 128
SEQ = 256
D_MODEL = 2048
D_FF = 5632
KT = D_MODEL // P
TT = SEQ // P
D_SSM = 1024
UT = D_SSM // P
GROUPS = 64
H = 16
NS = 64
G8 = P // H
STEP = 8
NCH = SEQ // STEP
HEADS = 16
NKV = 4
R = HEADS // NKV
DH = 64
CMP_STRIDE = 16
CMP_BLOCK = 32
NCMP = SEQ // CMP_STRIDE - 1
BUCKETS = 32
EPS = 1e-6
MASK = -1e30
SPAN = 384
PROJ_TILES = 28
GATE_COL = PROJ_TILES * P
NGATE = 3 * HEADS
V_ATTN, V_FFN, V_BGLU, V_D, NVEC = 0, 16, 32, 48, 56

IN_BODIES = PROJ_TILES // 4
GLU_BODIES = D_SSM // 256
OUT_BODIES = KT // 4
FFN_BODIES = D_FF // 256
DOWN_BODIES = D_FF // 512
GLU_0 = IN_BODIES
OUT_0 = GLU_0 + GLU_BODIES
FFN_0 = OUT_0 + OUT_BODIES
DOWN_0 = FFN_0 + FFN_BODIES

MAGIC = 12582912.0
PI = float(np.pi)
PI_IN = 3.1415925
TWO_PI_1 = 6.28125
TWO_PI_2 = float(np.float32(2 * np.pi - 6.28125))
TWO_PI_3 = float(2 * np.pi - 6.28125 - np.float64(np.float32(2 * np.pi - 6.28125)))

LO_CREDIT = 4
MM_CREDIT = 2
PROJ_CREDIT = 4
PAIR_CREDIT = 2


class Steps:

    def __init__(self, engine, sem):
        self.engine, self.sem, self.n = engine, sem, 0

    def __call__(self, instruction):
        instruction.then_inc(self.sem, 1)
        self.n = self.n + 1

    def wait(self):
        self.engine.wait_ge(self.sem, self.n)

    def then(self, instruction):
        self(instruction)
        self.wait()


def build(nc, x, rpb_table, attn_norm, ffn_norm, final_norm, w_in, a_re, a_im, log_dt, b_re, b_im, c_re, c_im,
          ssm_d, w_glu, b_glu, pos_k, w1_k, w2_k, pos_v, w1_v, w2_v, w_out, w_gate, w_up, w_down,
          selectors, onehot, out):
    bias_rows = nc.dram_tensor("bias_rows", [HEADS, SPAN], F32, kind="Internal").ap()
    bias_copies = nc.dram_tensor("bias_copies", [P, HEADS, SPAN], F32, kind="Internal").ap()

    with ExitStack() as ctx:
        place = [(nc.sbuf_base + 63) // 64 * 64]

        def lasting(name, shape, dtype=F32):
            t = nc.alloc_sbuf_tensor_at(name, shape, dtype, offset=place[0])
            place[0] += (4 * int(np.prod(shape[1:])) + 31) // 32 * 32
            return t

        def sem(name):
            return ctx.enter_context(nc.semaphore(name))

        raw = {"A": lasting("raw_a", [P, 4096]), "B": lasting("raw_b", [P, 4096])}
        w_hi = lasting("w_hi", [P, 2, 2048], F32R)
        w_lo = lasting("w_lo", [P, 2, 2048], F32R)
        act_hi = lasting("act_hi", [P, 4, SEQ], F32R)
        act_lo = lasting("act_lo", [P, 4, SEQ], F32R)
        pair = lasting("pair", [P, 2, SEQ])
        bias_sb = nc.alloc_sbuf_tensor_at("bias_sb", [HEADS, SPAN], F32, offset=place[0] - 4 * 2 * SEQ)
        proj_at = place[0]
        proj = lasting("proj", [P, PROJ_TILES, SEQ])
        shift = lasting("shift", [P, 240])
        select = lasting("select", [P, G8, 240])
        swap = lasting("swap", [P, P])
        vec_rows = lasting("vec_rows", [NVEC, P])
        vec = lasting("vec", [P, NVEC])
        gates = lasting("gates", [P, TT, NGATE])
        stat = lasting("stat", [P, 16])
        ssm_cols = lasting("ssm_cols", [P, 7, GROUPS])
        zone = place[0]
        ident = shift[:, 112:112 + P]

        def placed(start):
            where = [zone + int(start * 1024)]

            def put(name, shape, dtype=F32):
                t = nc.alloc_sbuf_tensor_at(name, shape, dtype, offset=where[0])
                where[0] += (4 * int(np.prod(shape[1:])) + 31) // 32 * 32
                assert where[0] <= nc.sbuf_usable_end, (name, where[0], nc.sbuf_usable_end)
                return t
            return put

        put = placed(0)
        h_hi = put("h_hi", [P, KT, SEQ], F32R)
        h_lo = put("h_lo", [P, KT, SEQ], F32R)
        xt = put("xt", [P, TT, D_MODEL])
        xs = put("xs", [P, TT, D_MODEL])
        put = placed(85)
        gate_raw = put("gate_raw", [P, KT, NGATE])
        gate_hi = put("gate_hi", [P, KT, NGATE], F32R)
        gate_lo = put("gate_lo", [P, KT, NGATE], F32R)
        put = placed((proj_at - zone) / 1024 + 16)
        lam = put("lam", [GROUPS, 2, P])
        dt_row = put("dt_row", [GROUPS, 8])
        ang = put("ang", [GROUPS, 2, P])
        rnd = put("rnd", [GROUPS, 2, P])
        red = put("red", [GROUPS, 2, P])
        sin_cos = put("sin_cos", [GROUPS, 2, 2, P])
        mag = put("mag", [GROUPS, P])
        ssm_rows = put("ssm_rows", [GROUPS, 7, P])
        tab_rows = put("tab_rows", [BUCKETS + 1, HEADS])
        hot = put("hot", [BUCKETS + 1, SPAN])
        assert 4 * (int(np.prod(hot.shape[1:]))) <= 4 * 512
        put = placed(32)
        pow_re = put("pow_re", [P, STEP + 1, GROUPS])
        pow_im = put("pow_im", [P, STEP + 1, GROUPS])
        rot_c = put("rot_c", [P, GROUPS, NCH])
        rot_s = put("rot_s", [P, GROUPS, NCH])
        bb = put("bb", [P, GROUPS, H])
        bbw = put("bbw", [P, GROUPS, H])
        cs = put("cs", [P, GROUPS, H])
        cw = put("cw", [P, GROUPS, H])
        put = placed(69)
        cn = put("cn", [P, 2, UT, P])
        bs_in = put("bs_in", [P, GROUPS, H])
        bw_in = put("bw_in", [P, GROUPS, H])
        tab1 = put("tab1", [P, 1024])
        tab2 = put("tab2", [P, 1024])
        phasor = put("phasor", [P, 2, 2, GROUPS])
        put = placed(0)
        uc = put("uc", [P, G8, UT, NCH])
        pb = put("pb", [P, G8, STEP, H])
        pt1 = put("pt1", [P, G8, STEP, H])
        pt2 = put("pt2", [P, G8, STEP, H])
        wt = put("wt", [P, G8, P])
        tp = put("tp", [P, G8, STEP, H])
        ca = put("ca", [P, G8, STEP, H])
        put = placed(69)
        msb = put("msb", [P, G8 * H])
        ssb = put("ssb", [P, G8 * NCH])
        decay = put("decay", [P, G8, NCH])
        v1 = put("v1", [P, G8, NCH])
        v2 = put("v2", [P, G8, NCH])
        zs = put("zs", [P, G8 * NCH])
        xp = put("xp", [P, G8, NCH])
        assert STEP * NCH == SEQ
        du = placed(85)("du", [P, UT, SEQ])
        yf = placed(8)("yf", [P, UT, SEQ])
        yg = placed(16)("yg", [P, UT, SEQ])
        put = placed(32)
        y_hi = put("y_hi", [P, UT, SEQ], F32R)
        y_lo = put("y_lo", [P, UT, SEQ], F32R)
        put = placed(0)
        bt = put("bt", [P, HEADS, SEQ])
        qs = put("qs", [DH, 2 * R, SEQ])
        kt = put("kt", [DH, 2, 2, SEQ])
        vt = put("vt", [P, 2, SEQ])
        vtok = put("vtok", [P, 2, TT, P])
        put = placed(48)
        w1 = put("w1", [P, 2, 16, P])
        kk = put("kk", [P, 2, NKV, SEQ])
        w2 = put("w2", [P, 2, DH])
        pos_rows = put("pos_rows", [16, 2, P])
        pos_t = put("pos_t", [P, 2, 16])
        hid_bias = put("hid_bias", [P, 2])
        hid = put("hid", [P, 2, NKV * NCMP])
        kct = put("kct", [DH, NKV, NCMP])
        vc = put("vc", [NCMP, NKV, DH])
        kcg = put("kcg", [DH, 2, NCMP])
        vcg = put("vcg", [NCMP, 2, DH])
        put = placed(48)
        lg = put("lg", [P, 2, R, SEQ])
        pr = put("pr", [P, 2, R, SEQ])
        put = placed(80.5)
        pts = put("pts", [P, R, TT, P])
        lgc = put("lgc", [P, R, 16])
        prc = put("prc", [P, R, 16])
        ptc = put("ptc", [NCMP, R, P])
        nmax = put("nmax", [P, 3, R])
        den = put("den", [P, 3, R])
        wgt = put("wgt", [P, 3, R])
        ot = put("ot", [P, 3, R, DH])
        put = placed(32)
        xr = put("xr", [P, TT, D_MODEL])
        ff = put("ff", [P, D_FF // P, SEQ])
        xs2 = placed(48)("xs2", [P, TT, D_MODEL])
        put = placed((proj_at - zone) / 1024)
        gain = put("gain", [P, D_MODEL])
        ynorm = put("ynorm", [P, TT, D_MODEL])

        ps = ctx.enter_context(nc.psum_tensor("ps", [P, 8, 512], F32))

        const_in, vec_in, row_in, x_in, b_in, c_in = map(sem, ("const_in", "vec_in", "row_in", "x_in", "b_in", "c_in"))
        raw_in = {"A": sem("raw_a_in"), "B": sem("raw_b_in")}
        gatew_in, cmp_in, tab_in, bias_out, bt_in, xr_in, gain_in, out_done = map(
            sem, ("gatew_in", "cmp_in", "tab_in", "bias_out", "bt_in", "xr_in", "gain_in", "out_done"))
        hi_done, lo_done, mm_done = sem("hi_done"), sem("lo_done"), sem("mm_done")
        proj_done, pair_act, glu_done, ff_done = map(sem, ("proj_done", "pair_act", "glu_done", "ff_done"))
        sumsq, std, rstd, xs_done, norm_ps, hh_done, hl_done, x1_done = map(
            sem, ("sumsq", "std", "rstd", "xs_done", "norm_ps", "hh_done", "hl_done", "x1_done"))
        vec_ps, vec_done = sem("vec_ps"), sem("vec_done")
        dt_done, ang_done, mag_done, red_done, trig_done, rows_done, cols_ps, cols_done = map(
            sem, ("dt_done", "ang_done", "mag_done", "red_done", "trig_done", "rows_done", "cols_ps", "cols_done"))
        gate_hi_done, gate_split, gate_ps, gate_done = map(sem, ("gate_hi_done", "gate_split", "gate_ps", "gate_done"))
        cn_done, c_ps, cs_done, tables_done = map(sem, ("cn_done", "c_ps", "cs_done", "tables_done"))
        uc_ps, uc_done, pb_done, ssm_a_ps, m_done, wt_done, s_ps, s_done, toep_ps, toep_done = map(
            sem, ("uc_ps", "uc_done", "pb_done", "ssm_a_ps", "m_done", "wt_done", "s_ps", "s_done", "toep_ps",
                  "toep_done"))
        swap_ps, z_done, zswap_ps, xp_done, ca_done, y_ps, y_done = map(
            sem, ("swap_ps", "z_done", "zswap_ps", "xp_done", "ca_done", "y_ps", "y_done"))
        yperm_ps, yf_done, gelu_done, yhi_done, ylo_done = map(
            sem, ("yperm_ps", "yf_done", "gelu_done", "yhi_done", "ylo_done"))
        dve_step, act_step, pool_step = sem("dve_step"), sem("act_step"), sem("pool_step")
        kk_done, pos_ps, pos_done, hid_ps, hidb_done, hid_done, kvc_ps, kvc_done = map(
            sem, ("kk_done", "pos_ps", "pos_done", "hid_ps", "hidb_done", "hid_done", "kvc_ps", "kvc_done"))
        tab_ready, bias_ps, bias_copied = sem("tab_ready"), sem("bias_ps"), sem("bias_copied")
        qk_done, vt_ps, vtok_done = sem("qk_done"), sem("vt_ps"), sem("vtok_done")
        sc_ps, max_done, prob_done, pt_ps, pt_done, o_ps, ot_done, otr_ps, nsa_done = map(
            sem, ("sc_ps", "max_done", "prob_done", "pt_ps", "pt_done", "o_ps", "ot_done", "otr_ps", "nsa_done"))
        fin_done = sem("fin_done")

        def raw_tile(form, q):
            t = raw["AB"[q // 2]]
            if form == "rows":
                return t[:, 2048 * (q % 2):2048 * (q % 2 + 1)]
            k = {"glu": UT, "cols": KT}[form]
            return t[:, 0:256 * k].rearrange("p (k n) -> p k n", k=k)[:, :, P * (q % 2):P * (q % 2 + 1)]

        def part_tile(t, form, q):
            if form == "rows":
                return t[:, q % 2, :]
            k = {"glu": UT, "cols": KT}[form]
            return t[:, q % 2, 0:P * k].rearrange("p (k n) -> p k n", k=k)

        STREAM = {"in": (0, IN_BODIES, "cols"), "glu": (GLU_0, GLU_BODIES, "glu"), "out": (OUT_0, OUT_BODIES, "rows"),
                  "ffn": (FFN_0, FFN_BODIES, "cols"), "down": (DOWN_0, DOWN_BODIES, "rows")}
        NEXT = {"in": "glu", "glu": "out", "out": "ffn", "ffn": "down", "down": None}

        block = ctx.enter_context(nc.Block())

        @block.sync
        def _(sp):
            sp.dma_start(xt[:, 0, :], x[0, 0:P, :]).then_inc(x_in, 16)
            sp.dma_start(xt[:, 1, :], x[0, P:SEQ, :]).then_inc(x_in, 16)

            def chunk(body, slot, src):
                if not isinstance(body, int) or body > 0:
                    sp.wait_ge(lo_done, 4 * body + (2 if slot == "A" else 4))
                k, n = src.shape[1], src.shape[2]
                dst = raw[slot][:, 0:k * n].rearrange("p (k n) -> p k n", k=k)
                sp.dma_start(dst, src).then_inc(raw_in[slot], 16)

            def cols(w, c):
                return w[0, :, ds(c, 256)].rearrange("(k p) n -> p k n", p=P)

            def rows(w, r):
                return w[0, ds(r, 256), :].rearrange("(k p) n -> p k n", p=P)

            def load_in(i):
                chunk(i, "A", cols(w_in, 512 * i))
                chunk(i, "B", cols(w_in, 512 * i + 256))

            load_in(0)
            sp.dma_start(gate_raw[:], w_in[0, :, GATE_COL:GATE_COL + NGATE].rearrange("(k p) n -> p k n", p=P)
                         ).then_inc(gatew_in, 16)
            with sp.Fori(1, IN_BODIES) as i:
                load_in(i)

            def load_glu(i):
                chunk(GLU_0 + i, "A", cols(w_glu, 256 * i))
                chunk(GLU_0 + i, "B", cols(w_glu, D_SSM + 256 * i))

            def load_out(i):
                chunk(OUT_0 + i, "A", rows(w_out, 512 * i))
                chunk(OUT_0 + i, "B", rows(w_out, 512 * i + 256))

            def load_ffn(i):
                chunk(FFN_0 + i, "A", cols(w_gate, 256 * i))
                chunk(FFN_0 + i, "B", cols(w_up, 256 * i))

            def load_down(i):
                chunk(DOWN_0 + i, "A", rows(w_down, 512 * i))
                chunk(DOWN_0 + i, "B", rows(w_down, 512 * i + 256))

            chunk(GLU_0, "A", cols(w_glu, 0))
            sp.wait_ge(y_ps, UT)
            for n, w in enumerate((w1_k, w1_v)):
                sp.dma_start(w1[:, n], w[0].rearrange("(k p) n -> p k n", p=P)).then_inc(cmp_in, 16)
            for n, w in enumerate((w2_k, w2_v)):
                sp.dma_start(w2[:, n], w[0]).then_inc(cmp_in, 16)
            for n, w in enumerate((pos_k, pos_v)):
                sp.dma_start(pos_rows[:, n], w[0].rearrange("(k j) d -> k (j d)", j=2)).then_inc(cmp_in, 16)
            chunk(GLU_0, "B", cols(w_glu, D_SSM))
            sp.wait_ge(bias_out, 32)
            sp.wait_ge(yf_done, 1)
            sp.wait_ge(yhi_done, 1)
            sp.wait_ge(ylo_done, 1)
            sp.dma_start(bt[:], bass.AP(bias_copies.tensor, P - 1, [[HEADS * SPAN - 1, P], [SPAN, HEADS], [1, SEQ]])
                         ).then_inc(bt_in, 16)
            with sp.Fori(1, GLU_BODIES) as i:
                load_glu(i)
            load_out(0)
            sp.wait_ge(mm_done, 4 * OUT_0 + MM_CREDIT)
            for t in range(TT):
                sp.dma_start(xr[:, t, :], x[0, P * t:P * (t + 1), :]).then_inc(xr_in, 16)
            with sp.Fori(1, OUT_BODIES) as i:
                load_out(i)
            load_ffn(0)
            sp.wait_ge(mm_done, 4 * FFN_0 + MM_CREDIT)
            sp.dma_start(gain[:], bass.AP(final_norm.tensor, 0, [[0, P], [1, D_MODEL]])).then_inc(gain_in, 16)
            with sp.Fori(1, FFN_BODIES) as i:
                load_ffn(i)
            with sp.Fori(0, DOWN_BODIES) as i:
                load_down(i)
            for t in range(TT):
                sp.wait_ge(fin_done, t + 1)
                sp.dma_start(out[0, P * t:P * (t + 1), :], ynorm[:, t, :]).then_inc(out_done, 16)
            sp.wait_ge(out_done, 16 * TT)

        @block.gpsimd
        def _(pool):
            step = Steps(pool, pool_step)
            for n, (half, src) in enumerate(((0, b_re), (1, b_im))):
                pool.dma_start(bs_in[NS * half:NS * (half + 1), :, :], src[0].rearrange("g p h -> p g h")
                               ).then_inc(b_in, 16)
                pool.dma_start(bw_in[NS * (1 - half):NS * (2 - half), :, :], src[0].rearrange("g p h -> p g h")
                               ).then_inc(b_in, 16)
            for n, half, src in ((0, 0, c_re), (0, 1, c_im), (1, 0, c_im), (1, 1, c_re)):
                pool.dma_start(cn[:, n, :, NS * half:NS * (half + 1)],
                               src[0].rearrange("(t g) h p -> (g h) t p", g=G8)).then_inc(c_in, 16)
            pool.wait_ge(bias_copied, 1)
            pool.dma_start(bias_rows[:, :], bias_sb[:]).then_inc(bias_out, 16)
            pool.wait_ge(bias_out, 16)
            pool.dma_start(bias_copies[:, :, :], bass.AP(bias_rows.tensor, 0, [[0, P], [1, HEADS * SPAN]])
                           ).then_inc(bias_out, 16)
            pool.wait_ge(c_in, 64)
            pool.wait_ge(b_in, 64)
            nc.gpsimd.tensor_scalar(cn[:, 0, :, NS:P], cn[:, 0, :, NS:P], -1.0, None, ALU.mult)
            nc.gpsimd.tensor_scalar(cn[:, 1, :, :], cn[:, 1, :, :], -1.0, None, ALU.mult).then_inc(cn_done, 1)
            step.then(nc.gpsimd.tensor_scalar(bw_in[0:NS], bw_in[0:NS], -1.0, None, ALU.mult))
            pool.wait_ge(cols_done, 1)
            pool.wait_ge(norm_ps, 1)
            pool.wait_ge(gate_ps, 1)

            def mul(o, a, b):
                step(nc.gpsimd.tensor_tensor(o, a, b, ALU.mult))

            def product(out_re, out_im, x_re, x_im, y_re, y_im, t1, t2):
                mul(t1, x_re, y_re)
                mul(t2, x_im, y_im)
                step.wait()
                step.then(nc.gpsimd.tensor_tensor(out_re, t1, t2, ALU.subtract))
                mul(t1, x_re, y_im)
                mul(t2, x_im, y_re)
                step.wait()
                step.then(nc.gpsimd.tensor_tensor(out_im, t1, t2, ALU.add))

            step(nc.gpsimd.memset(pow_re[:, 0, :], 1.0))
            step(nc.gpsimd.memset(pow_im[:, 0, :], 0.0))
            step(nc.gpsimd.tensor_copy(pow_re[:, 1, :], ssm_cols[:, 0, :]))
            step.then(nc.gpsimd.tensor_copy(pow_im[:, 1, :], ssm_cols[:, 1, :]))
            m = 1
            while m < STEP:
                t1 = tab1[:, 0:m * GROUPS].rearrange("p (k g) -> p k g", g=GROUPS)
                t2 = tab2[:, 0:m * GROUPS].rearrange("p (k g) -> p k g", g=GROUPS)
                product(pow_re[:, m + 1:2 * m + 1, :], pow_im[:, m + 1:2 * m + 1, :],
                        pow_re[:, 1:m + 1, :], pow_im[:, 1:m + 1, :],
                        pow_re[:, m:m + 1, :].broadcast_to([P, m, GROUPS]),
                        pow_im[:, m:m + 1, :].broadcast_to([P, m, GROUPS]), t1, t2)
                m *= 2
            f_re = ssm_cols[:, 2, :].unsqueeze(2).broadcast_to([P, GROUPS, H])
            f_im = ssm_cols[:, 3, :].unsqueeze(2).broadcast_to([P, GROUPS, H])
            t1 = tab1[:].rearrange("p (g h) -> p g h", h=H)
            t2 = tab2[:].rearrange("p (g h) -> p g h", h=H)
            mul(t1, f_re, bs_in[:])
            mul(t2, f_im, bw_in[:])
            step.wait()
            step.then(nc.gpsimd.tensor_tensor(bb[:], t1, t2, ALU.add))
            mul(t1, f_re, bw_in[:])
            mul(t2, f_im, bs_in[:])
            step.wait()
            step.then(nc.gpsimd.tensor_tensor(bbw[:], t1, t2, ALU.subtract))
            step(nc.gpsimd.memset(rot_c[:, :, 0:1], 1.0))
            step(nc.gpsimd.memset(rot_s[:, :, 0:1], 0.0))
            step(nc.gpsimd.tensor_copy(phasor[:, 0, 0, :], ssm_cols[:, 4, :]))
            step.then(nc.gpsimd.tensor_copy(phasor[:, 0, 1, :], ssm_cols[:, 5, :]))
            m, n = 1, 0
            while m < NCH:
                u_re, u_im = phasor[:, n, 0, :], phasor[:, n, 1, :]
                t1 = tab1[:, 0:m * GROUPS].rearrange("p (g c) -> p g c", c=m)
                t2 = tab2[:, 0:m * GROUPS].rearrange("p (g c) -> p g c", c=m)
                product(rot_c[:, :, m:2 * m], rot_s[:, :, m:2 * m], rot_c[:, :, 0:m], rot_s[:, :, 0:m],
                        u_re.unsqueeze(2).broadcast_to([P, GROUPS, m]),
                        u_im.unsqueeze(2).broadcast_to([P, GROUPS, m]), t1, t2)
                if 2 * m < NCH:
                    product(phasor[:, 1 - n, 0, :], phasor[:, 1 - n, 1, :], u_re, u_im, u_re, u_im,
                            tab1[:, 0:GROUPS], tab2[:, 0:GROUPS])
                m, n = 2 * m, 1 - n
            nc.gpsimd.sem_inc(tables_done, 1)
            pool.wait_ge(cs_done, 2)

            def readout(i):
                g = ds(G8 * i, G8)
                shape = [P, G8, STEP, H]
                p_re = pow_re[:, 1:STEP + 1, g].rearrange("p k g -> p g k").unsqueeze(3).broadcast_to(shape)
                p_im = pow_im[:, 1:STEP + 1, g].rearrange("p k g -> p g k").unsqueeze(3).broadcast_to(shape)
                t1 = tab1[:].rearrange("p (g k h) -> p g k h", g=G8, k=STEP)
                t2 = tab2[:].rearrange("p (g k h) -> p g k h", g=G8, k=STEP)
                mul(t1, p_re, cs[:, g, :].unsqueeze(2).broadcast_to(shape))
                mul(t2, p_im, cw[:, g, :].unsqueeze(2).broadcast_to(shape))
                step.wait()
                nc.gpsimd.tensor_tensor(ca[:], t1, t2, ALU.add).then_inc(ca_done, 1)

            pool.wait_ge(uc_ps, 1)
            readout(0)
            n0 = step.n
            with pool.Fori(1, UT) as i:
                step.n = n0 + 2 * (i - 1)
                pool.wait_ge(y_ps, i)
                pool.wait_ge(ca_done, i)
                readout(i)

        @block.scalar
        def _(act):
            step = Steps(act, act_step)

            def copy(o, a, **kw):
                return nc.scalar.activation(o, a, ACT.Copy, **kw)

            nc.scalar.sem_inc(proj_done, PROJ_CREDIT)
            act.dma_start(shift[:], selectors[:, 0:240]).then_inc(const_in, 16)
            for n, src in enumerate((a_re, a_im)):
                for half in range(2):
                    act.dma_start(lam[:, n, NS * half:NS * (half + 1)], src[0]).then_inc(row_in, 16)
            act.dma_start(dt_row[:, 0:1], log_dt[0].rearrange("(g o) -> g o", o=1)).then_inc(row_in, 16)
            at = 0
            for src in (attn_norm[0], ffn_norm[0], b_glu[0], ssm_d[0]):
                n = src.shape[0] // P
                act.dma_start(vec_rows[at:at + n, :], src.rearrange("(k p) -> k p", p=P)).then_inc(vec_in, 16)
                at += n
            act.dma_start(select[:], selectors[:, 240:240 * 9].rearrange("p (g n) -> p g n", g=G8)
                          ).then_inc(const_in, 16)
            act.dma_start(swap[:], selectors[:, 240 * 9:]).then_inc(const_in, 16)

            act.dma_start(tab_rows[0:BUCKETS, :], rpb_table[:, :]).then_inc(tab_in, 16)
            act.dma_start(hot[:], onehot[:, :]).then_inc(tab_in, 16)

            act.wait_ge(row_in, 80)
            nc.scalar.activation(dt_row[:, 1:2], dt_row[:, 0:1], ACT.Exp).then_inc(dt_done, 1)
            act.wait_ge(ang_done, 1)
            nc.scalar.activation(mag[:], rnd[:, 0, :], ACT.Exp)
            nc.scalar.activation(ssm_rows[:, 6, :], rnd[:, 0, :], ACT.Exp, scale=float(STEP)).then_inc(mag_done, 1)

            for t in range(TT):
                act.wait_ge(x_in, 32)
                nc.scalar.activation(xs[:, t, :], xt[:, t, :], ACT.Square, accum_out=stat[:, t:t + 1]
                                     ).then_inc(sumsq, 1)
            act.wait_ge(red_done, 1)
            nc.scalar.activation(sin_cos[:], sin_cos[:], ACT.Sin).then_inc(trig_done, 1)

            def root(n):
                act.wait_ge(std, n)
                nc.scalar.activation(stat[:, 4:4 + TT], stat[:, 2:2 + TT], ACT.Sqrt).then_inc(rstd, 1)

            root(1)
            act.wait_ge(vec_ps, 1)
            copy(vec[:], ps[:, 7, 0:NVEC]).then_inc(vec_done, 1)
            act.wait_ge(bias_ps, 1)
            copy(bias_sb[:], ps[0:HEADS, 5, 0:SPAN]).then_inc(bias_copied, 1)
            act.wait_ge(cols_ps, 1)
            copy(ssm_cols[:], ps[:, 6, 0:7 * GROUPS].rearrange("p (n g) -> p n g", n=7)).then_inc(cols_done, 1)

            def cut_hi(phase, i, q):
                first, _, form = STREAM[phase]
                n = 4 * (first + i) + q
                if q % 2 == 0:
                    act.wait_ge(raw_in["AB"[q // 2]], 16 * (first + i + 1))
                act.wait_ge(mm_done, n - 2 + 1 + MM_CREDIT if not isinstance(n, int) or n >= 2 else MM_CREDIT)
                if form == "rows":
                    whole = not (isinstance(i, int) and i == 0 and q < 2)
                    if phase == "out":
                        act.wait_ge(glu_done, (UT if whole else 2) + PAIR_CREDIT)
                        src = proj[:, ds(4 * i + q, 1), :]
                    else:
                        act.wait_ge(ff_done, (D_FF // P if whole else 2) + PAIR_CREDIT)
                        src = ff[:, ds(4 * i + q, 1), :]
                    copy(act_hi[:, q:q + 1, :], src)
                copy(part_tile(w_hi, form, q), raw_tile(form, q)).then_inc(hi_done, 1)

            def run(phase, use):
                first, bodies, form = STREAM[phase]

                def body(i, last):
                    for q in range(4):
                        if q < 2:
                            cut_hi(phase, i, q + 2)
                        elif not last:
                            cut_hi(phase, i + 1, q - 2)
                        elif NEXT[phase]:
                            cut_hi(NEXT[phase], 0, q - 2)
                        use(i, q)

                with act.Fori(0, bodies - 1) as i:
                    body(i, False)
                body(bodies - 1, True)

            cut_hi("in", 0, 0)
            cut_hi("in", 0, 1)

            act.wait_ge(gatew_in, 16)
            copy(gate_hi[:], gate_raw[:]).then_inc(gate_hi_done, 1)

            def norm_hi(v):
                for k in range(KT):
                    copy(h_hi[:, k, :], ps[:, k // 2, SEQ * (k % 2):SEQ * (k % 2 + 1)], scale=vec[:, v + k:v + k + 1]
                         ).then_inc(hh_done, 1)

            act.wait_ge(norm_ps, 1)
            act.wait_ge(vec_done, 1)
            norm_hi(V_ATTN)
            act.wait_ge(gate_ps, 1)
            nc.scalar.activation(gates[:], ps[:, 4, 0:TT * NGATE].rearrange("p (t n) -> p t n", t=TT), ACT.Sigmoid
                                 ).then_inc(gate_done, 1)

            def keep_proj(i, q):
                n = 4 * i + q
                act.wait_ge(mm_done, n + 1 + MM_CREDIT)
                copy(proj[:, ds(n, 1), :], ps[:, q:q + 1, 0:SEQ]).then_inc(proj_done, 1)

            run("in", keep_proj)

            act.wait_ge(c_ps, 1)
            for n, t in enumerate((cs, cw)):
                copy(t[:].rearrange("p (t g) h -> p t (g h)", t=UT),
                     ps[:, 4 + 2 * n:6 + 2 * n, :].rearrange("p b (t c) -> p (b t) c", c=P)).then_inc(cs_done, 1)
            act.wait_ge(uc_ps, 1)
            copy(uc[:].rearrange("p g t c -> p g (t c)"),
                 ps[:, 0:4, :].rearrange("p b (g c) -> p (b g) c", g=2)).then_inc(uc_done, 1)
            with act.Fori(0, UT) as i:
                act.wait_ge(ssm_a_ps, i + 1)
                copy(msb[:], ps[:, 6, 0:P]).then_inc(m_done, 1)
                copy(wt[:].rearrange("p g c -> p (g c)"), ps[:, 4:6, :].rearrange("p b c -> p (b c)")
                     ).then_inc(wt_done, 1)
                act.wait_ge(s_ps, i + 1)
                copy(ssb[:], ps[:, 6, P:P + G8 * NCH]).then_inc(s_done, 1)
                act.wait_ge(toep_ps, i + 1)
                for b in range(2):
                    copy(tp[:, :, 4 * b:4 * b + 4, :],
                         ps[:, 4 + b, :].rearrange("p (t g h) -> p g t h", t=4, g=G8)).then_inc(toep_done, 1)
                act.wait_ge(y_ps, i + 1)
                copy(uc[:, :, ds(i, 1), :],
                     ps[:, 7, 256:512].rearrange("p (g o c) -> p g o c", g=G8, o=1)).then_inc(y_done, 1)
            act.wait_ge(yf_done, 1)
            nc.scalar.activation(yg[:], yf[:], ACT.Gelu_apprx_tanh).then_inc(gelu_done, 1)
            act.wait_ge(gelu_done, 1)
            copy(y_hi[:], yg[:]).then_inc(yhi_done, 1)

            act.wait_ge(pos_ps, 1)
            copy(pos_t[:].rearrange("p n k -> p (n k)"), ps[:, 2, 0:32]).then_inc(pos_done, 1)
            act.wait_ge(hid_ps, 1)
            copy(hid_bias[:], ps[:, 0, 128:130]).then_inc(hidb_done, 1)
            act.wait_ge(hidb_done, 1)
            for n in range(2):
                nc.scalar.activation(hid[:, n, :], ps[:, 0, 64 * n:64 * n + NKV * NCMP], ACT.Gelu_apprx_tanh,
                                     bias=hid_bias[:, n:n + 1]).then_inc(hid_done, 1)
            act.wait_ge(kvc_ps, 1)
            copy(kct[:].rearrange("p g n -> p (g n)"), ps[0:DH, 1, 0:NKV * NCMP]).then_inc(kvc_done, 1)
            copy(vc[:].rearrange("p g d -> p (g d)"), ps[0:NCMP, 1, 128:128 + NKV * DH]).then_inc(kvc_done, 1)

            with act.Fori(0, 2) as gp:
                act.wait_ge(vt_ps, gp + 1)
                copy(vtok[:].rearrange("p n b c -> p (n b c)"), ps[:, 5, :]).then_inc(vtok_done, 1)
                for u in range(4):
                    tq = u % 2
                    ns = P * (tq + 1)
                    count = 4 * gp + u
                    for n in range(2):
                        act.wait_ge(max_done, 3 * count + n + 1)
                        for r in range(R):
                            nc.scalar.activation(pr[:, n, r, 0:ns], lg[:, n, r, 0:ns], ACT.Exp,
                                                 bias=nmax[:, n, r:r + 1], accum_out=den[:, n, r:r + 1]
                                                 ).then_inc(prob_done, 1)
                    act.wait_ge(max_done, 3 * count + 3)
                    ncm = (ns - CMP_BLOCK) // CMP_STRIDE + 1
                    for r in range(R):
                        nc.scalar.activation(prc[:, r, 0:ncm], lgc[:, r, 0:ncm], ACT.Exp,
                                             bias=nmax[:, 2, r:r + 1], accum_out=den[:, 2, r:r + 1]
                                             ).then_inc(prob_done, 1)
                    for n in range(2):
                        act.wait_ge(pt_ps, 3 * count + n + 1)
                        copy(pts[:, :, 0:tq + 1, :],
                             ps[:, 5:7, :].rearrange("p b (r s c) -> p (b r) s c", r=2, c=P)[:, :, 0:tq + 1, :]
                             ).then_inc(pt_done, 1)
                    act.wait_ge(pt_ps, 3 * count + 3)
                    copy(ptc[0:ncm].rearrange("p r c -> p (r c)"), ps[0:ncm, 5, :]).then_inc(pt_done, 1)
                    act.wait_ge(otr_ps, count + 1)
                    copy(proj[:, ds(UT + 4 * gp + 2 * (u // 2), 2), P * tq:P * (tq + 1)],
                         ps[:, 6, 0:2 * P].rearrange("p (n c) -> p n c", n=2)).then_inc(nsa_done, 1)

            def glu_gate(i, q):
                if q >= 2:
                    j = 2 * i + q - 2
                    act.wait_ge(mm_done, 4 * (GLU_0 + i) + q + 1 + MM_CREDIT)
                    act.wait_ge(glu_done, j - 1 + PAIR_CREDIT)
                    nc.scalar.activation(pair[:, q - 2:q - 1, :], ps[:, q:q + 1, 0:SEQ], ACT.Sigmoid,
                                         bias=vec[:, ds(V_BGLU + UT + j, 1)]).then_inc(pair_act, 1)

            run("glu", glu_gate)

            run("out", lambda i, q: None)
            act.wait_ge(x1_done, 2 * 4)
            for t in range(TT):
                nc.scalar.activation(xs2[:, t, :], xr[:, t, :], ACT.Square, accum_out=stat[:, t:t + 1]
                                     ).then_inc(sumsq, 1)
            root(2)
            act.wait_ge(norm_ps, 2)
            norm_hi(V_FFN)

            def silu(i, q):
                if q < 2:
                    act.wait_ge(mm_done, 4 * (FFN_0 + i) + q + 1 + MM_CREDIT)
                    act.wait_ge(ff_done, 2 * i + q - 1 + PAIR_CREDIT)
                    nc.scalar.activation(pair[:, q:q + 1, :], ps[:, q:q + 1, 0:SEQ], ACT.Silu).then_inc(pair_act, 1)

            run("ffn", silu)
            run("down", lambda i, q: None)

            act.wait_ge(x1_done, 4 * 4)
            for t in range(TT):
                nc.scalar.activation(xs2[:, t, :], xr[:, t, :], ACT.Square, accum_out=stat[:, t:t + 1]
                                     ).then_inc(sumsq, 1)
            root(3)

        @block.vector
        def _(dve):
            step = Steps(dve, dve_step)

            def tt(o, a, b, op):
                return nc.vector.tensor_tensor(o, a, b, op)

            def tsc(o, a, s1, op0, s2=None, op1=None):
                return nc.vector.tensor_scalar(o, a, s1, s2, op0, op1) if op1 else nc.vector.tensor_scalar(
                    o, a, s1, None, op0)

            def stt(o, a, s, b, op0, op1):
                return nc.vector.scalar_tensor_tensor(out=o, in0=a, scalar=s, in1=b, op0=op0, op1=op1)

            nc.vector.sem_inc(lo_done, LO_CREDIT)
            nc.vector.sem_inc(glu_done, PAIR_CREDIT)
            nc.vector.sem_inc(ff_done, PAIR_CREDIT)
            nc.vector.memset(tab_rows[BUCKETS:BUCKETS + 1, :], MASK).then_inc(tab_ready, 1)
            dve.wait_ge(row_in, 80)
            dve.wait_ge(dt_done, 1)
            step.then(tsc(lam[:, 0, :], lam[:, 0, :], -1e-4, ALU.min))
            tsc(rnd[:, 0, :], lam[:, 0, :], dt_row[:, 1:2], ALU.mult).then_inc(ang_done, 1)
            step.then(tsc(ang[:, 0, :], lam[:, 1, :], dt_row[:, 1:2], ALU.mult))
            step.then(tsc(ang[:, 1, :], ang[:, 0, :], float(STEP), ALU.mult))
            dve.wait_ge(mag_done, 1)
            step.then(tsc(rnd[:], ang[:], float(1 / (2 * np.pi)), ALU.mult, MAGIC, ALU.add))
            step.then(tsc(rnd[:], rnd[:], MAGIC, ALU.subtract))
            for k, piece in enumerate((TWO_PI_1, TWO_PI_2, TWO_PI_3)):
                step.then(stt(red[:], rnd[:], -piece, (red if k else ang)[:], ALU.mult, ALU.add))
            step.then(tsc(sin_cos[:, :, 0, :], red[:], -PI_IN, ALU.max, PI_IN, ALU.min))
            step.then(stt(sin_cos[:, :, 1, :], sin_cos[:, :, 0, :], -1.0, sin_cos[:, :, 0, :], ALU.mult, ALU.min))
            tsc(sin_cos[:, :, 1, :], sin_cos[:, :, 1, :], PI / 2, ALU.add).then_inc(red_done, 1)

            def mean_square(n):
                dve.wait_ge(sumsq, TT * n)
                tsc(stat[:, 2:2 + TT], stat[:, 0:TT], 1.0 / D_MODEL, ALU.mult, EPS, ALU.add).then_inc(std, 1)
                dve.wait_ge(rstd, n)
                step.then(nc.vector.reciprocal(stat[:, 6:6 + TT], stat[:, 4:4 + TT]))

            mean_square(1)
            for t in range(TT):
                tsc(xs[:, t, :], xt[:, t, :], stat[:, 6 + t:7 + t], ALU.mult).then_inc(xs_done, 1)

            dve.wait_ge(trig_done, 1)
            step(tt(ssm_rows[:, 0, :], mag[:], sin_cos[:, 0, 1, :], ALU.mult))
            step(tt(ssm_rows[:, 1, :], mag[:], sin_cos[:, 0, 0, :], ALU.mult))
            step(nc.vector.tensor_copy(ssm_rows[:, 4, :], sin_cos[:, 1, 1, :]))
            step(nc.vector.tensor_copy(ssm_rows[:, 5, :], sin_cos[:, 1, 0, :]))
            step(tt(ang[:, 0, :], lam[:, 0, :], lam[:, 0, :], ALU.mult))
            step.then(tt(ang[:, 1, :], lam[:, 1, :], lam[:, 1, :], ALU.mult))
            step(tsc(red[:, 0, :], ssm_rows[:, 0, :], -1.0, ALU.add))
            step.then(tt(red[:, 1, :], ang[:, 0, :], ang[:, 1, :], ALU.add))
            step(nc.vector.reciprocal(red[:, 1, :], red[:, 1, :]))
            step(tt(rnd[:, 0, :], red[:, 0, :], lam[:, 0, :], ALU.mult))
            step(tt(rnd[:, 1, :], ssm_rows[:, 1, :], lam[:, 1, :], ALU.mult))
            step(tt(ang[:, 0, :], ssm_rows[:, 1, :], lam[:, 0, :], ALU.mult))
            step.then(tt(ang[:, 1, :], red[:, 0, :], lam[:, 1, :], ALU.mult))
            step(tt(rnd[:, 0, :], rnd[:, 0, :], rnd[:, 1, :], ALU.add))
            step.then(tt(ang[:, 0, :], ang[:, 0, :], ang[:, 1, :], ALU.subtract))
            step(tt(ssm_rows[:, 2, :], rnd[:, 0, :], red[:, 1, :], ALU.mult))
            tt(ssm_rows[:, 3, :], ang[:, 0, :], red[:, 1, :], ALU.mult).then_inc(rows_done, 1)

            def cut_lo(phase, i, q):
                first, _, form = STREAM[phase]
                n = 4 * (first + i) + q
                dve.wait_ge(hi_done, n + 1)
                if form == "rows":
                    src = (proj if phase == "out" else ff)[:, ds(4 * i + q, 1), :]
                    tt(act_lo[:, q:q + 1, :], src, act_hi[:, q:q + 1, :].bitcast(F32), ALU.subtract)
                tt(part_tile(w_lo, form, q), raw_tile(form, q), part_tile(w_hi, form, q).bitcast(F32), ALU.subtract
                   ).then_inc(lo_done, 1)

            def run(phase, use):
                first, bodies, form = STREAM[phase]

                def body(i, last):
                    for q in range(4):
                        if q < 2:
                            cut_lo(phase, i, q + 2)
                        elif not last:
                            cut_lo(phase, i + 1, q - 2)
                        elif NEXT[phase]:
                            cut_lo(NEXT[phase], 0, q - 2)
                        use(i, q)

                with dve.Fori(0, bodies - 1) as i:
                    body(i, False)
                body(bodies - 1, True)

            cut_lo("in", 0, 0)
            cut_lo("in", 0, 1)
            dve.wait_ge(gate_hi_done, 1)
            tt(gate_lo[:], gate_raw[:], gate_hi[:].bitcast(F32), ALU.subtract).then_inc(gate_split, 1)

            def norm_lo(v, n):
                for k in range(KT):
                    dve.wait_ge(hh_done, KT * n + k // 2 * 2 + 2)
                    stt(h_lo[:, k, :], ps[:, k // 2, SEQ * (k % 2):SEQ * (k % 2 + 1)], vec[:, v + k:v + k + 1],
                        h_hi[:, k, :].bitcast(F32), ALU.mult, ALU.subtract).then_inc(hl_done, 1)

            norm_lo(V_ATTN, 0)
            run("in", lambda i, q: None)

            def inputs(i):
                g = ds(G8 * i, G8)
                shape = [P, G8, STEP, H]
                p_re = pow_re[:, 0:STEP, g].rearrange("p k g -> p g k").unsqueeze(3).broadcast_to(shape)
                p_im = pow_im[:, 0:STEP, g].rearrange("p k g -> p g k").unsqueeze(3).broadcast_to(shape)
                step(tt(pt1[:], p_re, bb[:, g, :].unsqueeze(2).broadcast_to(shape), ALU.mult))
                step.then(tt(pt2[:], p_im, bbw[:, g, :].unsqueeze(2).broadcast_to(shape), ALU.mult))
                tt(pb[:], pt1[:], pt2[:], ALU.add).then_inc(pb_done, 1)

            dve.wait_ge(tables_done, 1)
            dve.wait_ge(uc_ps, 1)
            inputs(0)
            step.then(nc.vector.memset(xp[:, :, 0:1], 0.0))

            def recurrence(i, last):
                g = ds(G8 * i, G8)
                if not last:
                    dve.wait_ge(ssm_a_ps, i + 1)
                    inputs(i + 1)
                step.then(nc.vector.tensor_copy(decay[:], ssm_cols[:, 6, g].unsqueeze(2).broadcast_to([P, G8, NCH])))
                step(nc.vector.memset(decay[:, :, 0:1], 0.0))
                ps3 = ps[:, 7, 0:G8 * NCH].rearrange("p (g c) -> p g c", g=G8)
                dve.wait_ge(s_done, i + 1)
                step(tt(v1[:], rot_c[:, g, :], ssb[:].rearrange("p (g c) -> p g c", g=G8), ALU.mult))
                dve.wait_ge(swap_ps, i + 1)
                step.then(tt(v2[:], rot_s[:, g, :], ps3, ALU.mult))
                step.then(tt(v1[:], v1[:], v2[:], ALU.add))
                nc.vector.tensor_tensor_scan(zs[:], decay[:].rearrange("p g c -> p (g c)"),
                                             v1[:].rearrange("p g c -> p (g c)"), 0.0, ALU.mult, ALU.add
                                             ).then_inc(z_done, 1)
                dve.wait_ge(z_done, i + 1)
                step(tt(v1[:], rot_c[:, g, :], zs[:].rearrange("p (g c) -> p g c", g=G8), ALU.mult))
                dve.wait_ge(zswap_ps, i + 1)
                step.then(tt(v2[:], rot_s[:, g, :], ps3, ALU.mult))
                tt(xp[:, :, 1:NCH], v1[:, :, 0:NCH - 1], v2[:, :, 0:NCH - 1], ALU.subtract).then_inc(xp_done, 1)

            per = 2 + 2 + 3 + 2
            n0 = step.n
            with dve.Fori(0, UT - 1) as i:
                step.n = n0 + per * i
                recurrence(i, False)
            step.n = n0 + per * (UT - 1)
            recurrence(UT - 1, True)

            dve.wait_ge(y_ps, UT)
            step.then(tt(du[:], proj[:, 0:UT, :], vec[:, V_D:V_D + UT].unsqueeze(2).broadcast_to([P, UT, SEQ]),
                         ALU.mult))
            for n in range(2):
                for half in range(2):
                    src = proj[DH * half:DH * (half + 1), 16 + 2 * n:18 + 2 * n, :]
                    nc.vector.tensor_copy(kk[0:DH, n, half::2, :], src)
                    last = nc.vector.tensor_copy(kk[DH:P, n, half::2, 0:SEQ - 1], src[:, :, 1:SEQ])
            last.then_inc(kk_done, 1)
            dve.wait_ge(yperm_ps, 1)
            for s in range(STEP):
                o = yf[:].rearrange("p t (c s) -> p t c s", s=STEP)[:, :, :, s]
                d = du[:].rearrange("p t (c s) -> p t c s", s=STEP)[:, :, :, s]
                y = ps[:, s // 2, 256 * (s % 2):256 * (s % 2 + 1)].rearrange("p (t c) -> p t c", t=UT)
                last = tt(o, y, d, ALU.add)
            last.then_inc(yf_done, 1)
            dve.wait_ge(yhi_done, 1)
            tt(y_lo[:], yg[:], y_hi[:].bitcast(F32), ALU.subtract).then_inc(ylo_done, 1)

            dve.wait_ge(bt_in, 16)
            dve.wait_ge(kvc_done, 2)
            dve.wait_ge(ylo_done, 1)

            def attend(gp, u):
                gl, tq = u // 2, u % 2
                ns = P * (tq + 1)
                ncm = (ns - CMP_BLOCK) // CMP_STRIDE + 1
                count = 4 * gp + u
                heads = ds(8 * gp + R * gl, R)
                for n in range(2):
                    dve.wait_ge(sc_ps, 3 * count + n + 1)
                    step.then(tt(lg[:, n, :, 0:ns],
                                 ps[:, 2 * n:2 * n + 2, :].rearrange("p b (r s) -> p (b r) s", r=2)[:, :, 0:ns],
                                 bt[:, heads, SEQ - ns:SEQ], ALU.add))
                    step.then(nc.vector.reduce_max(nmax[:, n, :], lg[:, n, :, 0:ns], AX_X))
                    tsc(nmax[:, n, :], nmax[:, n, :], -1.0, ALU.mult).then_inc(max_done, 1)
                dve.wait_ge(sc_ps, 3 * count + 3)
                first = SEQ - ns + CMP_BLOCK - 1
                step.then(tt(lgc[:, :, 0:ncm], ps[:, 4, 0:R * 16].rearrange("p (r s) -> p r s", r=R)[:, :, 0:ncm],
                             bt[:, heads, first:SEQ:CMP_STRIDE], ALU.add))
                step.then(nc.vector.reduce_max(nmax[:, 2, :], lgc[:, :, 0:ncm], AX_X))
                tsc(nmax[:, 2, :], nmax[:, 2, :], -1.0, ALU.mult, -0.1 * MASK, ALU.min).then_inc(max_done, 1)
                dve.wait_ge(prob_done, 3 * R * count + 3 * R)
                step.then(tsc(den[:], den[:], 1e-30, ALU.max))
                step.then(nc.vector.reciprocal(den[:], den[:]))
                gate = gates[:, tq, ds(24 * gp + 12 * gl, 12)].rearrange("p (r n) -> p n r", n=3)
                step(tt(wgt[:, 0:2], gate[:, 1:3], den[:, 0:2], ALU.mult))
                step.then(tt(wgt[:, 2:3], gate[:, 0:1], den[:, 2:3], ALU.mult))
                dve.wait_ge(o_ps, count + 1)
                step(tt(ot[:, 0:2], ps[:, 7, :].rearrange("p (n r d) -> p n r d", n=2, r=R),
                        wgt[:, 0:2].unsqueeze(3).broadcast_to([P, 2, R, DH]), ALU.mult))
                step.then(tt(ot[:, 2], ps[:, 4, P:P + R * DH].rearrange("p (r d) -> p r d", r=R),
                             wgt[:, 2].unsqueeze(2).broadcast_to([P, R, DH]), ALU.mult))
                step.then(tt(ot[:, 0], ot[:, 0], ot[:, 1], ALU.add))
                tt(ot[:, 0], ot[:, 0], ot[:, 2], ALU.add).then_inc(ot_done, 1)

            per = 4 * (4 + 2 + 4 + 3)
            n0 = step.n
            with dve.Fori(0, 2) as gp:
                step.n = n0 + per * gp
                for b in range(2):
                    tsc(qs[:, b::2, :], proj[DH * b:DH * (b + 1), ds(UT + 4 * gp, 4), :], DH ** -0.5, ALU.mult)
                for n in range(2):
                    for gl in range(2):
                        nc.vector.tensor_copy(kt[:, n, gl:gl + 1, :],
                                              proj[DH * gl:DH * (gl + 1), ds(20 + 4 * n + gp, 1), :])
                    nc.vector.tensor_copy(vt[:, n:n + 1, :], proj[:, ds(22 + 4 * n + gp, 1), :])
                nc.vector.tensor_copy(kcg[:], kct[:, ds(2 * gp, 2), :])
                nc.vector.tensor_copy(vcg[:], vc[:, ds(2 * gp, 2), :]).then_inc(qk_done, 1)
                for u in range(4):
                    attend(gp, u)
            step.n = n0 + per * 2

            def glu(i, q):
                if q >= 2:
                    j = 2 * i + q - 2
                    dve.wait_ge(pair_act, j + 1)
                    stt(proj[:, ds(j, 1), :], ps[:, q - 2:q - 1, 0:SEQ], vec[:, ds(V_BGLU + j, 1)],
                        pair[:, q - 2:q - 1, :], ALU.add, ALU.mult).then_inc(glu_done, 1)

            run("glu", glu)

            def add_residual(phase):
                dve.wait_ge(mm_done, 4 * (STREAM[phase][0] + STREAM[phase][1]) + MM_CREDIT)
                for t in range(TT):
                    for b in range(4):
                        tt(xr[:, t, 512 * b:512 * (b + 1)], ps[:, 4 * t + b, :], xr[:, t, 512 * b:512 * (b + 1)],
                           ALU.add).then_inc(x1_done, 1)

            run("out", lambda i, q: None)
            dve.wait_ge(xr_in, 32)
            add_residual("out")
            mean_square(2)
            for t in range(TT):
                tsc(xs2[:, t, :], xr[:, t, :], stat[:, 6 + t:7 + t], ALU.mult).then_inc(xs_done, 1)
            norm_lo(V_FFN, 1)

            def swiglu(i, q):
                if q >= 2:
                    j = 2 * i + q - 2
                    dve.wait_ge(pair_act, UT + j + 1)
                    dve.wait_ge(mm_done, 4 * (FFN_0 + i) + q + 1 + MM_CREDIT)
                    tt(ff[:, ds(j, 1), :], ps[:, q:q + 1, 0:SEQ], pair[:, q - 2:q - 1, :], ALU.mult
                       ).then_inc(ff_done, 1)

            run("ffn", swiglu)
            run("down", lambda i, q: None)
            add_residual("down")
            mean_square(3)
            dve.wait_ge(gain_in, 16)
            for t in range(TT):
                stt(ynorm[:, t, :], xr[:, t, :], stat[:, 6 + t:7 + t], gain[:], ALU.mult, ALU.mult
                    ).then_inc(fin_done, 1)

        @block.tensor
        def _(pe):
            def mm(o, a, b, start=True, stop=True):
                return nc.tensor.matmul(o, a, b, start=start, stop=stop)

            def flip(o, a):
                k = a.shape[0]
                return nc.tensor.transpose(o, a, ident[0:k, 0:k])

            nc.tensor.sem_inc(mm_done, MM_CREDIT)
            pe.wait_ge(const_in, 48)
            pe.wait_ge(vec_in, 64)
            flip(ps[:, 7, 0:NVEC], vec_rows[:]).then_inc(vec_ps, 1)
            pe.wait_ge(tab_ready, 1)
            pe.wait_ge(tab_in, 32)
            mm(ps[0:HEADS, 5, 0:SPAN], tab_rows[:], hot[:]).then_inc(bias_ps, 1)
            pe.wait_ge(rows_done, 1)
            for n in range(7):
                last = flip(ps[:, 6, GROUPS * n:GROUPS * (n + 1)], ssm_rows[:, n, :])
            last.then_inc(cols_ps, 1)

            def norm_flip(src, n):
                for t in range(TT):
                    pe.wait_ge(xs_done, TT * n + t + 1)
                    for k in range(KT):
                        last = flip(ps[:, k // 2, SEQ * (k % 2) + P * t:SEQ * (k % 2) + P * (t + 1)],
                                    src[:, t, P * k:P * (k + 1)])
                last.then_inc(norm_ps, 1)

            pe.wait_ge(vec_done, 1)
            pe.wait_ge(cols_done, 1)
            pe.wait_ge(bias_copied, 1)
            norm_flip(xs, 0)

            pe.wait_ge(gate_split, 1)
            pe.wait_ge(hl_done, KT)
            for t in range(TT):
                o = ps[:, 4, NGATE * t:NGATE * (t + 1)]
                for k in range(KT):
                    a_hi, a_lo = (h[:, k, P * t:P * (t + 1)] for h in (h_hi, h_lo))
                    mm(o, a_hi, gate_hi[:, k, :], start=(k == 0), stop=False)
                    mm(o, a_hi, gate_lo[:, k, :], start=False, stop=False)
                    last = mm(o, a_lo, gate_hi[:, k, :], start=False, stop=(k == KT - 1))
            last.then_inc(gate_ps, 1)

            def column_tile(form, q, x_hi, x_lo):
                hi, lo = part_tile(w_hi, form, q), part_tile(w_lo, form, q)
                o = ps[:, q, 0:SEQ]
                kn = UT if form == "glu" else KT
                for k in range(kn):
                    mm(o, hi[:, k, :], x_hi[:, k, :], start=(k == 0), stop=False)
                    mm(o, hi[:, k, :], x_lo[:, k, :], start=False, stop=False)
                    last = mm(o, lo[:, k, :], x_hi[:, k, :], start=False, stop=(k == kn - 1))
                last.then_inc(mm_done, 1)

            def cut(phase, i, q):
                pe.wait_ge(lo_done, 4 * (STREAM[phase][0] + i) + q + 1 + LO_CREDIT)

            with pe.Fori(0, IN_BODIES) as i:
                for q in range(4):
                    cut("in", i, q)
                    pe.wait_ge(proj_done, 4 * i + q - 3 + PROJ_CREDIT)
                    column_tile("cols", q, h_hi, h_lo)

            pe.wait_ge(cn_done, 1)
            pe.wait_ge(gate_done, 1)
            for n in range(2):
                for t in range(UT):
                    last = flip(ps[:, 4 + 2 * n + t // 4, P * (t % 4):P * (t % 4 + 1)], cn[:, n, t, :])
            last.then_inc(c_ps, 1)
            pe.wait_ge(proj_done, 4 * IN_BODIES + PROJ_CREDIT)
            u4 = proj[:, 0:UT, :].rearrange("p t (c s) -> p t c s", s=STEP)
            for g in range(G8):
                for s in range(STEP):
                    last = mm(ps[:, g // 2, 256 * (g % 2):256 * (g % 2 + 1)], select[:, g, H * s:H * s + P],
                              u4[:, :, :, s], start=(s == 0), stop=(s == STEP - 1))
            last.then_inc(uc_ps, 1)
            pe.wait_ge(cs_done, 2)
            with pe.Fori(0, UT) as i:
                pe.wait_ge(pb_done, i + 1)
                for g in range(G8):
                    flip(ps[:, 4 + g // 4, P * (g % 4):P * (g % 4 + 1)], pb[:, g].rearrange("p k h -> p (k h)"))
                for g in range(G8):
                    last = mm(ps[:, 6, H * g:H * (g + 1)], pb[:, g].rearrange("p k h -> p (k h)"),
                              cs[:, ds(G8 * i + g, 1), :])
                last.then_inc(ssm_a_ps, 1)
                pe.wait_ge(m_done, i + 1)
                pe.wait_ge(wt_done, i + 1)
                pe.wait_ge(uc_done, 1)
                for g in range(G8):
                    last = mm(ps[:, 6, P + NCH * g:P + NCH * (g + 1)], wt[:, g, :], uc[:, g, ds(i, 1), :])
                last.then_inc(s_ps, 1)
                for t in range(STEP):
                    last = mm(ps[:, 4 + t // 4, P * (t % 4):P * (t % 4 + 1)], shift[:, H * t:H * t + P], msb[:])
                last.then_inc(toep_ps, 1)
                pe.wait_ge(s_done, i + 1)
                mm(ps[:, 7, 0:G8 * NCH], swap[:], ssb[:]).then_inc(swap_ps, 1)
                pe.wait_ge(z_done, i + 1)
                mm(ps[:, 7, 0:G8 * NCH], swap[:], zs[:]).then_inc(zswap_ps, 1)
                pe.wait_ge(xp_done, i + 1)
                pe.wait_ge(toep_done, 2 * (i + 1))
                pe.wait_ge(ca_done, i + 1)
                for g in range(G8):
                    o = ps[:, 7, 256 + NCH * g:256 + NCH * (g + 1)]
                    mm(o, tp[:, g].rearrange("p k h -> p (k h)"), uc[:, g, ds(i, 1), :], stop=False)
                    last = mm(o, ca[:, g].rearrange("p k h -> p (k h)"), xp[:, g, :], start=False)
                last.then_inc(y_ps, 1)
            pe.wait_ge(y_done, UT)
            for s in range(STEP):
                for g in range(G8):
                    last = mm(ps[:, s // 2, 256 * (s % 2):256 * (s % 2 + 1)],
                              select[:, s, P - H - H * g:2 * P - H - H * g],
                              uc[:, g].rearrange("p t c -> p (t c)"), start=(g == 0), stop=(g == G8 - 1))
            last.then_inc(yperm_ps, 1)

            pe.wait_ge(yf_done, 1)
            pe.wait_ge(cmp_in, 96)
            for n in range(2):
                last = flip(ps[:, 2, 16 * n:16 * (n + 1)], pos_rows[:, n, :])
            last.then_inc(pos_ps, 1)
            pe.wait_ge(kk_done, 1)
            for n in range(2):
                for k in range(16):
                    mm(ps[:, 0, 64 * n:64 * n + NKV * NCMP], w1[:, n, k, :],
                       kk[:, n, :, 2 * k:2 * k + CMP_STRIDE * (NCMP - 1) + 1:CMP_STRIDE],
                       start=(k == 0), stop=(k == 15))
            pe.wait_ge(pos_done, 1)
            for n in range(2):
                for k in range(16):
                    last = mm(ps[:, 0, 128 + n:129 + n], w1[:, n, k, :], pos_t[:, n, k:k + 1],
                              start=(k == 0), stop=(k == 15))
            last.then_inc(hid_ps, 1)
            pe.wait_ge(hid_done, 2)
            mm(ps[0:DH, 1, 0:NKV * NCMP], w2[:, 0, :], hid[:, 0, :])
            for g in range(NKV):
                last = mm(ps[0:NCMP, 1, 128 + DH * g:128 + DH * (g + 1)], hid[:, 1, NCMP * g:NCMP * (g + 1)],
                          w2[:, 1, :])
            last.then_inc(kvc_ps, 1)
            pe.wait_ge(kvc_done, 2)
            with pe.Fori(0, 2) as gp:
                pe.wait_ge(qk_done, gp + 1)
                for n in range(2):
                    for b in range(TT):
                        last = flip(ps[:, 5, P * (2 * n + b):P * (2 * n + b + 1)], vt[:, n, P * b:P * (b + 1)])
                last.then_inc(vt_ps, 1)
                pe.wait_ge(vtok_done, gp + 1)
                for u in range(4):
                    gl, tq = u // 2, u % 2
                    ns = P * (tq + 1)
                    ncm = (ns - CMP_BLOCK) // CMP_STRIDE + 1
                    count = 4 * gp + u
                    for n in range(2):
                        for r in range(R):
                            last = mm(ps[:, 2 * n + r // 2, 256 * (r % 2):256 * (r % 2) + ns],
                                      qs[:, R * gl + r, P * tq:P * (tq + 1)], kt[:, n, gl, 0:ns])
                        last.then_inc(sc_ps, 1)
                    for r in range(R):
                        last = mm(ps[:, 4, 16 * r:16 * r + ncm], qs[:, R * gl + r, P * tq:P * (tq + 1)],
                                  kcg[:, gl, 0:ncm])
                    last.then_inc(sc_ps, 1)
                    for n in range(2):
                        pe.wait_ge(prob_done, 3 * R * count + R * (n + 1))
                        for r in range(R):
                            for b in range(tq + 1):
                                last = flip(ps[:, 5 + r // 2, 256 * (r % 2) + P * b:256 * (r % 2) + P * (b + 1)],
                                            pr[:, n, r, P * b:P * (b + 1)])
                        last.then_inc(pt_ps, 1)
                        pe.wait_ge(pt_done, 3 * count + n + 1)
                        for r in range(R):
                            for b in range(tq + 1):
                                mm(ps[:, 7, 256 * n + DH * r:256 * n + DH * (r + 1)], pts[:, r, b, :],
                                   vtok[:, n, b, DH * gl:DH * (gl + 1)], start=(b == 0), stop=(b == tq))
                    pe.wait_ge(prob_done, 3 * R * count + 3 * R)
                    for r in range(R):
                        last = flip(ps[0:ncm, 5, P * r:P * (r + 1)], prc[:, r, 0:ncm])
                    last.then_inc(pt_ps, 1)
                    pe.wait_ge(pt_done, 3 * count + 3)
                    for r in range(R):
                        last = mm(ps[:, 4, P + DH * r:P + DH * (r + 1)], ptc[0:ncm, r, :],
                                  vcg[0:ncm, gl, :])
                    last.then_inc(o_ps, 1)
                    pe.wait_ge(ot_done, count + 1)
                    for n in range(2):
                        last = flip(ps[:, 6, P * n:P * (n + 1)], ot[:, 0, 2 * n:2 * n + 2, :].rearrange(
                            "p r d -> p (r d)"))
                    last.then_inc(otr_ps, 1)

            pe.wait_ge(ylo_done, 1)
            with pe.Fori(0, GLU_BODIES) as i:
                for q in range(4):
                    cut("glu", i, q)
                    pe.wait_ge(glu_done, 2 * i + q % 2 - 1 + PAIR_CREDIT)
                    column_tile("glu", q, y_hi, y_lo)

            def row_phase(phase):
                _, bodies, form = STREAM[phase]

                def body(i, first, final):
                    for q in range(4):
                        cut(phase, i, q)
                        passes = ((act_hi, w_hi), (act_hi, w_lo), (act_lo, w_hi))
                        for t in range(TT):
                            for n, (a, w) in enumerate(passes):
                                for b in range(4):
                                    last = mm(ps[:, 4 * t + b, :], a[:, q, P * t:P * (t + 1)],
                                              w[:, q % 2, 512 * b:512 * (b + 1)],
                                              start=(first and q == 0 and n == 0),
                                              stop=(final and q == 3 and n == 2))
                        last.then_inc(mm_done, 1)
                    return last

                body(0, True, False)
                with pe.Fori(1, bodies - 1) as i:
                    body(i, False, False)
                body(bodies - 1, False, True)

            pe.wait_ge(glu_done, UT + PAIR_CREDIT)
            pe.wait_ge(nsa_done, 8)
            row_phase("out")
            pe.wait_ge(x1_done, 8)
            norm_flip(xs2, 1)

            pe.wait_ge(hl_done, 2 * KT)
            with pe.Fori(0, FFN_BODIES) as i:
                for q in range(4):
                    cut("ffn", i, q)
                    pe.wait_ge(ff_done, 2 * i + q % 2 - 1 + PAIR_CREDIT)
                    column_tile("cols", q, h_hi, h_lo)
            pe.wait_ge(ff_done, D_FF // P + PAIR_CREDIT)
            row_phase("down")


_INS = ["x", "rpb_table", "attn_norm", "ffn_norm", "final_norm", "w_in", "ssm_a_re", "ssm_a_im", "ssm_log_dt",
        "ssm_b_re", "ssm_b_im", "ssm_c_re", "ssm_c_im", "ssm_d", "w_glu", "b_glu", "cmp_pos_k", "cmp_w1_k", "cmp_w2_k",
        "cmp_pos_v", "cmp_w1_v", "cmp_w2_v", "w_out", "w_ffn_gate", "w_ffn_up", "w_ffn_down"]


def selector_rows():
    rows = np.zeros((P, 240 * 9 + P), np.float32)
    k = np.arange(P)
    rows[k, k + 112] = 1
    for g in range(G8):
        own = k[H * g:H * (g + 1)]
        rows[own, 240 * (g + 1) + 112 + own - H * g] = 1
    rows[k[NS:], 240 * 9 + k[NS:] - NS] = 1
    rows[k[:NS], 240 * 9 + k[:NS] + NS] = -1
    return rows


def bucket_rows():
    dist = SEQ - 1 - np.arange(SPAN)
    n = np.maximum(dist, 1).astype(np.float32)
    exact = BUCKETS // 2
    large = exact + (np.log(n / np.float32(exact)) / np.float32(np.log(1024 / exact)) * np.float32(exact)
                     ).astype(np.int32)
    bucket = np.where(dist < exact, np.maximum(dist, 0), np.minimum(large, BUCKETS - 1))
    rows = np.zeros((BUCKETS + 1, SPAN), np.float32)
    valid = dist >= 0
    rows[bucket[valid], np.arange(SPAN)[valid]] = 1
    rows[BUCKETS, ~valid] = 1
    return rows


_CONST = [("selectors", selector_rows), ("onehot", bucket_rows)]


def kernel(**inputs):
    import concourse.bacc as _bacc
    from concourse.bass_utils import run_bass_kernel_spmd as _run

    nc = _bacc.Bacc("TRN2", target_bir_lowering=False, num_devices=1)
    arrays, args = {}, []
    given = [(name, np.ascontiguousarray(inputs[name])) for name in _INS]
    given += [(name, rows()) for name, rows in _CONST]
    for name, a in given:
        arrays[f"in_{name}_dram"] = a
        args.append(nc.dram_tensor(f"in_{name}_dram", a.shape, mybir.dt.from_np(a.dtype), kind="ExternalInput").ap())
    args.append(nc.dram_tensor("out_0_dram", (1, SEQ, D_MODEL), F32, kind="ExternalOutput").ap())
    build(nc, *args)
    r = _run(nc, [arrays], core_ids=[0])
    return r.results[0]["out_0_dram"]
```

```python
from contextlib import ExitStack

import numpy as np

import concourse.bass as bass
from concourse import mybir

F32 = mybir.dt.float32
F32R = mybir.dt.float32r
ACT = mybir.ActivationFunctionType
ALU = mybir.AluOpType
AX_X = mybir.AxisListType.X
ds = bass.ds

P = 128
SEQ = 256
D_MODEL = 2048
D_FF = 5632
KT = D_MODEL // P
TT = SEQ // P
D_SSM = 1024
UT = D_SSM // P
GROUPS = 64
H = 16
NS = 64
G8 = P // H
STEP = 8
NCH = SEQ // STEP
HEADS = 16
NKV = 4
R = HEADS // NKV
DH = 64
CMP_STRIDE = 16
CMP_BLOCK = 32
NCMP = SEQ // CMP_STRIDE - 1
BUCKETS = 32
EPS = 1e-6
MASK = -1e30
SPAN = 384
PROJ_TILES = 28
GATE_COL = PROJ_TILES * P
NGATE = 3 * HEADS
V_ATTN, V_FFN, V_BGLU, V_POS, NVEC = 0, 16, 32, 48, 80

IN_BODIES = PROJ_TILES // 4
GLU_BODIES = D_SSM // 256
OUT_BODIES = KT // 4
FFN_BODIES = D_FF // 256
DOWN_BODIES = D_FF // 512
GLU_0 = IN_BODIES
OUT_0 = GLU_0 + GLU_BODIES
FFN_0 = OUT_0 + OUT_BODIES
DOWN_0 = FFN_0 + FFN_BODIES

MAGIC = 12582912.0
PI = float(np.pi)
PI_IN = 3.1415925
TWO_PI_1 = 6.28125
TWO_PI_2 = float(np.float32(2 * np.pi - 6.28125))
TWO_PI_3 = float(2 * np.pi - 6.28125 - np.float64(np.float32(2 * np.pi - 6.28125)))

LO_CREDIT = 4
MM_CREDIT = 2
PROJ_CREDIT = 4
PAIR_CREDIT = 2


class Steps:

    def __init__(self, engine, sem):
        self.engine, self.sem, self.n = engine, sem, 0

    def __call__(self, instruction):
        instruction.then_inc(self.sem, 1)
        self.n = self.n + 1

    def wait(self):
        self.engine.wait_ge(self.sem, self.n)

    def then(self, instruction):
        self(instruction)
        self.wait()


def build(nc, x, rpb_table, attn_norm, ffn_norm, final_norm, w_in, a_re, a_im, log_dt, b_re, b_im, c_re, c_im,
          ssm_d, w_glu, b_glu, pos_k, w1_k, w2_k, pos_v, w1_v, w2_v, w_out, w_gate, w_up, w_down,
          selectors, onehot, out):
    bias_rows = nc.dram_tensor("bias_rows", [HEADS, SPAN], F32, kind="Internal").ap()
    u_turn = nc.dram_tensor("u_turn", [UT, G8, P, NCH], F32, kind="Internal").ap()
    y_turn = nc.dram_tensor("y_turn", [UT, G8, P, NCH], F32, kind="Internal").ap()
    bias_copies = nc.dram_tensor("bias_copies", [P, HEADS, SPAN], F32, kind="Internal").ap()

    with ExitStack() as ctx:
        place = [(nc.sbuf_base + 63) // 64 * 64]

        def lasting(name, shape, dtype=F32):
            t = nc.alloc_sbuf_tensor_at(name, shape, dtype, offset=place[0])
            place[0] += (4 * int(np.prod(shape[1:])) + 31) // 32 * 32
            return t

        def sem(name):
            return ctx.enter_context(nc.semaphore(name))

        raw = {"A": lasting("raw_a", [P, 4096]), "B": lasting("raw_b", [P, 4096])}
        w_hi = lasting("w_hi", [P, 2, 2048], F32R)
        w_lo = lasting("w_lo", [P, 2, 2048], F32R)
        act_at = place[0]
        act_hi = lasting("act_hi", [P, 4, SEQ], F32R)
        act_lo = lasting("act_lo", [P, 4, SEQ], F32R)
        pair = lasting("pair", [P, 2, SEQ])
        bias_sb = nc.alloc_sbuf_tensor_at("bias_sb", [HEADS, SPAN], F32, offset=place[0] - 4 * 2 * SEQ)
        hot = nc.alloc_sbuf_tensor_at("hot", [BUCKETS + 1, SPAN], F32, offset=place[0] - 4 * 2 * SEQ)
        proj_at = place[0]
        proj = lasting("proj", [P, PROJ_TILES, SEQ])
        delay = lasting("delay", [P, STEP, P])
        swap = lasting("swap", [P, P])
        vec_rows = lasting("vec_rows", [NVEC, P])
        vec = lasting("vec", [P, NVEC])
        gates = lasting("gates", [P, TT, NGATE])
        dcol = lasting("dcol", [P, GROUPS])
        own_rows = lasting("own_rows", [P, H])
        stat = lasting("stat", [P, 16])
        ssm_cols = lasting("ssm_cols", [P, 7, GROUPS])
        zone = place[0]
        ident = delay[:, STEP - 1, :]

        def placed(start):
            where = [zone + int(start * 1024)]

            def put(name, shape, dtype=F32):
                t = nc.alloc_sbuf_tensor_at(name, shape, dtype, offset=where[0])
                where[0] += (4 * int(np.prod(shape[1:])) + 31) // 32 * 32
                assert where[0] <= nc.sbuf_usable_end, (name, where[0], nc.sbuf_usable_end)
                return t
            return put

        put = placed(0)
        h_hi = put("h_hi", [P, KT, SEQ], F32R)
        h_lo = put("h_lo", [P, KT, SEQ], F32R)
        xt = put("xt", [P, TT, D_MODEL])
        xs = put("xs", [P, TT, D_MODEL])
        put = placed((proj_at - zone) / 1024 + 8)
        gate_hi = put("gate_hi", [P, KT, NGATE], F32R)
        gate_lo = put("gate_lo", [P, KT, NGATE], F32R)
        gate_t = put("gate_t", [NGATE, SEQ])
        tab_rows = put("tab_rows", [BUCKETS + 1, HEADS])
        gate_raw = placed(94.5)("gate_raw", [P, KT, NGATE])
        w2 = placed(97.5)("w2", [P, 2, DH])
        put = placed((proj_at - zone) / 1024 + 16)
        lam = put("lam", [GROUPS, 2, P])
        dt_row = put("dt_row", [GROUPS, 8])
        ang = put("ang", [GROUPS, 2, P])
        rnd = put("rnd", [GROUPS, 2, P])
        red = put("red", [GROUPS, 2, P])
        sin_cos = put("sin_cos", [GROUPS, 2, 2, P])
        mag = put("mag", [GROUPS, P])
        ssm_rows = put("ssm_rows", [GROUPS, 7, P])
        d_rows = put("d_rows", [GROUPS, H])
        d_wide = put("d_wide", [GROUPS, H, STEP])
        put = placed(32)
        pow_re = put("pow_re", [P, STEP + 1, GROUPS])
        pow_im = put("pow_im", [P, STEP + 1, GROUPS])
        inp_re = put("inp_re", [P, STEP, GROUPS])
        inp_im = put("inp_im", [P, STEP, GROUPS])
        rot_c = put("rot_c", [P, GROUPS, NCH])
        rot_s = put("rot_s", [P, GROUPS, NCH])
        bb = put("bb", [P, GROUPS, H])
        bbw = put("bbw", [P, GROUPS, H])
        cs = put("cs", [P, GROUPS, H])
        cw = put("cw", [P, GROUPS, H])
        b_rows = nc.alloc_sbuf_tensor_at("b_rows", [GROUPS, 2, NS, H], F32, offset=act_at)
        put = placed(73)
        cn = put("cn", [P, UT, P])
        bs = put("bs", [P, GROUPS, H])
        sw = put("sw", [P, GROUPS, H])
        tab1 = put("tab1", [P, 1024])
        tab2 = put("tab2", [P, 1024])
        phasor = put("phasor", [P, 2, 2, GROUPS])
        pb = nc.alloc_sbuf_tensor_at("pb", [P, G8, H, STEP], F32, offset=act_at)
        pt = nc.alloc_sbuf_tensor_at("pt", [P, G8, H, STEP], F32, offset=act_at + 4 * 1024)
        v1 = nc.alloc_sbuf_tensor_at("v1", [P, G8, NCH], F32, offset=act_at + 8 * 1024)
        v2 = nc.alloc_sbuf_tensor_at("v2", [P, G8, NCH], F32, offset=act_at + 9 * 1024)
        put = placed(73)
        wt = put("wt", [P, G8, P])
        tp = put("tp", [P, G8, H, STEP])
        ca = put("ca", [P, G8, H, STEP])
        cat = put("cat", [P, G8, H, STEP])
        msb = put("msb", [P, G8, H])
        ssb = put("ssb", [P, G8 * NCH])
        decay = put("decay", [P, G8, NCH])
        zs = put("zs", [P, G8 * NCH])
        xp = put("xp", [P, G8, NCH])
        dmat = put("dmat", [P, GROUPS, H])
        assert STEP * NCH == SEQ
        uc = proj[:, 0:UT, :].rearrange("p t (g c) -> p t g c", g=G8)
        yg = placed(73)("yg", [P, UT, SEQ])
        put = placed(32)
        y_hi = put("y_hi", [P, UT, SEQ], F32R)
        y_lo = put("y_lo", [P, UT, SEQ], F32R)
        put = placed(0)
        bt = put("bt", [P, HEADS, SEQ])
        qs = put("qs", [DH, 2 * R, SEQ])
        kt = put("kt", [DH, 2, 2, SEQ])
        vt = put("vt", [P, 2, SEQ])
        vtok = put("vtok", [P, 2, TT, P])
        put = placed(48)
        w1 = [raw[slot][:, 2048:4096].rearrange("p (k n) -> p k n", n=P) for slot in "AB"]
        kk = put("kk", [P, 2, CMP_BLOCK // 2, NKV, NCMP])
        put = placed(64)
        hid_rows = put("hid_rows", [NKV * NCMP, 2, P])
        hid = put("hid", [P, 2, NKV * NCMP])
        kct = put("kct", [DH, NKV, NCMP])
        vc = put("vc", [NCMP, NKV, DH])
        kcg = put("kcg", [DH, 2, NCMP])
        vcg = put("vcg", [NCMP, 2, DH])
        put = placed(48)
        lg = put("lg", [P, 2, R, SEQ])
        pr = put("pr", [P, 2, R, SEQ])
        put = placed(80.5)
        pts = put("pts", [P, R, TT, P])
        lgc = put("lgc", [P, R, 16])
        prc = put("prc", [P, R, 16])
        ptc = put("ptc", [NCMP, R, P])
        nmax = put("nmax", [P, 3, R])
        den = put("den", [P, 2, 3, R])
        wgt = put("wgt", [P, 3, R])
        ot = put("ot", [P, 3, R, DH])
        put = placed(32)
        xr = put("xr", [P, TT, D_MODEL])
        ff = put("ff", [P, D_FF // P, SEQ])
        xs2 = placed(48)("xs2", [P, TT, D_MODEL])
        put = placed((proj_at - zone) / 1024)
        gain = put("gain", [P, D_MODEL])
        ynorm = put("ynorm", [P, TT, D_MODEL])

        ps = ctx.enter_context(nc.psum_tensor("ps", [P, 8, 512], F32))

        const_in, delay_in, vec_in, row_in, d_in, b_in, c_in = map(
            sem, ("const_in", "delay_in", "vec_in", "row_in", "d_in", "b_in", "c_in"))
        x_in = [sem("x0_in"), sem("x1_in")]
        u_out, u_in, y_out, y_in = map(sem, ("u_out", "u_in", "y_out", "y_in"))
        raw_in = {"A": sem("raw_a_in"), "B": sem("raw_b_in")}
        gatew_in, cmp_in, tab_in, bias_out, bt_in, xr_in, gain_in, out_done = map(
            sem, ("gatew_in", "cmp_in", "tab_in", "bias_out", "bt_in", "xr_in", "gain_in", "out_done"))
        hi_done, lo_done, mm_done = sem("hi_done"), sem("lo_done"), sem("mm_done")
        proj_done, pair_act, glu_done, ff_done = map(sem, ("proj_done", "pair_act", "glu_done", "ff_done"))
        sumsq, std, rstd, xs_done, norm_ps, hh_done, hl_done, x1_done = map(
            sem, ("sumsq", "std", "rstd", "xs_done", "norm_ps", "hh_done", "hl_done", "x1_done"))
        vec_ps, vec_done = sem("vec_ps"), sem("vec_done")
        dt_done, ang_done, mag_done, red_done, trig_done, rows_done, cols_ps, cols_done = map(
            sem, ("dt_done", "ang_done", "mag_done", "red_done", "trig_done", "rows_done", "cols_ps", "cols_done"))
        gate_hi_done, gate_split, gate_ps, gate_done = map(sem, ("gate_hi_done", "gate_split", "gate_ps", "gate_done"))
        cn_done, bc_ps, bc_done, bcw_ps, bcw_done, tables_done, dcol_ps, dcol_done = map(
            sem, ("cn_done", "bc_ps", "bc_done", "bcw_ps", "bcw_done", "tables_done", "dcol_ps", "dcol_done"))
        pb_done, ssm_a_ps, m_done, wt_done, s_ps, s_done, toep_ps, toep_done = map(
            sem, ("pb_done", "ssm_a_ps", "m_done", "wt_done", "s_ps", "s_done", "toep_ps",
                  "toep_done"))
        m_copied = sem("m_copied")
        swap_ps, z_done, zswap_ps, xp_done, ca_done, y_ps, y_done = map(
            sem, ("swap_ps", "z_done", "zswap_ps", "xp_done", "ca_done", "y_ps", "y_done"))
        gelu_done, yhi_done, ylo_done = map(sem, ("gelu_done", "yhi_done", "ylo_done"))
        wide_done, bbw_done, gatet_done, gatet_ps = map(sem, ("wide_done", "bbw_done", "gatet_done", "gatet_ps"))
        dve_step, act_step, pool_step = sem("dve_step"), sem("act_step"), sem("pool_step")
        hidrows_done, hidt_ps = sem("hidrows_done"), sem("hidt_ps")
        w2_in, kk_done, hid_ps, hid_done, kvc_ps, kvc_done, kcg_done, pow_done = map(
            sem, ("w2_in", "kk_done", "hid_ps", "hid_done", "kvc_ps", "kvc_done", "kcg_done", "pow_done"))
        t0_done, act_cut = sem("t0_done"), sem("act_cut")
        tab_ready, bias_ps, bias_copied = sem("tab_ready"), sem("bias_ps"), sem("bias_copied")
        qk_done, vt_ps, vtok_done = sem("qk_done"), sem("vt_ps"), sem("vtok_done")
        sc_ps, lg_done, max_done, prob_done, pt_ps, pt_done, o_ps, ot_done, otr_ps, nsa_done = map(
            sem, ("sc_ps", "lg_done", "max_done", "prob_done", "pt_ps", "pt_done", "o_ps", "ot_done", "otr_ps",
                  "nsa_done"))
        scc_ps, maxc_done, probc_done, ptc_ps, ptc_done = map(
            sem, ("scc_ps", "maxc_done", "probc_done", "ptc_ps", "ptc_done"))
        glu_in = {"A": sem("glu_a_in"), "B": sem("glu_b_in")}
        fin_done = sem("fin_done")

        def raw_tile(form, q):
            t = raw["AB"[q // 2]]
            if form == "rows":
                return t[:, 2048 * (q % 2):2048 * (q % 2 + 1)]
            if form == "glu":
                return t[:, 1024 * (q % 2):1024 * (q % 2 + 1)].rearrange("p (k n) -> p k n", n=P)
            return t[:].rearrange("p (k n) -> p k n", k=KT)[:, :, P * (q % 2):P * (q % 2 + 1)]

        def part_tile(t, form, q):
            if form == "rows":
                return t[:, q % 2, :]
            k = {"glu": UT, "cols": KT}[form]
            return t[:, q % 2, 0:P * k].rearrange("p (k n) -> p k n", k=k)

        def flipped(k):
            return ps[:, k // 4 * 2:k // 4 * 2 + 2, P * (k % 4):P * (k % 4 + 1)]

        STREAM = {"in": (0, IN_BODIES, "cols"), "glu": (GLU_0, GLU_BODIES, "glu"), "out": (OUT_0, OUT_BODIES, "rows"),
                  "ffn": (FFN_0, FFN_BODIES, "cols"), "down": (DOWN_0, DOWN_BODIES, "rows")}
        NEXT = {"in": None, "glu": None, "out": None, "ffn": "down", "down": None}

        block = ctx.enter_context(nc.Block())

        @block.sync
        def _(sp):
            for t in range(TT):
                sp.dma_start(xt[:, t, :], x[0, P * t:P * (t + 1), :]).then_inc(x_in[t], 16)

            def chunk(body, slot, src):
                if not isinstance(body, int) or body > 0:
                    sp.wait_ge(lo_done, 4 * body + (2 if slot == "A" else 4))
                k, n = src.shape[1], src.shape[2]
                dst = raw[slot][:, 0:k * n].rearrange("p (k n) -> p k n", k=k)
                sp.dma_start(dst, src).then_inc(raw_in[slot], 16)

            def cols(w, c):
                return w[0, :, ds(c, 256)].rearrange("(k p) n -> p k n", p=P)

            def rows(w, r):
                return w[0, ds(r, 256), :].rearrange("(k p) n -> p k n", p=P)

            def load_in(i, slot):
                chunk(i, slot, cols(w_in, 512 * i + (256 if slot == "B" else 0)))

            def turn_u(t):
                sp.wait_ge(proj_done, t + 1 + PROJ_CREDIT)
                sp.dma_start(u_turn[t].rearrange("g (h s) c -> (g h) (s c)", s=STEP), proj[:, t, :]
                             ).then_inc(u_out, 16)
                sp.wait_ge(u_out, 16 * (t + 1))
                sp.dma_start(uc[:, t], u_turn[t].rearrange("g r c -> r g c")).then_inc(u_in, 16)

            def turn_y(t):
                sp.wait_ge(y_done, t + 1)
                sp.dma_start(y_turn[ds(t, 1)].rearrange("o g r c -> r (o g) c"),
                             proj[:, ds(t, 1), :].rearrange("p o (g c) -> p (o g) c", g=G8)).then_inc(y_out, 16)
                sp.wait_ge(y_out, 16 * (t + 1))
                sp.dma_start(proj[:, ds(t, 1), :],
                             y_turn[ds(t, 1)].rearrange("o g (h s) c -> (g h) o (s c)", s=STEP)).then_inc(y_in, 16)

            sp.wait_ge(row_in, 80)
            sp.wait_ge(vec_in, 80)
            load_in(0, "A")
            load_in(0, "B")
            sp.dma_start(d_rows[:], ssm_d[0].rearrange("(g h) -> g h", h=H)).then_inc(d_in, 16)
            sp.dma_start(tab_rows[0:BUCKETS, :], rpb_table[:, :]).then_inc(tab_in, 16)
            sp.dma_start(hot[:], onehot[:, :]).then_inc(tab_in, 16)
            sp.dma_start(delay[:, 0:STEP - 1, :].rearrange("p t n -> p (t n)"), selectors[:, 0:P * (STEP - 1)]
                          ).then_inc(delay_in, 16)
            sp.dma_start(swap[:], selectors[:, P * STEP:P * (STEP + 1)]).then_inc(delay_in, 16)
            sp.dma_start(own_rows[:], selectors[:, P * (STEP + 1):]).then_inc(delay_in, 16)
            for n, w in enumerate((w2_k, w2_v)):
                sp.dma_start(w2[:, n], w[0]).then_inc(w2_in, 16)
            for n, src in enumerate((b_re, b_im)):
                sp.dma_start(b_rows[:, n], src[0]).then_inc(b_in, 16)
            sp.dma_start(gate_raw[:], w_in[0, :, GATE_COL:GATE_COL + NGATE].rearrange("(k p) n -> p k n", p=P)
                         ).then_inc(gatew_in, 16)
            load_in(1, "A")
            for i in range(2):
                turn_u(4 * i)
                turn_u(4 * i + 1)
                load_in(i + 1, "B")
                turn_u(4 * i + 2)
                turn_u(4 * i + 3)
                load_in(i + 2, "A")
            load_in(3, "B")
            with sp.Fori(0, 3) as j:
                load_in(4 + j, "A")
                load_in(4 + j, "B")
                turn_y(2 * j)
                turn_y(2 * j + 1)

            def load_glu(i):
                for n, slot in enumerate("AB"):
                    sp.wait_ge(lo_done, 4 * (GLU_0 + i) + 2 * (n + 1))
                    for half in range(2):
                        sp.dma_start(raw[slot][:, 1024 * half:1024 * (half + 1)].rearrange("p (k n) -> p k n", n=P),
                                     w_glu[0, :, ds(D_SSM * half + 256 * i + P * n, P)].rearrange(
                                         "(k p) n -> p k n", p=P)).then_inc(glu_in[slot], 16)

            def load_out(i):
                chunk(OUT_0 + i, "A", rows(w_out, 512 * i))
                chunk(OUT_0 + i, "B", rows(w_out, 512 * i + 256))

            def load_ffn(i):
                chunk(FFN_0 + i, "A", cols(w_gate, 256 * i))
                chunk(FFN_0 + i, "B", cols(w_up, 256 * i))

            def load_down(i):
                chunk(DOWN_0 + i, "A", rows(w_down, 512 * i))
                chunk(DOWN_0 + i, "B", rows(w_down, 512 * i + 256))

            load_glu(0)
            for n, w in enumerate((w1_k, w1_v)):
                sp.dma_start(w1[n], w[0].rearrange("(k p) n -> p k n", p=P)).then_inc(cmp_in, 16)
            turn_y(6)
            turn_y(7)
            sp.wait_ge(mm_done, 4 * IN_BODIES + MM_CREDIT)
            sp.wait_ge(bias_out, 32)
            sp.dma_start(bt[:], bass.AP(bias_copies.tensor, P - 1, [[HEADS * SPAN - 1, P], [SPAN, HEADS], [1, SEQ]])
                         ).then_inc(bt_in, 16)
            with sp.Fori(1, GLU_BODIES) as i:
                load_glu(i)
            load_out(0)
            sp.wait_ge(mm_done, 4 * OUT_0 + MM_CREDIT)
            for t in range(TT):
                sp.dma_start(xr[:, t, :], x[0, P * t:P * (t + 1), :]).then_inc(xr_in, 16)
            with sp.Fori(1, OUT_BODIES) as i:
                load_out(i)
            load_ffn(0)
            sp.wait_ge(mm_done, 4 * FFN_0 + MM_CREDIT)
            sp.dma_start(gain[:], bass.AP(final_norm.tensor, 0, [[0, P], [1, D_MODEL]])).then_inc(gain_in, 16)
            with sp.Fori(1, FFN_BODIES) as i:
                load_ffn(i)
            with sp.Fori(0, DOWN_BODIES) as i:
                load_down(i)
            for t in range(TT):
                for b in range(2):
                    c = slice(D_MODEL // 2 * b, D_MODEL // 2 * (b + 1))
                    sp.wait_ge(fin_done, 2 * t + b + 1)
                    sp.dma_start(out[0, P * t:P * (t + 1), c], ynorm[:, t, c]).then_inc(out_done, 16)
            sp.wait_ge(out_done, 32 * TT)
            sp.wait_ge(u_in, 16 * UT)
            sp.wait_ge(y_in, 16 * UT)

        @block.gpsimd
        def _(pool):
            step = Steps(pool, pool_step)
            for n, src in enumerate((c_re, c_im)):
                pool.dma_start(cn[:, :, NS * n:NS * (n + 1)], src[0].rearrange("(t g) h p -> (g h) t p", g=G8)
                               ).then_inc(c_in, 16)
            pool.wait_ge(bias_copied, 1)
            pool.dma_start(bias_rows[:, :], bias_sb[:]).then_inc(bias_out, 16)
            pool.wait_ge(c_in, 32)
            nc.gpsimd.tensor_scalar(cn[:, :, NS:P], cn[:, :, NS:P], -1.0, None, ALU.mult).then_inc(cn_done, 1)
            pool.wait_ge(bias_out, 16)
            pool.dma_start(bias_copies[:, :, :], bass.AP(bias_rows.tensor, 0, [[0, P], [1, HEADS * SPAN]])
                           ).then_inc(bias_out, 16)
            pool.wait_ge(cols_done, 1)
            pool.wait_ge(norm_ps, 1)

            def mul(o, a, b):
                step(nc.gpsimd.tensor_tensor(o, a, b, ALU.mult))

            def product(out_re, out_im, x_re, x_im, y_re, y_im, t1, t2):
                mul(t1, x_re, y_re)
                mul(t2, x_im, y_im)
                step.wait()
                step.then(nc.gpsimd.tensor_tensor(out_re, t1, t2, ALU.subtract))
                mul(t1, x_re, y_im)
                mul(t2, x_im, y_re)
                step.wait()
                step.then(nc.gpsimd.tensor_tensor(out_im, t1, t2, ALU.add))

            step(nc.gpsimd.memset(pow_re[:, 0, :], 1.0))
            step(nc.gpsimd.memset(pow_im[:, 0, :], 0.0))
            step(nc.gpsimd.tensor_copy(pow_re[:, 1, :], ssm_cols[:, 0, :]))
            step.then(nc.gpsimd.tensor_copy(pow_im[:, 1, :], ssm_cols[:, 1, :]))
            m = 1
            while m < STEP:
                t1 = tab1[:, 0:m * GROUPS].rearrange("p (k g) -> p k g", g=GROUPS)
                t2 = tab2[:, 0:m * GROUPS].rearrange("p (k g) -> p k g", g=GROUPS)
                product(pow_re[:, m + 1:2 * m + 1, :], pow_im[:, m + 1:2 * m + 1, :],
                        pow_re[:, 1:m + 1, :], pow_im[:, 1:m + 1, :],
                        pow_re[:, m:m + 1, :].broadcast_to([P, m, GROUPS]),
                        pow_im[:, m:m + 1, :].broadcast_to([P, m, GROUPS]), t1, t2)
                m *= 2
            pool.wait_ge(pool_step, step.n)
            pool.sem_inc(pow_done, 1)
            step(nc.gpsimd.memset(rot_c[:, :, 0:1], 1.0))
            step(nc.gpsimd.memset(rot_s[:, :, 0:1], 0.0))
            step(nc.gpsimd.tensor_copy(phasor[:, 0, 0, :], ssm_cols[:, 4, :]))
            step.then(nc.gpsimd.tensor_copy(phasor[:, 0, 1, :], ssm_cols[:, 5, :]))
            m, n = 1, 0
            while m < NCH:
                u_re, u_im = phasor[:, n, 0, :], phasor[:, n, 1, :]
                t1 = tab1[:, 0:m * GROUPS].rearrange("p (g c) -> p g c", c=m)
                t2 = tab2[:, 0:m * GROUPS].rearrange("p (g c) -> p g c", c=m)
                product(rot_c[:, :, m:2 * m], rot_s[:, :, m:2 * m], rot_c[:, :, 0:m], rot_s[:, :, 0:m],
                        u_re.unsqueeze(2).broadcast_to([P, GROUPS, m]),
                        u_im.unsqueeze(2).broadcast_to([P, GROUPS, m]), t1, t2)
                if 2 * m < NCH:
                    product(phasor[:, 1 - n, 0, :], phasor[:, 1 - n, 1, :], u_re, u_im, u_re, u_im,
                            tab1[:, 0:GROUPS], tab2[:, 0:GROUPS])
                m, n = 2 * m, 1 - n
            pool.wait_ge(pool_step, step.n)
            nc.gpsimd.tensor_copy(phasor[:, 0, 0, :], phasor[:, 1, 0, :]).then_inc(tables_done, 1)

            def readout(i):
                g = ds(G8 * i, G8)
                shape = [P, G8, H, STEP]
                p_re = pow_re[:, 1:STEP + 1, g].rearrange("p k g -> p g k").unsqueeze(2).broadcast_to(shape)
                p_im = pow_im[:, 1:STEP + 1, g].rearrange("p k g -> p g k").unsqueeze(2).broadcast_to(shape)
                mul(ca[:], p_re, cs[:, g, :].unsqueeze(3).broadcast_to(shape))
                mul(cat[:], p_im, cw[:, g, :].unsqueeze(3).broadcast_to(shape))
                step.wait()
                nc.gpsimd.tensor_tensor(ca[:], ca[:], cat[:], ALU.add).then_inc(ca_done, 1)

            pool.wait_ge(bcw_done, 2)
            pool.wait_ge(bbw_done, 1)
            readout(0)
            n0 = step.n
            with pool.Fori(1, UT) as i:
                step.n = n0 + 2 * (i - 1)
                pool.wait_ge(y_ps, i)
                pool.wait_ge(ca_done, i)
                readout(i)

        @block.scalar
        def _(act):
            step = Steps(act, act_step)

            def copy(o, a, **kw):
                return nc.scalar.activation(o, a, ACT.Copy, **kw)

            nc.scalar.sem_inc(proj_done, PROJ_CREDIT)
            act.dma_start(ident, selectors[:, P * (STEP - 1):P * STEP]).then_inc(const_in, 16)
            for n, src in enumerate((a_re, a_im)):
                for half in range(2):
                    act.dma_start(lam[:, n, NS * half:NS * (half + 1)], src[0]).then_inc(row_in, 16)
            act.dma_start(dt_row[:, 0:1], log_dt[0].rearrange("(g o) -> g o", o=1)).then_inc(row_in, 16)
            at = 0
            for src in (attn_norm[0], ffn_norm[0], b_glu[0]):
                n = src.shape[0] // P
                act.dma_start(vec_rows[at:at + n, :], src.rearrange("(k p) -> k p", p=P)).then_inc(vec_in, 16)
                at += n
            for n, src in enumerate((pos_k[0], pos_v[0])):
                act.dma_start(vec_rows[at:at + 16, :], src.rearrange("(k j) d -> k (j d)", j=2)).then_inc(vec_in, 16)
                at += 16
            def square(t):
                nc.scalar.activation(xs[:, t, :], xt[:, t, :], ACT.Square, accum_out=stat[:, 4 * t:4 * t + 1]
                                     ).then_inc(sumsq, 1)

            def squares(n, t):
                for b in range(4):
                    act.wait_ge(x1_done, 8 * (n - 2) + 4 * t + b + 1)
                    nc.scalar.activation(xs2[:, t, 512 * b:512 * (b + 1)], xr[:, t, 512 * b:512 * (b + 1)], ACT.Square,
                                         accum_out=stat[:, 4 * t + b:4 * t + b + 1]).then_inc(sumsq, 1)

            def load_table(function):
                nc.scalar.activation(stat[:, 14:15], vec[:, 0:1], function)

            act.wait_ge(row_in, 80)
            nc.scalar.activation(dt_row[:, 1:2], dt_row[:, 0:1], ACT.Exp).then_inc(dt_done, 1)
            act.wait_ge(x_in[0], 16)
            square(0)
            act.wait_ge(ang_done, 1)
            nc.scalar.activation(mag[:], rnd[:, 0, :], ACT.Exp)
            nc.scalar.activation(ssm_rows[:, 6, :], rnd[:, 0, :], ACT.Exp, scale=float(STEP)).then_inc(mag_done, 1)
            act.wait_ge(x_in[1], 16)
            square(1)

            def root(n, t):
                act.wait_ge(std, 2 * (n - 1) + t + 1)
                nc.scalar.activation(stat[:, 10 + t:11 + t], stat[:, 8 + t:9 + t], ACT.Sqrt).then_inc(rstd, 1)

            act.wait_ge(vec_ps, 1)
            copy(vec[:], ps[:, 7, 0:NVEC]).then_inc(vec_done, 1)
            for t in range(TT):
                root(1, t)
            act.wait_ge(red_done, 1)
            nc.scalar.activation(sin_cos[:], sin_cos[:], ACT.Sin).then_inc(trig_done, 1)

            def cut_hi(phase, i, q):
                first, _, form = STREAM[phase]
                n = 4 * (first + i) + q
                if phase == "glu":
                    act.wait_ge(glu_in["AB"[q // 2]], 32 * (i + 1))
                elif q % 2 == 0:
                    past = first - (GLU_BODIES if first > GLU_0 else 0)
                    act.wait_ge(raw_in["AB"[q // 2]], 16 * (past + i + 1))
                if form == "rows":
                    whole = not (isinstance(i, int) and i == 0 and q < 2)
                    if phase == "out":
                        act.wait_ge(glu_done, UT + PAIR_CREDIT)
                        src = proj[:, ds(4 * i + q, 1), :]
                    else:
                        act.wait_ge(ff_done, (D_FF // P if whole else 2) + PAIR_CREDIT)
                        src = ff[:, ds(4 * i + q, 1), :]
                    copy(act_hi[:, q:q + 1, :], src).then_inc(act_cut, 1)
                act.wait_ge(mm_done, n - 2 + 1 + MM_CREDIT if not isinstance(n, int) or n >= 2 else MM_CREDIT)
                copy(part_tile(w_hi, form, q), raw_tile(form, q)).then_inc(hi_done, 1)

            def run(phase, use):
                first, bodies, form = STREAM[phase]

                def body(i, last):
                    for q in range(4):
                        if q < 2:
                            cut_hi(phase, i, q + 2)
                        elif not last:
                            cut_hi(phase, i + 1, q - 2)
                        elif NEXT[phase]:
                            cut_hi(NEXT[phase], 0, q - 2)
                        use(i, q)

                with act.Fori(0, bodies - 1) as i:
                    body(i, False)
                body(bodies - 1, True)

            cut_hi("in", 0, 0)
            cut_hi("in", 0, 1)

            def norm_hi(v):
                for k in range(KT):
                    copy(h_hi[:, k, :].rearrange("p (t c) -> p t c", t=TT), flipped(k), scale=vec[:, v + k:v + k + 1]
                         ).then_inc(hh_done, 1)

            act.wait_ge(norm_ps, 1)
            act.wait_ge(vec_done, 1)
            norm_hi(V_ATTN)
            act.wait_ge(gatew_in, 16)
            copy(gate_hi[:], gate_raw[:]).then_inc(gate_hi_done, 1)

            def keep_proj(i, q):
                n = 4 * i + q
                act.wait_ge(mm_done, n + 1 + MM_CREDIT)
                copy(proj[:, ds(n, 1), :], ps[:, q:q + 1, 0:SEQ]).then_inc(proj_done, 1)

            def keep_nsa(gp, u):
                act.wait_ge(otr_ps, 4 * gp + u + 1)
                copy(proj[:, ds(UT + 4 * gp + 2 * (u // 2), 2), P * (u % 2):P * (u % 2 + 1)],
                     ps[:, 7, 0:2 * P].rearrange("p (n c) -> p n c", n=2)).then_inc(nsa_done, 1)

            def proj_body(i, last=False):
                for q in range(4):
                    if q < 2:
                        cut_hi("in", i, q + 2)
                    elif not last:
                        cut_hi("in", i + 1, q - 2)
                    keep_proj(i, q)

            def keep_u(i, q):
                n = 4 * i + q
                act.wait_ge(mm_done, n + 1 + MM_CREDIT)
                copy(proj[:, n, :].rearrange("p (s c) -> p c s", s=STEP),
                     ps[:, q, 0:SEQ].rearrange("p (c s) -> p c s", s=STEP)).then_inc(proj_done, 1)

            cut_hi("in", 0, 2)
            keep_u(0, 0)
            act.wait_ge(cols_ps, 1)
            copy(ssm_cols[:], ps[:, 6, 0:7 * GROUPS].rearrange("p (n g) -> p n g", n=7)).then_inc(cols_done, 1)
            act.wait_ge(bias_ps, 1)
            copy(bias_sb[:], ps[0:HEADS, 5, 0:SPAN]).then_inc(bias_copied, 1)
            act.wait_ge(dcol_ps, 1)
            copy(dcol[:], ps[:, 4, 0:GROUPS]).then_inc(dcol_done, 1)
            cut_hi("in", 0, 3)
            keep_u(0, 1)
            act.wait_ge(gatet_ps, 1)
            nc.scalar.activation(gate_t[:], ps[0:NGATE, 7, 0:SEQ], ACT.Sigmoid).then_inc(gatet_done, 1)
            cut_hi("in", 1, 0)
            keep_u(0, 2)
            act.wait_ge(gate_ps, 1)
            copy(gates[:], ps[:, 7, SEQ:SEQ + TT * NGATE].rearrange("p (t n) -> p t n", t=TT)).then_inc(gate_done, 1)
            cut_hi("in", 1, 1)
            keep_u(0, 3)
            cut_hi("in", 1, 2)
            act.wait_ge(bc_ps, 1)
            copy(bs[:].rearrange("p g h -> p h g"), ps[:, 4:6, :].rearrange("p b (h g) -> p (b h) g", g=GROUPS)
                 ).then_inc(bc_done, 1)
            copy(cs[:].rearrange("p (t g) h -> p t (g h)", t=UT),
                 ps[:, 6:8, :].rearrange("p b (t c) -> p (b t) c", c=P)).then_inc(bc_done, 1)
            keep_u(1, 0)
            cut_hi("in", 1, 3)
            keep_u(1, 1)
            cut_hi("in", 2, 0)
            act.wait_ge(bcw_ps, 1)
            for n, t in enumerate((sw, cw)):
                copy(t[:].rearrange("p g h -> p (g h)"), ps[:, 4 + 2 * n:6 + 2 * n, :].rearrange("p b c -> p (b c)")
                     ).then_inc(bcw_done, 1)
            keep_u(1, 2)
            cut_hi("in", 2, 1)
            keep_u(1, 3)
            proj_body(2)

            def ssm_body(j, last):
                i = 3 + j
                for a in range(2):
                    it = 2 * j + a
                    act.wait_ge(ssm_a_ps, it + 1)
                    copy(msb[:].rearrange("p g h -> p (g h)"), ps[:, 6, 0:P]).then_inc(m_copied, 1)
                    copy(wt[:].rearrange("p g c -> p (g c)"), ps[:, 4:6, :].rearrange("p b c -> p (b c)")
                         ).then_inc(wt_done, 1)
                    act.wait_ge(s_ps, it + 1)
                    copy(ssb[:], ps[:, 6, P:P + G8 * NCH]).then_inc(s_done, 1)
                    act.wait_ge(toep_ps, it + 1)
                    for b in range(2):
                        copy(tp[:, :, :, 4 * b:4 * b + 4],
                             ps[:, 4 + b, :].rearrange("p (t g h) -> p g h t", t=4, g=G8)).then_inc(toep_done, 1)
                    for q in (2 * a, 2 * a + 1):
                        if q < 2:
                            cut_hi("in", i, q + 2)
                        elif not last:
                            cut_hi("in", i + 1, q - 2)
                        keep_proj(i, q)
                    act.wait_ge(y_ps, it + 1)
                    copy(proj[:, ds(it, 1), :], ps[:, 7:8, 256:512]).then_inc(y_done, 1)

            act.wait_ge(tables_done, 1)
            with act.Fori(0, 3) as j:
                ssm_body(j, False)
            ssm_body(3, True)

            act.wait_ge(y_in, 16 * UT)
            nc.scalar.activation(yg[:].rearrange("p t (c s) -> p t s c", s=STEP),
                                 proj[:, 0:UT, :].rearrange("p t (s c) -> p t s c", s=STEP),
                                 ACT.Gelu_apprx_tanh).then_inc(gelu_done, 1)
            act.wait_ge(gelu_done, 1)
            copy(y_hi[:], yg[:]).then_inc(yhi_done, 1)
            act.wait_ge(hid_ps, 1)
            nc.scalar.activation(hid_rows[:].rearrange("p n c -> p (n c)"), ps[0:NKV * NCMP, 0, 0:2 * P],
                                 ACT.Gelu_apprx_tanh).then_inc(hidrows_done, 1)
            act.wait_ge(hidt_ps, 1)
            copy(hid[:], ps[:, 2, 0:P].rearrange("p (n c) -> p n c", n=2)[:, :, 0:NKV * NCMP]).then_inc(hid_done, 1)
            act.wait_ge(kvc_ps, 1)
            copy(kct[:].rearrange("p g n -> p (g n)"), ps[0:DH, 1, 0:NKV * NCMP]).then_inc(kvc_done, 1)
            copy(vc[:].rearrange("p g d -> p (g d)"), ps[0:NCMP, 1, 128:128 + NKV * DH]).then_inc(kvc_done, 1)

            act.wait_ge(ylo_done, 1)
            def attend(gp):
                cut_hi("glu", 2 * gp, 0)
                act.wait_ge(vt_ps, gp + 1)
                copy(vtok[:].rearrange("p n b c -> p (n b c)"), ps[:, 4, :]).then_inc(vtok_done, 1)
                for b in range(8):
                    u, n = b // 2, b % 2
                    tq = u % 2
                    ns = P * (tq + 1)
                    ncm = (ns - CMP_BLOCK) // CMP_STRIDE + 1
                    at, unit = 8 * gp + b, 4 * gp + u
                    act.wait_ge(max_done, at + 1)
                    for r in range(R):
                        nc.scalar.activation(pr[:, n, r, 0:ns], lg[:, n, r, 0:ns], ACT.Exp,
                                             bias=nmax[:, n, r:r + 1], accum_out=den[:, u % 2, n, r:r + 1]
                                             ).then_inc(prob_done, 1)
                    if n == 0:
                        act.wait_ge(maxc_done, unit + 1)
                        for r in range(R):
                            nc.scalar.activation(prc[:, r, 0:ncm], lgc[:, r, 0:ncm], ACT.Exp,
                                                 bias=nmax[:, 2, r:r + 1], accum_out=den[:, u % 2, 2, r:r + 1]
                                                 ).then_inc(probc_done, 1)
                    if b < 7:
                        cut_hi("glu", 2 * gp + (b + 1) // 4, (b + 1) % 4)
                    act.wait_ge(pt_ps, at + 1)
                    copy(pts[:, :, 0:tq + 1, :],
                         ps[:, 4:6, :].rearrange("p b (r s c) -> p (b r) s c", r=2, c=P)[:, :, 0:tq + 1, :]
                         ).then_inc(pt_done, 1)
                    if n == 1:
                        j = 4 * gp + u
                        nc.scalar.activation(pair[:, u % 2, :], ps[:, 1, 0:SEQ], ACT.Exp, scale=-1.0,
                                             bias=vec[:, ds(V_BGLU + UT + j, 1)]).then_inc(pair_act, 1)
                        act.wait_ge(ptc_ps, unit + 1)
                        copy(ptc[0:ncm].rearrange("p r c -> p (r c)"), ps[0:ncm, 6, :]).then_inc(ptc_done, 1)
                    elif u > 0:
                        keep_nsa(gp, u - 1)
                if gp == 1:
                    cut_hi("out", 0, 0)
                keep_nsa(gp, 3)

            attend(0)
            attend(1)

            cut_hi("out", 0, 1)
            run("out", lambda i, q: None)
            load_table(ACT.Sqrt)
            for t in range(TT):
                squares(2, t)
                root(2, t)
            cut_hi("ffn", 0, 0)
            cut_hi("ffn", 0, 1)
            load_table(ACT.Silu)
            act.wait_ge(norm_ps, 2)
            norm_hi(V_FFN)

            def silu(i, q):
                if q < 2:
                    act.wait_ge(mm_done, 4 * (FFN_0 + i) + q + 1 + MM_CREDIT)
                    act.wait_ge(ff_done, 2 * i + q - 1 + PAIR_CREDIT)
                    nc.scalar.activation(pair[:, q:q + 1, :], ps[:, q:q + 1, 0:SEQ], ACT.Silu).then_inc(pair_act, 1)

            run("ffn", silu)
            run("down", lambda i, q: None)

            load_table(ACT.Sqrt)
            for t in range(TT):
                squares(3, t)
                root(3, t)

        @block.vector
        def _(dve):
            step = Steps(dve, dve_step)

            def tt(o, a, b, op):
                return nc.vector.tensor_tensor(o, a, b, op)

            def tsc(o, a, s1, op0, s2=None, op1=None):
                return nc.vector.tensor_scalar(o, a, s1, s2, op0, op1) if op1 else nc.vector.tensor_scalar(
                    o, a, s1, None, op0)

            def stt(o, a, s, b, op0, op1):
                return nc.vector.scalar_tensor_tensor(out=o, in0=a, scalar=s, in1=b, op0=op0, op1=op1)

            nc.vector.sem_inc(lo_done, LO_CREDIT)
            nc.vector.sem_inc(glu_done, PAIR_CREDIT)
            nc.vector.sem_inc(ff_done, PAIR_CREDIT)
            nc.vector.memset(tab_rows[BUCKETS:BUCKETS + 1, :], MASK).then_inc(tab_ready, 1)
            dve.wait_ge(row_in, 80)
            dve.wait_ge(dt_done, 1)
            step.then(tsc(lam[:, 0, :], lam[:, 0, :], -1e-4, ALU.min))
            tsc(rnd[:, 0, :], lam[:, 0, :], dt_row[:, 1:2], ALU.mult).then_inc(ang_done, 1)
            step.then(tsc(ang[:, 0, :], lam[:, 1, :], dt_row[:, 1:2], ALU.mult))
            step.then(tsc(ang[:, 1, :], ang[:, 0, :], float(STEP), ALU.mult))
            dve.wait_ge(mag_done, 1)
            step.then(tsc(rnd[:], ang[:], float(1 / (2 * np.pi)), ALU.mult, MAGIC, ALU.add))
            step.then(tsc(rnd[:], rnd[:], MAGIC, ALU.subtract))
            for k, piece in enumerate((TWO_PI_1, TWO_PI_2, TWO_PI_3)):
                step.then(stt(red[:], rnd[:], -piece, (red if k else ang)[:], ALU.mult, ALU.add))
            step.then(tsc(sin_cos[:, :, 0, :], red[:], -PI_IN, ALU.max, PI_IN, ALU.min))
            step.then(stt(sin_cos[:, :, 1, :], sin_cos[:, :, 0, :], -1.0, sin_cos[:, :, 0, :], ALU.mult, ALU.min))
            tsc(sin_cos[:, :, 1, :], sin_cos[:, :, 1, :], PI / 2, ALU.add).then_inc(red_done, 1)

            def mean_square(n, t):
                if n == 1:
                    dve.wait_ge(sumsq, t + 1)
                    total = stat[:, 4 * t:4 * t + 1]
                else:
                    dve.wait_ge(sumsq, TT + 8 * (n - 2) + 4 * (t + 1))
                    total = stat[:, 8 + t:9 + t]
                    step.then(nc.vector.reduce_sum(total, stat[:, 4 * t:4 * t + 4], AX_X))
                tsc(stat[:, 8 + t:9 + t], total, 1.0 / D_MODEL, ALU.mult, EPS, ALU.add).then_inc(std, 1)
                dve.wait_ge(rstd, 2 * (n - 1) + t + 1)
                step.then(nc.vector.reciprocal(stat[:, 12 + t:13 + t], stat[:, 10 + t:11 + t]))

            def scale_rows(dst, src, t):
                tsc(dst[:, t, :], src[:, t, :], stat[:, 12 + t:13 + t], ALU.mult).then_inc(xs_done, 1)

            for t in range(TT):
                mean_square(1, t)
                scale_rows(xs, xt, t)

            def cut_lo(phase, i, q):
                first, _, form = STREAM[phase]
                n = 4 * (first + i) + q
                if form == "rows":
                    dve.wait_ge(act_cut, (4 * OUT_BODIES if phase == "down" else 0) + 4 * i + q + 1)
                    src = (proj if phase == "out" else ff)[:, ds(4 * i + q, 1), :]
                    tt(act_lo[:, q:q + 1, :], src, act_hi[:, q:q + 1, :].bitcast(F32), ALU.subtract)
                dve.wait_ge(hi_done, n + 1)
                tt(part_tile(w_lo, form, q), raw_tile(form, q), part_tile(w_hi, form, q).bitcast(F32), ALU.subtract
                   ).then_inc(lo_done, 1)

            def run(phase, use):
                first, bodies, form = STREAM[phase]

                def body(i, last):
                    for q in range(4):
                        if q < 2:
                            cut_lo(phase, i, q + 2)
                        elif not last:
                            cut_lo(phase, i + 1, q - 2)
                        use(i, q)
                        if last and q >= 2 and NEXT[phase]:
                            cut_lo(NEXT[phase], 0, q - 2)

                with dve.Fori(0, bodies - 1) as i:
                    body(i, False)
                body(bodies - 1, True)

            def columns():
                dve.wait_ge(trig_done, 1)
                step(tt(ssm_rows[:, 0, :], mag[:], sin_cos[:, 0, 1, :], ALU.mult))
                step(tt(ssm_rows[:, 1, :], mag[:], sin_cos[:, 0, 0, :], ALU.mult))
                step(nc.vector.tensor_copy(ssm_rows[:, 4, :], sin_cos[:, 1, 1, :]))
                step(nc.vector.tensor_copy(ssm_rows[:, 5, :], sin_cos[:, 1, 0, :]))
                step(tt(ang[:, 0, :], lam[:, 0, :], lam[:, 0, :], ALU.mult))
                step.then(tt(ang[:, 1, :], lam[:, 1, :], lam[:, 1, :], ALU.mult))
                step(tsc(red[:, 0, :], ssm_rows[:, 0, :], -1.0, ALU.add))
                step.then(tt(red[:, 1, :], ang[:, 0, :], ang[:, 1, :], ALU.add))
                step(nc.vector.reciprocal(red[:, 1, :], red[:, 1, :]))
                step(tt(rnd[:, 0, :], red[:, 0, :], lam[:, 0, :], ALU.mult))
                step(tt(rnd[:, 1, :], ssm_rows[:, 1, :], lam[:, 1, :], ALU.mult))
                step(tt(ang[:, 0, :], ssm_rows[:, 1, :], lam[:, 0, :], ALU.mult))
                step.then(tt(ang[:, 1, :], red[:, 0, :], lam[:, 1, :], ALU.mult))
                step(tt(rnd[:, 0, :], rnd[:, 0, :], rnd[:, 1, :], ALU.add))
                step.then(tt(ang[:, 0, :], ang[:, 0, :], ang[:, 1, :], ALU.subtract))
                step(tt(ssm_rows[:, 2, :], rnd[:, 0, :], red[:, 1, :], ALU.mult))
                tt(ssm_rows[:, 3, :], ang[:, 0, :], red[:, 1, :], ALU.mult).then_inc(rows_done, 1)
                step.then(nc.vector.memset(d_wide[:], 0.0))
                dve.wait_ge(d_in, 16)
                nc.vector.tensor_copy(d_wide[:, :, STEP - 1], d_rows[:]).then_inc(wide_done, 1)

            cut_lo("in", 0, 0)
            cut_lo("in", 0, 1)

            def norm_lo(v, n):
                for k in range(KT):
                    dve.wait_ge(hh_done, KT * n + k // 4 * 4 + 4)
                    stt(h_lo[:, k, :].rearrange("p (t c) -> p t c", t=TT), flipped(k), vec[:, v + k:v + k + 1],
                        h_hi[:, k, :].bitcast(F32).rearrange("p (t c) -> p t c", t=TT), ALU.mult, ALU.subtract
                        ).then_inc(hl_done, 1)

            norm_lo(V_ATTN, 0)
            columns()
            dve.wait_ge(gate_hi_done, 1)
            tt(gate_lo[:], gate_raw[:], gate_hi[:].bitcast(F32), ALU.subtract).then_inc(gate_split, 1)

            for n in range(4):
                cut_lo("in", (2 + n) // 4, (2 + n) % 4)
            for n in range(3):
                cut_lo("in", 1 + (2 + n) // 4, (2 + n) % 4)
            dve.wait_ge(bcw_done, 2)
            dve.wait_ge(cols_done, 1)
            f_re = ssm_cols[:, 2, :].unsqueeze(2).broadcast_to([P, GROUPS, H])
            f_im = ssm_cols[:, 3, :].unsqueeze(2).broadcast_to([P, GROUPS, H])
            t1 = pb[:].rearrange("p g h s -> p (g h s)").rearrange("p (g h) -> p g h", h=H)
            t2 = pt[:].rearrange("p g h s -> p (g h s)").rearrange("p (g h) -> p g h", h=H)
            step(tt(t1, f_re, bs[:], ALU.mult))
            step.then(tt(t2, f_im, sw[:], ALU.mult))
            step(tt(bb[:], t1, t2, ALU.subtract))
            cut_lo("in", 2, 1)
            step.wait()
            step(tt(t1, f_re, sw[:], ALU.mult))
            step.then(tt(t2, f_im, bs[:], ALU.mult))
            tt(bbw[:], t1, t2, ALU.add).then_inc(bbw_done, 1)
            cut_lo("in", 2, 2)
            dve.wait_ge(pow_done, 1)
            for k in range(STEP):
                step(nc.vector.tensor_copy(inp_re[:, k, :], pow_re[:, STEP - 1 - k, :]))
                step(nc.vector.tensor_copy(inp_im[:, k, :], pow_im[:, STEP - 1 - k, :]))
            cut_lo("in", 2, 3)

            def inputs(i):
                g = ds(G8 * i, G8)
                shape = [P, G8, H, STEP]
                p_re = inp_re[:, :, g].rearrange("p k g -> p g k").unsqueeze(2).broadcast_to(shape)
                p_im = inp_im[:, :, g].rearrange("p k g -> p g k").unsqueeze(2).broadcast_to(shape)
                step(tt(pb[:], p_re, bb[:, g, :].unsqueeze(3).broadcast_to(shape), ALU.mult))
                step.then(tt(pt[:], p_im, bbw[:, g, :].unsqueeze(3).broadcast_to(shape), ALU.mult))
                tt(pb[:], pb[:], pt[:], ALU.subtract).then_inc(pb_done, 1)

            dve.wait_ge(bbw_done, 1)
            step.wait()
            inputs(0)
            cut_lo("in", 3, 0)
            dve.wait_ge(tables_done, 1)
            dve.wait_ge(dcol_done, 1)
            dve.wait_ge(delay_in, 48)
            step(tt(dmat[:], dcol[:].unsqueeze(2).broadcast_to([P, GROUPS, H]),
                    own_rows[:].unsqueeze(1).broadcast_to([P, GROUPS, H]), ALU.mult))
            cut_lo("in", 3, 1)
            step.then(nc.vector.memset(xp[:, :, 0:1], 0.0))

            def recurrence(j, a, last):
                i = 2 * j + a
                g = ds(G8 * i, G8)
                dve.wait_ge(m_copied, i + 1)
                tt(msb[:], msb[:], dmat[:, g, :], ALU.add).then_inc(m_done, 1)
                if not (last and a == 1):
                    dve.wait_ge(ssm_a_ps, i + 1)
                    inputs(i + 1)
                step.then(nc.vector.tensor_copy(decay[:], ssm_cols[:, 6, g].unsqueeze(2).broadcast_to([P, G8, NCH])))
                step(nc.vector.memset(decay[:, :, 0:1], 0.0))
                ps3 = ps[:, 7, 0:G8 * NCH].rearrange("p (g c) -> p g c", g=G8)
                dve.wait_ge(s_done, i + 1)
                step(tt(v1[:], rot_c[:, g, :], ssb[:].rearrange("p (g c) -> p g c", g=G8), ALU.mult))
                dve.wait_ge(swap_ps, i + 1)
                step.then(tt(v2[:], rot_s[:, g, :], ps3, ALU.mult))
                step.then(tt(v1[:], v1[:], v2[:], ALU.add))
                nc.vector.tensor_tensor_scan(zs[:], decay[:].rearrange("p g c -> p (g c)"),
                                             v1[:].rearrange("p g c -> p (g c)"), 0.0, ALU.mult, ALU.add
                                             ).then_inc(z_done, 1)
                dve.wait_ge(z_done, i + 1)
                step(tt(v1[:], rot_c[:, g, :], zs[:].rearrange("p (g c) -> p g c", g=G8), ALU.mult))
                if a == 0:
                    cut_lo("in", 3 + j, 2)
                elif not last:
                    cut_lo("in", 4 + j, 0)
                dve.wait_ge(zswap_ps, i + 1)
                step.then(tt(v2[:], rot_s[:, g, :], ps3, ALU.mult))
                tt(xp[:, :, 1:NCH], v1[:, :, 0:NCH - 1], v2[:, :, 0:NCH - 1], ALU.subtract).then_inc(xp_done, 1)
                if a == 0:
                    cut_lo("in", 3 + j, 3)
                elif not last:
                    cut_lo("in", 4 + j, 1)

            per = 2 * (2 + 2 + 3 + 2)
            n0 = step.n
            with dve.Fori(0, 3) as j:
                step.n = n0 + per * j
                recurrence(j, 0, False)
                recurrence(j, 1, False)
            step.n = n0 + per * 3
            recurrence(3, 0, True)
            recurrence(3, 1, True)

            step.wait()
            dve.wait_ge(xp_done, UT)
            dve.wait_ge(proj_done, 20 + PROJ_CREDIT)
            for n in range(2):
                for half in range(2):
                    for j in range(2):
                        rows = slice(DH * j, DH * (j + 1))
                        v = proj[DH * half:DH * (half + 1), 16 + 2 * n:18 + 2 * n, :]
                        tokens = bass.AP(v.tensor, v.offset + j, [v.ap[0], [SEQ, 2], [2, 16], [CMP_STRIDE, NCMP]])
                        pos = vec[rows, V_POS + 16 * n:V_POS + 16 * (n + 1)]
                        last = tt(kk[rows, n, :, half::2, :].rearrange("p k t i -> p t k i"), tokens,
                                  pos.unsqueeze(1).unsqueeze(3).broadcast_to([DH, 2, 16, NCMP]), ALU.add)
            last.then_inc(kk_done, 1)

            step.then(tsc(vec[:, V_BGLU + UT:V_POS], vec[:, V_BGLU + UT:V_POS], -1.0, ALU.mult))

            def logits(gp, b):
                u, n = b // 2, b % 2
                gl, tq = u // 2, u % 2
                ns = P * (tq + 1)
                at, unit = 8 * gp + b, 4 * gp + u
                heads = ds(8 * gp + R * gl, R)
                dve.wait_ge(sc_ps, at + 1)
                if b >= 2:
                    dve.wait_ge(prob_done, R * (at - 1))
                tt(lg[:, n, :, 0:ns], ps[:, 2:4, :].rearrange("p b (r s) -> p (b r) s", r=2)[:, :, 0:ns],
                   bt[:, heads, SEQ - ns:SEQ], ALU.add).then_inc(lg_done, 1)
                dve.wait_ge(lg_done, at + 1)
                step.then(nc.vector.reduce_max(nmax[:, n, :], lg[:, n, :, 0:ns], AX_X))
                tsc(nmax[:, n, :], nmax[:, n, :], -1.0, ALU.mult).then_inc(max_done, 1)
                if n == 0:
                    ncm = (ns - CMP_BLOCK) // CMP_STRIDE + 1
                    first = SEQ - ns + CMP_BLOCK - 1
                    dve.wait_ge(scc_ps, unit + 1)
                    if u > 0:
                        dve.wait_ge(probc_done, R * unit)
                    step.then(tt(lgc[:, :, 0:ncm], ps[:, 6, 0:R * 16].rearrange("p (r s) -> p r s", r=R)[:, :, 0:ncm],
                                 bt[:, heads, first:SEQ:CMP_STRIDE], ALU.add))
                    step.then(nc.vector.reduce_max(nmax[:, 2, :], lgc[:, :, 0:ncm], AX_X))
                    tsc(nmax[:, 2, :], nmax[:, 2, :], -1.0, ALU.mult, -0.1 * MASK, ALU.min).then_inc(maxc_done, 1)

            def combine(gp, u):
                gl, tq = u // 2, u % 2
                d = den[:, u % 2]
                step.then(tsc(d, d, 1e-30, ALU.max))
                step.then(nc.vector.reciprocal(d, d))
                gate = gates[:, tq, ds(24 * gp + 12 * gl, 12)].rearrange("p (r n) -> p n r", n=3)
                step(tt(wgt[:, 0:2], gate[:, 1:3], d[:, 0:2], ALU.mult))
                step.then(tt(wgt[:, 2:3], gate[:, 0:1], d[:, 2:3], ALU.mult))
                dve.wait_ge(o_ps, 4 * gp + u + 1)
                step(tt(ot[:, 0:2], ps[:, 7, :].rearrange("p (n r d) -> p n r d", n=2, r=R),
                        wgt[:, 0:2].unsqueeze(3).broadcast_to([P, 2, R, DH]), ALU.mult))
                step.then(tt(ot[:, 2], ps[:, 6, P:P + R * DH].rearrange("p (r d) -> p r d", r=R),
                             wgt[:, 2].unsqueeze(2).broadcast_to([P, R, DH]), ALU.mult))
                step.then(tt(ot[:, 0], ot[:, 0], ot[:, 1], ALU.add))
                tt(ot[:, 0], ot[:, 0], ot[:, 2], ALU.add).then_inc(ot_done, 1)

            def keys_of(gp):
                for b in range(2):
                    tsc(qs[:, b::2, :], proj[DH * b:DH * (b + 1), UT + 4 * gp:UT + 4 * gp + 4, :], DH ** -0.5, ALU.mult)
                for n in range(2):
                    for gl in range(2):
                        nc.vector.tensor_copy(kt[:, n, gl, :], proj[DH * gl:DH * (gl + 1), 20 + 4 * n + gp, :])
                    last = nc.vector.tensor_copy(vt[:, n, :], proj[:, 22 + 4 * n + gp, :])
                last.then_inc(qk_done, 1)

            def attend(gp):
                nc.vector.tensor_copy(vcg[:], vc[:, 2 * gp:2 * gp + 2, :])
                nc.vector.tensor_copy(kcg[:], kct[:, 2 * gp:2 * gp + 2, :]).then_inc(kcg_done, 1)
                cut_lo("glu", 2 * gp, 0)
                logits(gp, 0)
                for b in range(8):
                    u, n = b // 2, b % 2
                    if b < 7:
                        logits(gp, b + 1)
                    if n == 0 and u > 0:
                        combine(gp, u - 1)
                    if b < 7:
                        cut_lo("glu", 2 * gp + (b + 1) // 4, (b + 1) % 4)
                    if n == 1:
                        j = 4 * gp + u
                        dve.wait_ge(pair_act, j + 1)
                        gate = pair[:, u % 2, :]
                        step.then(tsc(gate, gate, 1.0, ALU.add))
                        step.then(nc.vector.reciprocal(gate, gate))
                        stt(proj[:, j, :], ps[:, 0, 0:SEQ], vec[:, V_BGLU + j:V_BGLU + j + 1], gate, ALU.add, ALU.mult
                            ).then_inc(glu_done, 1)
                if gp == 0:
                    keys_of(1)
                combine(gp, 3)

            dve.wait_ge(proj_done, 4 * IN_BODIES + PROJ_CREDIT)
            keys_of(0)
            dve.wait_ge(yhi_done, 1)
            tt(y_lo[:], yg[:], y_hi[:].bitcast(F32), ALU.subtract).then_inc(ylo_done, 1)
            dve.wait_ge(bt_in, 16)
            dve.wait_ge(kvc_done, 2)
            attend(0)
            attend(1)

            def add_residual(n, t):
                phase = {2: "out", 3: "down"}[n]
                if t == 0:
                    dve.wait_ge(t0_done, n - 1)
                else:
                    dve.wait_ge(mm_done, 4 * (STREAM[phase][0] + STREAM[phase][1]) + MM_CREDIT)
                for b in range(4):
                    tt(xr[:, t, 512 * b:512 * (b + 1)], ps[:, 2 * b + t, :], xr[:, t, 512 * b:512 * (b + 1)],
                       ALU.add).then_inc(x1_done, 1)

            cut_lo("out", 0, 0)
            cut_lo("out", 0, 1)
            run("out", lambda i, q: None)
            dve.wait_ge(xr_in, 32)
            for t in range(TT):
                add_residual(2, t)
                mean_square(2, t)
                scale_rows(xs2, xr, t)
            cut_lo("ffn", 0, 0)
            cut_lo("ffn", 0, 1)
            norm_lo(V_FFN, 1)

            def swiglu(i, q):
                if q >= 2:
                    j = 2 * i + q - 2
                    dve.wait_ge(pair_act, UT + j + 1)
                    dve.wait_ge(mm_done, 4 * (FFN_0 + i) + q + 1 + MM_CREDIT)
                    tt(ff[:, ds(j, 1), :], ps[:, q:q + 1, 0:SEQ], pair[:, q - 2:q - 1, :], ALU.mult
                       ).then_inc(ff_done, 1)

            run("ffn", swiglu)
            run("down", lambda i, q: None)
            dve.wait_ge(gain_in, 16)
            for t in range(TT):
                add_residual(3, t)
                mean_square(3, t)
                for b in range(2):
                    c = slice(D_MODEL // 2 * b, D_MODEL // 2 * (b + 1))
                    stt(ynorm[:, t, c], xr[:, t, c], stat[:, 12 + t:13 + t], gain[:, c], ALU.mult, ALU.mult
                        ).then_inc(fin_done, 1)

        @block.tensor
        def _(pe):
            def mm(o, a, b, start=True, stop=True):
                return nc.tensor.matmul(o, a, b, start=start, stop=stop)

            def flip(o, a):
                k = a.shape[0]
                return nc.tensor.transpose(o, a, ident[0:k, 0:k])

            nc.tensor.sem_inc(mm_done, MM_CREDIT)
            pe.wait_ge(const_in, 16)
            pe.wait_ge(vec_in, 80)
            flip(ps[:, 7, 0:NVEC], vec_rows[:]).then_inc(vec_ps, 1)
            def norm_flip(src, n):
                for t in range(TT):
                    pe.wait_ge(xs_done, TT * n + t + 1)
                    for k in range(KT):
                        last = flip(ps[:, k // 4 * 2 + t, P * (k % 4):P * (k % 4 + 1)],
                                    src[:, t, P * k:P * (k + 1)])
                last.then_inc(norm_ps, 1)

            pe.wait_ge(vec_done, 1)
            norm_flip(xs, 0)

            def column_tile(form, q, x_hi, x_lo, k0=0, k1=KT, bank=None, parts=None):
                hi, lo = part_tile(w_hi, form, q), part_tile(w_lo, form, q)
                o = ps[:, q if bank is None else bank, 0:SEQ]
                kn = UT if form == "glu" else KT
                for k in range(k0, min(k1, kn)):
                    if parts is not None:
                        pe.wait_ge(hl_done, parts + max(k + 1, 4))
                    mm(o, hi[:, k, :], x_hi[:, k, :], start=(k == 0), stop=False)
                    mm(o, hi[:, k, :], x_lo[:, k, :], start=False, stop=False)
                    last = mm(o, lo[:, k, :], x_hi[:, k, :], start=False, stop=(k == kn - 1))
                if k1 >= kn:
                    last.then_inc(mm_done, 1)

            def cut(phase, i, q):
                pe.wait_ge(lo_done, 4 * (STREAM[phase][0] + i) + q + 1 + LO_CREDIT)

            def proj_tile(i, q, k0=0, k1=KT):
                if k0 == 0:
                    cut("in", i, q)
                    pe.wait_ge(proj_done, 4 * i + q - 3 + PROJ_CREDIT)
                column_tile("cols", q, h_hi, h_lo, k0, k1)

            cut("in", 0, 0)
            pe.wait_ge(proj_done, PROJ_CREDIT)
            column_tile("cols", 0, h_hi, h_lo, parts=0)
            pe.wait_ge(rows_done, 1)
            for n in range(7):
                last = flip(ps[:, 6, GROUPS * n:GROUPS * (n + 1)], ssm_rows[:, n, :])
            last.then_inc(cols_ps, 1)
            pe.wait_ge(tab_ready, 1)
            pe.wait_ge(tab_in, 32)
            mm(ps[0:HEADS, 5, 0:SPAN], tab_rows[:], hot[:]).then_inc(bias_ps, 1)
            pe.wait_ge(wide_done, 1)
            flip(ps[:, 4, 0:GROUPS], d_wide[:].rearrange("g h s -> g (h s)")).then_inc(dcol_ps, 1)
            proj_tile(0, 1)
            pe.wait_ge(gate_split, 1)
            for k in range(KT):
                o = ps[0:NGATE, 7, 0:SEQ]
                mm(o, gate_hi[:, k, :], h_hi[:, k, :], start=(k == 0), stop=False)
                mm(o, gate_hi[:, k, :], h_lo[:, k, :], start=False, stop=False)
                last = mm(o, gate_lo[:, k, :], h_hi[:, k, :], start=False, stop=(k == KT - 1))
            last.then_inc(gatet_ps, 1)
            proj_tile(0, 2)
            pe.wait_ge(gatet_done, 1)
            for t in range(TT):
                last = flip(ps[:, 7, SEQ + NGATE * t:SEQ + NGATE * (t + 1)], gate_t[:, P * t:P * (t + 1)])
            last.then_inc(gate_ps, 1)
            proj_tile(0, 3)
            pe.wait_ge(b_in, 32)
            pe.wait_ge(cn_done, 1)
            pe.wait_ge(cols_done, 1)
            pe.wait_ge(bias_copied, 1)
            pe.wait_ge(dcol_done, 1)
            pe.wait_ge(gate_done, 1)
            for h in range(H):
                flip(ps[:, 4 + h // 8, GROUPS * (h % 8):GROUPS * (h % 8 + 1)],
                     b_rows[:, :, :, h].rearrange("g n p -> g (n p)"))
            for t in range(UT):
                last = flip(ps[:, 6 + t // 4, P * (t % 4):P * (t % 4 + 1)], cn[:, t, :])
            last.then_inc(bc_ps, 1)
            proj_tile(1, 0)
            proj_tile(1, 1)
            pe.wait_ge(bc_done, 2)
            pe.wait_ge(delay_in, 48)
            for n, t in enumerate((bs, cs)):
                for b in range(2):
                    last = mm(ps[:, 4 + 2 * n + b, :], swap[:], t[:].rearrange("p g h -> p (g h)")[:, 512 * b:512 * (b + 1)])
            last.then_inc(bcw_ps, 1)
            proj_tile(1, 2)
            proj_tile(1, 3)
            for q in range(4):
                proj_tile(2, q)
            pe.wait_ge(bcw_done, 2)
            pe.wait_ge(u_in, 16 * UT)

            with pe.Fori(0, 4) as j:
                for a in range(2):
                    i = 2 * j + a
                    pe.wait_ge(pb_done, i + 1)
                    for g in range(G8):
                        flip(ps[:, 4 + g // 4, P * (g % 4):P * (g % 4 + 1)], pb[:, g].rearrange("p h s -> p (h s)"))
                    for g in range(G8):
                        last = mm(ps[:, 6, H * g:H * (g + 1)], pb[:, g].rearrange("p h s -> p (h s)"),
                                  cs[:, ds(G8 * i + g, 1), :])
                    last.then_inc(ssm_a_ps, 1)
                    proj_tile(3 + j, 2 * a, 0, KT // 2)
                    pe.wait_ge(m_copied, i + 1)
                    pe.wait_ge(wt_done, i + 1)
                    for g in range(G8):
                        last = mm(ps[:, 6, P + NCH * g:P + NCH * (g + 1)], wt[:, g, :], uc[:, ds(i, 1), g, :])
                    last.then_inc(s_ps, 1)
                    pe.wait_ge(m_done, i + 1)
                    for t in range(STEP):
                        last = mm(ps[:, 4 + t // 4, P * (t % 4):P * (t % 4 + 1)], delay[:, t, :],
                                  msb[:].rearrange("p g h -> p (g h)"))
                    last.then_inc(toep_ps, 1)
                    proj_tile(3 + j, 2 * a, KT // 2, KT)
                    pe.wait_ge(s_done, i + 1)
                    mm(ps[:, 7, 0:G8 * NCH], swap[:], ssb[:]).then_inc(swap_ps, 1)
                    proj_tile(3 + j, 2 * a + 1, 0, KT // 2)
                    pe.wait_ge(z_done, i + 1)
                    mm(ps[:, 7, 0:G8 * NCH], swap[:], zs[:]).then_inc(zswap_ps, 1)
                    proj_tile(3 + j, 2 * a + 1, KT // 2, KT)
                    pe.wait_ge(xp_done, i + 1)
                    pe.wait_ge(toep_done, 2 * (i + 1))
                    pe.wait_ge(ca_done, i + 1)
                    for g in range(G8):
                        o = ps[:, 7, 256 + NCH * g:256 + NCH * (g + 1)]
                        mm(o, tp[:, g].rearrange("p h t -> p (h t)"), uc[:, ds(i, 1), g, :], stop=False)
                        last = mm(o, ca[:, g].rearrange("p h t -> p (h t)"), xp[:, g, :], start=False)
                    last.then_inc(y_ps, 1)
            pe.wait_ge(y_done, UT)
            pe.wait_ge(proj_done, 4 * IN_BODIES + PROJ_CREDIT)

            pe.wait_ge(cmp_in, 32)
            pe.wait_ge(w2_in, 32)
            pe.wait_ge(kk_done, 1)
            for n in range(2):
                for k in range(16):
                    last = mm(ps[0:NKV * NCMP, 0, P * n:P * (n + 1)], kk[:, n, k].rearrange("p g i -> p (g i)"),
                              w1[n][:, k, :], start=(k == 0), stop=(k == 15))
            last.then_inc(hid_ps, 1)
            pe.wait_ge(hidrows_done, 1)
            for n in range(2):
                last = flip(ps[:, 2, 64 * n:64 * n + NKV * NCMP], hid_rows[:, n, :])
            last.then_inc(hidt_ps, 1)
            pe.wait_ge(hid_done, 1)
            mm(ps[0:DH, 1, 0:NKV * NCMP], w2[:, 0, :], hid[:, 0, :])
            for g in range(NKV):
                last = mm(ps[0:NCMP, 1, 128 + DH * g:128 + DH * (g + 1)], hid[:, 1, NCMP * g:NCMP * (g + 1)],
                          w2[:, 1, :])
            last.then_inc(kvc_ps, 1)
            pe.wait_ge(kvc_done, 2)
            def scores(gp, b):
                u, n = b // 2, b % 2
                gl, tq = u // 2, u % 2
                ns = P * (tq + 1)
                ncm = (ns - CMP_BLOCK) // CMP_STRIDE + 1
                if b > 0:
                    pe.wait_ge(lg_done, 8 * gp + b)
                for r in range(R):
                    last = mm(ps[:, 2 + r // 2, 256 * (r % 2):256 * (r % 2) + ns],
                              qs[:, R * gl + r, P * tq:P * (tq + 1)], kt[:, n, gl, 0:ns])
                last.then_inc(sc_ps, 1)
                if n == 0:
                    if b == 0:
                        pe.wait_ge(kcg_done, gp + 1)
                    for r in range(R):
                        last = mm(ps[:, 6, 16 * r:16 * r + ncm], qs[:, R * gl + r, P * tq:P * (tq + 1)],
                                  kcg[:, gl, 0:ncm])
                    last.then_inc(scc_ps, 1)

            def values(gp, b):
                u, n = b // 2, b % 2
                gl, tq = u // 2, u % 2
                ncm = (P * (tq + 1) - CMP_BLOCK) // CMP_STRIDE + 1
                pe.wait_ge(pt_done, 8 * gp + b + 1)
                if n == 0 and u > 0:
                    pe.wait_ge(nsa_done, 4 * gp + u)
                for r in range(R):
                    for k in range(tq + 1):
                        last = mm(ps[:, 7, 256 * n + DH * r:256 * n + DH * (r + 1)], pts[:, r, k, :],
                                  vtok[:, n, k, DH * gl:DH * (gl + 1)], start=(k == 0), stop=(k == tq))
                if n == 1:
                    pe.wait_ge(ptc_done, 4 * gp + u + 1)
                    for r in range(R):
                        last = mm(ps[:, 6, P + DH * r:P + DH * (r + 1)], ptc[0:ncm, r, :], vcg[0:ncm, gl, :])
                    last.then_inc(o_ps, 1)

            def outputs(gp, u):
                pe.wait_ge(ot_done, 4 * gp + u + 1)
                for n in range(2):
                    last = flip(ps[:, 7, P * n:P * (n + 1)], ot[:, 0, 2 * n:2 * n + 2, :].rearrange("p r d -> p (r d)"))
                last.then_inc(otr_ps, 1)

            with pe.Fori(0, 2) as gp:
                pe.wait_ge(qk_done, gp + 1)
                for n in range(2):
                    for k in range(TT):
                        last = flip(ps[:, 4, P * (2 * n + k):P * (2 * n + k + 1)], vt[:, n, P * k:P * (k + 1)])
                last.then_inc(vt_ps, 1)
                scores(gp, 0)
                pe.wait_ge(vtok_done, gp + 1)
                for b in range(8):
                    u, n = b // 2, b % 2
                    tq = u % 2
                    ncm = (P * (tq + 1) - CMP_BLOCK) // CMP_STRIDE + 1
                    if b < 7:
                        if n == 1:
                            if u > 0:
                                pe.wait_ge(ot_done, 4 * gp + u)
                        scores(gp, b + 1)
                    if b > 0:
                        values(gp, b - 1)
                    i, q = 2 * gp + b // 4, b % 4
                    cut("glu", i, q)
                    if b == 0:
                        pe.wait_ge(ylo_done, 1)
                    if n == 0:
                        pe.wait_ge(glu_done, 4 * gp + u + PAIR_CREDIT)
                    column_tile("glu", q, y_hi, y_lo, bank=n)
                    pe.wait_ge(prob_done, R * (8 * gp + b + 1))
                    for r in range(R):
                        for k in range(tq + 1):
                            last = flip(ps[:, 4 + r // 2, 256 * (r % 2) + P * k:256 * (r % 2) + P * (k + 1)],
                                        pr[:, n, r, P * k:P * (k + 1)])
                    last.then_inc(pt_ps, 1)
                    if n == 1:
                        pe.wait_ge(probc_done, R * (4 * gp + u + 1))
                        if u < 3:
                            pe.wait_ge(maxc_done, 4 * gp + u + 2)
                        for r in range(R):
                            last = flip(ps[0:ncm, 6, P * r:P * (r + 1)], prc[:, r, 0:ncm])
                        last.then_inc(ptc_ps, 1)
                    elif u > 0:
                        outputs(gp, u - 1)
                values(gp, 7)
                outputs(gp, 3)

            def row_phase(phase):
                _, bodies, form = STREAM[phase]

                passes = ((act_hi, w_hi), (act_hi, w_lo), (act_lo, w_hi))

                def token_tile(q, t, first=False, final=False):
                    for n, (a, w) in enumerate(passes):
                        for b in range(4):
                            last = mm(ps[:, 2 * b + t, :], a[:, q, P * t:P * (t + 1)],
                                      w[:, q % 2, 512 * b:512 * (b + 1)],
                                      start=(first and n == 0), stop=(final and n == 2))
                    return last

                def tile(i, q, first=False):
                    cut(phase, i, q)
                    for t in range(TT):
                        last = token_tile(q, t, first)
                    last.then_inc(mm_done, 1)

                for q in range(4):
                    tile(0, q, first=(q == 0))
                with pe.Fori(1, bodies - 1) as i:
                    for q in range(4):
                        tile(i, q)
                for q in range(2):
                    tile(bodies - 1, q)
                for q in (2, 3):
                    cut(phase, bodies - 1, q)
                    last = token_tile(q, 0, final=(q == 3))
                last.then_inc(t0_done, 1)
                for q in (2, 3):
                    token_tile(q, 1, final=(q == 3)).then_inc(mm_done, 1)

            pe.wait_ge(glu_done, UT + PAIR_CREDIT)
            pe.wait_ge(nsa_done, 8)
            row_phase("out")
            norm_flip(xs2, 1)

            def ffn_tile(i, q, parts=None):
                cut("ffn", i, q)
                pe.wait_ge(ff_done, 2 * i + q % 2 - 1 + PAIR_CREDIT)
                column_tile("cols", q, h_hi, h_lo, parts=parts)

            for q in range(4):
                ffn_tile(0, q, KT if q == 0 else None)
            with pe.Fori(1, FFN_BODIES) as i:
                for q in range(4):
                    ffn_tile(i, q)
            pe.wait_ge(ff_done, D_FF // P + PAIR_CREDIT)
            row_phase("down")


_INS = ["x", "rpb_table", "attn_norm", "ffn_norm", "final_norm", "w_in", "ssm_a_re", "ssm_a_im", "ssm_log_dt",
        "ssm_b_re", "ssm_b_im", "ssm_c_re", "ssm_c_im", "ssm_d", "w_glu", "b_glu", "cmp_pos_k", "cmp_w1_k", "cmp_w2_k",
        "cmp_pos_v", "cmp_w1_v", "cmp_w2_v", "w_out", "w_ffn_gate", "w_ffn_up", "w_ffn_down"]


def selector_rows():
    rows = np.zeros((P, P * STEP + P + H), np.float32)
    h, s = np.divmod(np.arange(P), STEP)
    for t in range(STEP):
        to = s <= t
        rows[np.arange(P)[to] + STEP - 1 - t, P * t + np.arange(P)[to]] = 1
    k = np.arange(P)
    rows[k[NS:], P * STEP + k[NS:] - NS] = 1
    rows[k[:NS], P * STEP + k[:NS] + NS] = -1
    rows[k, P * (STEP + 1) + h] = 1
    return rows


def bucket_rows():
    dist = SEQ - 1 - np.arange(SPAN)
    n = np.maximum(dist, 1).astype(np.float32)
    exact = BUCKETS // 2
    large = exact + (np.log(n / np.float32(exact)) / np.float32(np.log(1024 / exact)) * np.float32(exact)
                     ).astype(np.int32)
    bucket = np.where(dist < exact, np.maximum(dist, 0), np.minimum(large, BUCKETS - 1))
    rows = np.zeros((BUCKETS + 1, SPAN), np.float32)
    valid = dist >= 0
    rows[bucket[valid], np.arange(SPAN)[valid]] = 1
    rows[BUCKETS, ~valid] = 1
    return rows


_CONST = [("selectors", selector_rows), ("onehot", bucket_rows)]


def kernel(**inputs):
    import concourse.bacc as _bacc
    from concourse.bass_utils import run_bass_kernel_spmd as _run

    nc = _bacc.Bacc("TRN2", target_bir_lowering=False, num_devices=1)
    arrays, args = {}, []
    given = [(name, np.ascontiguousarray(inputs[name])) for name in _INS]
    given += [(name, rows()) for name, rows in _CONST]
    for name, a in given:
        arrays[f"in_{name}_dram"] = a
        args.append(nc.dram_tensor(f"in_{name}_dram", a.shape, mybir.dt.from_np(a.dtype), kind="ExternalInput").ap())
    args.append(nc.dram_tensor("out_0_dram", (1, SEQ, D_MODEL), F32, kind="ExternalOutput").ap())
    build(nc, *args)
    r = _run(nc, [arrays], core_ids=[0])
    return r.results[0]["out_0_dram"]
```

```python
from contextlib import ExitStack

import numpy as np

import concourse.bass as bass
from concourse import mybir

F32 = mybir.dt.float32
F32R = mybir.dt.float32r
ACT = mybir.ActivationFunctionType
ALU = mybir.AluOpType
AX_X = mybir.AxisListType.X
ds = bass.ds

P = 128
SEQ = 256
D_MODEL = 2048
D_FF = 5632
KT = D_MODEL // P
TT = SEQ // P
D_SSM = 1024
UT = D_SSM // P
GROUPS = 64
H = 16
NS = 64
G8 = P // H
STEP = 8
NCH = SEQ // STEP
HEADS = 16
NKV = 4
R = HEADS // NKV
DH = 64
CMP_STRIDE = 16
CMP_BLOCK = 32
NCMP = SEQ // CMP_STRIDE - 1
BUCKETS = 32
EPS = 1e-6
MASK = -1e30
SPAN = 384
PROJ_TILES = 28
GATE_COL = PROJ_TILES * P
NGATE = 3 * HEADS
V_ATTN, V_FFN, V_BGLU, V_POS, NVEC = 0, 16, 32, 48, 80

IN_BODIES = PROJ_TILES // 4
GLU_BODIES = D_SSM // 256
OUT_BODIES = KT // 4
FFN_BODIES = D_FF // 256
DOWN_BODIES = D_FF // 512
GLU_0 = IN_BODIES
OUT_0 = GLU_0 + GLU_BODIES
FFN_0 = OUT_0 + OUT_BODIES
DOWN_0 = FFN_0 + FFN_BODIES

MAGIC = 12582912.0
PI = float(np.pi)
PI_IN = 3.1415925
TWO_PI_1 = 6.28125
TWO_PI_2 = float(np.float32(2 * np.pi - 6.28125))
TWO_PI_3 = float(2 * np.pi - 6.28125 - np.float64(np.float32(2 * np.pi - 6.28125)))

LO_CREDIT = 4
MM_CREDIT = 2
PROJ_CREDIT = 4
PAIR_CREDIT = 2


class Steps:

    def __init__(self, engine, sem):
        self.engine, self.sem, self.n = engine, sem, 0

    def __call__(self, instruction):
        instruction.then_inc(self.sem, 1)
        self.n = self.n + 1

    def wait(self):
        self.engine.wait_ge(self.sem, self.n)

    def then(self, instruction):
        self(instruction)
        self.wait()


def build(nc, x, rpb_table, attn_norm, ffn_norm, final_norm, w_in, a_re, a_im, log_dt, b_re, b_im, c_re, c_im,
          ssm_d, w_glu, b_glu, pos_k, w1_k, w2_k, pos_v, w1_v, w2_v, w_out, w_gate, w_up, w_down,
          selectors, onehot, out):
    bias_rows = nc.dram_tensor("bias_rows", [HEADS, SPAN], F32, kind="Internal").ap()
    u_turn = nc.dram_tensor("u_turn", [UT, G8, P, NCH], F32, kind="Internal").ap()
    y_turn = nc.dram_tensor("y_turn", [UT, G8, P, NCH], F32, kind="Internal").ap()
    bias_copies = nc.dram_tensor("bias_copies", [P, HEADS, SPAN], F32, kind="Internal").ap()

    with ExitStack() as ctx:
        place = [(nc.sbuf_base + 63) // 64 * 64]

        def lasting(name, shape, dtype=F32):
            t = nc.alloc_sbuf_tensor_at(name, shape, dtype, offset=place[0])
            place[0] += (4 * int(np.prod(shape[1:])) + 31) // 32 * 32
            return t

        def sem(name):
            return ctx.enter_context(nc.semaphore(name))

        raw = {"A": lasting("raw_a", [P, 4096]), "B": lasting("raw_b", [P, 4096])}
        w_hi = lasting("w_hi", [P, 2, 2048], F32R)
        w_lo = lasting("w_lo", [P, 2, 2048], F32R)
        act_at = place[0]
        act_hi = lasting("act_hi", [P, 4, SEQ], F32R)
        act_lo = lasting("act_lo", [P, 4, SEQ], F32R)
        pair = lasting("pair", [P, 2, SEQ])
        bias_sb = nc.alloc_sbuf_tensor_at("bias_sb", [HEADS, SPAN], F32, offset=place[0] - 4 * 2 * SEQ)
        hot = nc.alloc_sbuf_tensor_at("hot", [BUCKETS + 1, SPAN], F32, offset=place[0] - 4 * 2 * SEQ)
        proj_at = place[0]
        proj = lasting("proj", [P, PROJ_TILES, SEQ])
        delay = lasting("delay", [P, STEP, P])
        swap = lasting("swap", [P, P])
        vec_rows = lasting("vec_rows", [NVEC, P])
        vec = lasting("vec", [P, NVEC])
        gates = lasting("gates", [P, TT, NGATE])
        dcol = lasting("dcol", [P, GROUPS])
        own_rows = lasting("own_rows", [P, H])
        stat = lasting("stat", [P, 16])
        ssm_cols = lasting("ssm_cols", [P, 7, GROUPS])
        zone = place[0]
        ident = delay[:, STEP - 1, :]

        def placed(start):
            where = [zone + int(start * 1024)]

            def put(name, shape, dtype=F32):
                t = nc.alloc_sbuf_tensor_at(name, shape, dtype, offset=where[0])
                where[0] += (4 * int(np.prod(shape[1:])) + 31) // 32 * 32
                assert where[0] <= nc.sbuf_usable_end, (name, where[0], nc.sbuf_usable_end)
                return t
            return put

        put = placed(0)
        h_hi = put("h_hi", [P, KT, SEQ], F32R)
        h_lo = put("h_lo", [P, KT, SEQ], F32R)
        xt = put("xt", [P, TT, D_MODEL])
        xs = put("xs", [P, TT, D_MODEL])
        put = placed((proj_at - zone) / 1024 + 8)
        gate_hi = put("gate_hi", [P, KT, NGATE], F32R)
        gate_lo = put("gate_lo", [P, KT, NGATE], F32R)
        gate_t = put("gate_t", [NGATE, SEQ])
        tab_rows = put("tab_rows", [BUCKETS + 1, HEADS])
        gate_raw = placed(94.5)("gate_raw", [P, KT, NGATE])
        w2 = placed(97.5)("w2", [P, 2, DH])
        put = placed((proj_at - zone) / 1024 + 16)
        lam = put("lam", [GROUPS, 2, P])
        dt_row = put("dt_row", [GROUPS, 8])
        ang = put("ang", [GROUPS, 2, P])
        rnd = put("rnd", [GROUPS, 2, P])
        red = put("red", [GROUPS, 2, P])
        sin_cos = put("sin_cos", [GROUPS, 2, 2, P])
        mag = put("mag", [GROUPS, P])
        ssm_rows = put("ssm_rows", [GROUPS, 7, P])
        d_rows = put("d_rows", [GROUPS, H])
        d_wide = put("d_wide", [GROUPS, H, STEP])
        put = placed(32)
        pow_re = put("pow_re", [P, STEP + 1, GROUPS])
        pow_im = put("pow_im", [P, STEP + 1, GROUPS])
        inp_re = put("inp_re", [P, STEP, GROUPS])
        inp_im = put("inp_im", [P, STEP, GROUPS])
        rot_c = put("rot_c", [P, GROUPS, NCH])
        rot_s = put("rot_s", [P, GROUPS, NCH])
        bb = put("bb", [P, GROUPS, H])
        bbw = put("bbw", [P, GROUPS, H])
        cs = put("cs", [P, GROUPS, H])
        cw = put("cw", [P, GROUPS, H])
        b_rows = nc.alloc_sbuf_tensor_at("b_rows", [GROUPS, 2, NS, H], F32, offset=act_at)
        put = placed(73)
        cn = put("cn", [P, UT, P])
        bs = put("bs", [P, GROUPS, H])
        sw = put("sw", [P, GROUPS, H])
        tab1 = put("tab1", [P, 1024])
        tab2 = put("tab2", [P, 1024])
        phasor = put("phasor", [P, 2, 2, GROUPS])
        pb = nc.alloc_sbuf_tensor_at("pb", [P, G8, H, STEP], F32, offset=act_at)
        pt = nc.alloc_sbuf_tensor_at("pt", [P, G8, H, STEP], F32, offset=act_at + 4 * 1024)
        v1 = nc.alloc_sbuf_tensor_at("v1", [P, G8, NCH], F32, offset=act_at + 8 * 1024)
        v2 = nc.alloc_sbuf_tensor_at("v2", [P, G8, NCH], F32, offset=act_at + 9 * 1024)
        put = placed(73)
        wt = put("wt", [P, G8, P])
        tp = put("tp", [P, G8, H, STEP])
        ca = put("ca", [P, G8, H, STEP])
        cat = put("cat", [P, G8, H, STEP])
        msb = put("msb", [P, G8, H])
        ssb = put("ssb", [P, G8 * NCH])
        decay = put("decay", [P, G8, NCH])
        zs = put("zs", [P, G8 * NCH])
        xp = put("xp", [P, G8, NCH])
        dmat = put("dmat", [P, GROUPS, H])
        assert STEP * NCH == SEQ
        uc = proj[:, 0:UT, :].rearrange("p t (g c) -> p t g c", g=G8)
        yg = placed(73)("yg", [P, UT, SEQ])
        put = placed(32)
        y_hi = put("y_hi", [P, UT, SEQ], F32R)
        y_lo = put("y_lo", [P, UT, SEQ], F32R)
        put = placed(0)
        bt = put("bt", [P, HEADS, SEQ])
        qs = put("qs", [DH, 2 * R, SEQ])
        kt = put("kt", [DH, 2, 2, SEQ])
        vt = put("vt", [P, 2, SEQ])
        vtok = put("vtok", [P, 2, TT, P])
        put = placed(48)
        w1 = [raw[slot][:, 2048:4096].rearrange("p (k n) -> p k n", n=P) for slot in "AB"]
        kk = put("kk", [P, 2, CMP_BLOCK // 2, NKV, NCMP])
        put = placed(64)
        hid_rows = put("hid_rows", [NKV * NCMP, 2, P])
        hid = put("hid", [P, 2, NKV * NCMP])
        kct = put("kct", [DH, NKV, NCMP])
        vc = put("vc", [NCMP, NKV, DH])
        kcg = put("kcg", [DH, 2, NCMP])
        vcg = put("vcg", [NCMP, 2, DH])
        put = placed(48)
        lg = put("lg", [P, 2, R, SEQ])
        pr = put("pr", [P, 2, R, SEQ])
        put = placed(80.5)
        pts = put("pts", [P, R, TT, P])
        lgc = put("lgc", [P, R, 16])
        prc = put("prc", [P, R, 16])
        ptc = put("ptc", [NCMP, R, P])
        nmax = put("nmax", [P, 3, R])
        den = put("den", [P, 2, 3, R])
        wgt = put("wgt", [P, 3, R])
        ot = put("ot", [P, 3, R, DH])
        a_sb = put("a_sb", [P, 2, SEQ])
        put = placed(32)
        xr = put("xr", [P, TT, D_MODEL])
        ff = put("ff", [P, D_FF // P, SEQ])
        xs2 = placed(48)("xs2", [P, TT, D_MODEL])
        put = placed((proj_at - zone) / 1024)
        gain = put("gain", [P, D_MODEL])
        ynorm = put("ynorm", [P, TT, D_MODEL])

        ps = ctx.enter_context(nc.psum_tensor("ps", [P, 8, 512], F32))

        const_in, delay_in, vec_in, row_in, d_in, b_in, c_in = map(
            sem, ("const_in", "delay_in", "vec_in", "row_in", "d_in", "b_in", "c_in"))
        x_in = [sem("x0_in"), sem("x1_in")]
        u_out, u_in, y_out, y_in = map(sem, ("u_out", "u_in", "y_out", "y_in"))
        raw_in = {"A": sem("raw_a_in"), "B": sem("raw_b_in")}
        gatew_in, cmp_in, tab_in, bias_out, bt_in, xr_in, gain_in, out_done = map(
            sem, ("gatew_in", "cmp_in", "tab_in", "bias_out", "bt_in", "xr_in", "gain_in", "out_done"))
        hi_done, lo_done, mm_done = sem("hi_done"), sem("lo_done"), sem("mm_done")
        proj_done, pair_act, glu_done, ff_done = map(sem, ("proj_done", "pair_act", "glu_done", "ff_done"))
        sumsq, std, rstd, xs_done, norm_ps, hh_done, hl_done, x1_done = map(
            sem, ("sumsq", "std", "rstd", "xs_done", "norm_ps", "hh_done", "hl_done", "x1_done"))
        vec_ps, vec_done = sem("vec_ps"), sem("vec_done")
        dt_done, ang_done, mag_done, red_done, trig_done, rows_done, cols_ps, cols_done = map(
            sem, ("dt_done", "ang_done", "mag_done", "red_done", "trig_done", "rows_done", "cols_ps", "cols_done"))
        gate_hi_done, gate_split, gate_ps, gate_done = map(sem, ("gate_hi_done", "gate_split", "gate_ps", "gate_done"))
        cn_done, bc_ps, bc_done, bcw_ps, bcw_done, tables_done, dcol_ps, dcol_done = map(
            sem, ("cn_done", "bc_ps", "bc_done", "bcw_ps", "bcw_done", "tables_done", "dcol_ps", "dcol_done"))
        pb_done, ssm_a_ps, m_done, wt_done, s_ps, s_done, toep_ps, toep_done = map(
            sem, ("pb_done", "ssm_a_ps", "m_done", "wt_done", "s_ps", "s_done", "toep_ps",
                  "toep_done"))
        m_copied = sem("m_copied")
        swap_ps, z_done, zswap_ps, xp_done, ca_done, y_ps, y_done = map(
            sem, ("swap_ps", "z_done", "zswap_ps", "xp_done", "ca_done", "y_ps", "y_done"))
        gelu_done, yhi_done, ylo_done = map(sem, ("gelu_done", "yhi_done", "ylo_done"))
        wide_done, bbw_done, gatet_done, gatet_ps = map(sem, ("wide_done", "bbw_done", "gatet_done", "gatet_ps"))
        dve_step, act_step, pool_step = sem("dve_step"), sem("act_step"), sem("pool_step")
        hidrows_done, hidt_ps = sem("hidrows_done"), sem("hidt_ps")
        w2_in, kk_done, hid_ps, hid_done, kvc_ps, kvc_done, kcg_done, vcg_done, pow_done = map(
            sem, ("w2_in", "kk_done", "hid_ps", "hid_done", "kvc_ps", "kvc_done", "kcg_done", "vcg_done", "pow_done"))
        a_act = sem("a_act")
        t0_done, act_cut = sem("t0_done"), sem("act_cut")
        tab_ready, bias_ps, bias_copied = sem("tab_ready"), sem("bias_ps"), sem("bias_copied")
        qk_done, vt_ps, vtok_done = sem("qk_done"), sem("vt_ps"), sem("vtok_done")
        sc_ps, lg_done, max_done, prob_done, pt_ps, pt_done, o_ps, ot_done, otr_ps, nsa_done = map(
            sem, ("sc_ps", "lg_done", "max_done", "prob_done", "pt_ps", "pt_done", "o_ps", "ot_done", "otr_ps",
                  "nsa_done"))
        scc_ps, maxc_done, probc_done, ptc_ps, ptc_done = map(
            sem, ("scc_ps", "maxc_done", "probc_done", "ptc_ps", "ptc_done"))
        glu_in = {"A": sem("glu_a_in"), "B": sem("glu_b_in")}
        fin_dve, fin_act = sem("fin_dve"), sem("fin_act")
        gained, scales_done = sem("gained"), sem("scales_done")

        def raw_tile(form, q):
            t = raw["AB"[q // 2]]
            if form == "rows":
                return t[:, 2048 * (q % 2):2048 * (q % 2 + 1)]
            if form == "glu":
                return t[:, 1024 * (q % 2):1024 * (q % 2 + 1)].rearrange("p (k n) -> p k n", n=P)
            return t[:].rearrange("p (k n) -> p k n", k=KT)[:, :, P * (q % 2):P * (q % 2 + 1)]

        def part_tile(t, form, q):
            if form == "rows":
                return t[:, q % 2, :]
            k = {"glu": UT, "cols": KT}[form]
            return t[:, q % 2, 0:P * k].rearrange("p (k n) -> p k n", k=k)

        STEPS = 4 * NKV

        def parts_of(at):
            unit, n = at // 2, at % 2
            tq = unit % 2
            keys = P * (tq + 1)
            return unit, n, unit // 4, unit // 2 % 2, tq, keys, (keys - CMP_BLOCK) // CMP_STRIDE + 1

        def flipped(k):
            return ps[:, k // 4 * 2:k // 4 * 2 + 2, P * (k % 4):P * (k % 4 + 1)]

        STREAM = {"in": (0, IN_BODIES, "cols"), "glu": (GLU_0, GLU_BODIES, "glu"), "out": (OUT_0, OUT_BODIES, "rows"),
                  "ffn": (FFN_0, FFN_BODIES, "cols"), "down": (DOWN_0, DOWN_BODIES, "rows")}
        NEXT = {"in": None, "glu": None, "out": None, "ffn": "down", "down": None}

        block = ctx.enter_context(nc.Block())

        @block.sync
        def _(sp):
            for t in range(TT):
                sp.dma_start(xt[:, t, :], x[0, P * t:P * (t + 1), :]).then_inc(x_in[t], 16)

            def chunk(body, slot, src):
                if not isinstance(body, int) or body > 0:
                    sp.wait_ge(lo_done, 4 * body + (2 if slot == "A" else 4))
                k, n = src.shape[1], src.shape[2]
                dst = raw[slot][:, 0:k * n].rearrange("p (k n) -> p k n", k=k)
                sp.dma_start(dst, src).then_inc(raw_in[slot], 16)

            def cols(w, c):
                return w[0, :, ds(c, 256)].rearrange("(k p) n -> p k n", p=P)

            def rows(w, r):
                return w[0, ds(r, 256), :].rearrange("(k p) n -> p k n", p=P)

            def load_in(i, slot):
                chunk(i, slot, cols(w_in, 512 * i + (256 if slot == "B" else 0)))

            def turn_u(t):
                sp.wait_ge(proj_done, t + 1 + PROJ_CREDIT)
                sp.dma_start(u_turn[t].rearrange("g (h s) c -> (g h) (s c)", s=STEP), proj[:, t, :]
                             ).then_inc(u_out, 16)
                sp.wait_ge(u_out, 16 * (t + 1))
                sp.dma_start(uc[:, t], u_turn[t].rearrange("g r c -> r g c")).then_inc(u_in, 16)

            def turn_y(t):
                sp.wait_ge(y_done, t + 1)
                sp.dma_start(y_turn[ds(t, 1)].rearrange("o g r c -> r (o g) c"),
                             proj[:, ds(t, 1), :].rearrange("p o (g c) -> p (o g) c", g=G8)).then_inc(y_out, 16)
                sp.wait_ge(y_out, 16 * (t + 1))
                sp.dma_start(proj[:, ds(t, 1), :],
                             y_turn[ds(t, 1)].rearrange("o g (h s) c -> (g h) o (s c)", s=STEP)).then_inc(y_in, 16)

            sp.wait_ge(row_in, 80)
            sp.wait_ge(vec_in, 80)
            load_in(0, "A")
            load_in(0, "B")
            sp.dma_start(d_rows[:], ssm_d[0].rearrange("(g h) -> g h", h=H)).then_inc(d_in, 16)
            sp.dma_start(tab_rows[0:BUCKETS, :], rpb_table[:, :]).then_inc(tab_in, 16)
            sp.dma_start(hot[:], onehot[:, :]).then_inc(tab_in, 16)
            sp.dma_start(delay[:, 0:STEP - 1, :].rearrange("p t n -> p (t n)"), selectors[:, 0:P * (STEP - 1)]
                          ).then_inc(delay_in, 16)
            sp.dma_start(swap[:], selectors[:, P * STEP:P * (STEP + 1)]).then_inc(delay_in, 16)
            sp.dma_start(own_rows[:], selectors[:, P * (STEP + 1):]).then_inc(delay_in, 16)
            for n, w in enumerate((w2_k, w2_v)):
                sp.dma_start(w2[:, n], w[0]).then_inc(w2_in, 16)
            for n, src in enumerate((b_re, b_im)):
                sp.dma_start(b_rows[:, n], src[0]).then_inc(b_in, 16)
            sp.dma_start(gate_raw[:], w_in[0, :, GATE_COL:GATE_COL + NGATE].rearrange("(k p) n -> p k n", p=P)
                         ).then_inc(gatew_in, 16)
            load_in(1, "A")
            for i in range(2):
                turn_u(4 * i)
                turn_u(4 * i + 1)
                load_in(i + 1, "B")
                turn_u(4 * i + 2)
                turn_u(4 * i + 3)
                load_in(i + 2, "A")
            load_in(3, "B")
            with sp.Fori(0, 3) as j:
                load_in(4 + j, "A")
                load_in(4 + j, "B")
                turn_y(2 * j)
                turn_y(2 * j + 1)

            def load_glu(i):
                for n, slot in enumerate("AB"):
                    sp.wait_ge(lo_done, 4 * (GLU_0 + i) + 2 * (n + 1))
                    for half in range(2):
                        sp.dma_start(raw[slot][:, 1024 * half:1024 * (half + 1)].rearrange("p (k n) -> p k n", n=P),
                                     w_glu[0, :, ds(D_SSM * half + 256 * i + P * n, P)].rearrange(
                                         "(k p) n -> p k n", p=P)).then_inc(glu_in[slot], 16)

            def load_out(i):
                chunk(OUT_0 + i, "A", rows(w_out, 512 * i))
                chunk(OUT_0 + i, "B", rows(w_out, 512 * i + 256))

            def load_ffn(i):
                chunk(FFN_0 + i, "A", cols(w_gate, 256 * i))
                chunk(FFN_0 + i, "B", cols(w_up, 256 * i))

            def load_down(i):
                chunk(DOWN_0 + i, "A", rows(w_down, 512 * i))
                chunk(DOWN_0 + i, "B", rows(w_down, 512 * i + 256))

            load_glu(0)
            for n, w in enumerate((w1_k, w1_v)):
                sp.dma_start(w1[n], w[0].rearrange("(k p) n -> p k n", p=P)).then_inc(cmp_in, 16)
            turn_y(6)
            turn_y(7)
            sp.wait_ge(mm_done, 4 * IN_BODIES + MM_CREDIT)
            sp.wait_ge(bias_out, 32)
            sp.dma_start(bt[:], bass.AP(bias_copies.tensor, P - 1, [[HEADS * SPAN - 1, P], [SPAN, HEADS], [1, SEQ]])
                         ).then_inc(bt_in, 16)
            with sp.Fori(1, GLU_BODIES) as i:
                load_glu(i)
            load_out(0)
            sp.wait_ge(mm_done, 4 * OUT_0 + MM_CREDIT)
            for t in range(TT):
                sp.dma_start(xr[:, t, :], x[0, P * t:P * (t + 1), :]).then_inc(xr_in, 16)
            with sp.Fori(1, OUT_BODIES) as i:
                load_out(i)
            load_ffn(0)
            sp.wait_ge(mm_done, 4 * FFN_0 + MM_CREDIT)
            sp.dma_start(gain[:], bass.AP(final_norm.tensor, 0, [[0, P], [1, D_MODEL]])).then_inc(gain_in, 16)
            with sp.Fori(1, FFN_BODIES) as i:
                load_ffn(i)
            with sp.Fori(0, DOWN_BODIES) as i:
                load_down(i)
            for t, b, finished, count in ((0, 0, fin_dve, 1), (0, 1, fin_act, 1), (1, 0, fin_dve, 2),
                                          (1, 1, fin_dve, 3)):
                c = slice(D_MODEL // 2 * b, D_MODEL // 2 * (b + 1))
                sp.wait_ge(finished, count)
                sp.dma_start(out[0, P * t:P * (t + 1), c], ynorm[:, t, c]).then_inc(out_done, 16)
            sp.wait_ge(out_done, 32 * TT)
            sp.wait_ge(u_in, 16 * UT)
            sp.wait_ge(y_in, 16 * UT)

        @block.gpsimd
        def _(pool):
            step = Steps(pool, pool_step)
            pool.wait_ge(row_in, 80)
            for n, src in enumerate((c_re, c_im)):
                pool.dma_start(cn[:, :, NS * n:NS * (n + 1)], src[0].rearrange("(t g) h p -> (g h) t p", g=G8)
                               ).then_inc(c_in, 16)
            pool.wait_ge(bias_copied, 1)
            pool.dma_start(bias_rows[:, :], bias_sb[:]).then_inc(bias_out, 16)
            pool.wait_ge(c_in, 32)
            nc.gpsimd.tensor_scalar(cn[:, :, NS:P], cn[:, :, NS:P], -1.0, None, ALU.mult).then_inc(cn_done, 1)
            pool.wait_ge(bias_out, 16)
            pool.dma_start(bias_copies[:, :, :], bass.AP(bias_rows.tensor, 0, [[0, P], [1, HEADS * SPAN]])
                           ).then_inc(bias_out, 16)
            pool.wait_ge(cols_done, 1)
            pool.wait_ge(norm_ps, 1)

            def mul(o, a, b):
                step(nc.gpsimd.tensor_tensor(o, a, b, ALU.mult))

            def product(out_re, out_im, x_re, x_im, y_re, y_im, t1, t2):
                mul(t1, x_re, y_re)
                mul(t2, x_im, y_im)
                step.wait()
                step.then(nc.gpsimd.tensor_tensor(out_re, t1, t2, ALU.subtract))
                mul(t1, x_re, y_im)
                mul(t2, x_im, y_re)
                step.wait()
                step.then(nc.gpsimd.tensor_tensor(out_im, t1, t2, ALU.add))

            step(nc.gpsimd.memset(pow_re[:, 0, :], 1.0))
            step(nc.gpsimd.memset(pow_im[:, 0, :], 0.0))
            step(nc.gpsimd.tensor_copy(pow_re[:, 1, :], ssm_cols[:, 0, :]))
            step.then(nc.gpsimd.tensor_copy(pow_im[:, 1, :], ssm_cols[:, 1, :]))
            m = 1
            while m < STEP:
                t1 = tab1[:, 0:m * GROUPS].rearrange("p (k g) -> p k g", g=GROUPS)
                t2 = tab2[:, 0:m * GROUPS].rearrange("p (k g) -> p k g", g=GROUPS)
                product(pow_re[:, m + 1:2 * m + 1, :], pow_im[:, m + 1:2 * m + 1, :],
                        pow_re[:, 1:m + 1, :], pow_im[:, 1:m + 1, :],
                        pow_re[:, m:m + 1, :].broadcast_to([P, m, GROUPS]),
                        pow_im[:, m:m + 1, :].broadcast_to([P, m, GROUPS]), t1, t2)
                m *= 2
            step.wait()
            nc.gpsimd.sem_inc(pow_done, 1)
            step(nc.gpsimd.memset(rot_c[:, :, 0:1], 1.0))
            step(nc.gpsimd.memset(rot_s[:, :, 0:1], 0.0))
            step(nc.gpsimd.tensor_copy(phasor[:, 0, 0, :], ssm_cols[:, 4, :]))
            step.then(nc.gpsimd.tensor_copy(phasor[:, 0, 1, :], ssm_cols[:, 5, :]))
            m, n = 1, 0
            while m < NCH:
                u_re, u_im = phasor[:, n, 0, :], phasor[:, n, 1, :]
                t1 = tab1[:, 0:m * GROUPS].rearrange("p (g c) -> p g c", c=m)
                t2 = tab2[:, 0:m * GROUPS].rearrange("p (g c) -> p g c", c=m)
                product(rot_c[:, :, m:2 * m], rot_s[:, :, m:2 * m], rot_c[:, :, 0:m], rot_s[:, :, 0:m],
                        u_re.unsqueeze(2).broadcast_to([P, GROUPS, m]),
                        u_im.unsqueeze(2).broadcast_to([P, GROUPS, m]), t1, t2)
                if 2 * m < NCH:
                    product(phasor[:, 1 - n, 0, :], phasor[:, 1 - n, 1, :], u_re, u_im, u_re, u_im,
                            tab1[:, 0:GROUPS], tab2[:, 0:GROUPS])
                m, n = 2 * m, 1 - n
            step.wait()
            nc.gpsimd.sem_inc(tables_done, 1)

            def readout(i):
                g = ds(G8 * i, G8)
                shape = [P, G8, H, STEP]
                p_re = pow_re[:, 1:STEP + 1, g].rearrange("p k g -> p g k").unsqueeze(2).broadcast_to(shape)
                p_im = pow_im[:, 1:STEP + 1, g].rearrange("p k g -> p g k").unsqueeze(2).broadcast_to(shape)
                mul(ca[:], p_re, cs[:, g, :].unsqueeze(3).broadcast_to(shape))
                mul(cat[:], p_im, cw[:, g, :].unsqueeze(3).broadcast_to(shape))
                step.wait()
                nc.gpsimd.tensor_tensor(ca[:], ca[:], cat[:], ALU.add).then_inc(ca_done, 1)

            pool.wait_ge(bcw_done, 2)
            pool.wait_ge(bbw_done, 1)
            readout(0)
            n0 = step.n
            with pool.Fori(1, UT) as i:
                step.n = n0 + 2 * (i - 1)
                pool.wait_ge(y_ps, i)
                pool.wait_ge(ca_done, i)
                readout(i)
            pool.wait_ge(gain_in, 16)
            pool.wait_ge(x1_done, 8 + 4)
            c = slice(D_MODEL // 2, D_MODEL)
            nc.gpsimd.tensor_tensor(ynorm[:, 0, c], xr[:, 0, c], gain[:, c], ALU.mult).then_inc(gained, 1)

        @block.scalar
        def _(act):
            step = Steps(act, act_step)

            def copy(o, a, **kw):
                return nc.scalar.activation(o, a, ACT.Copy, **kw)

            nc.scalar.sem_inc(proj_done, PROJ_CREDIT)
            act.dma_start(ident, selectors[:, P * (STEP - 1):P * STEP]).then_inc(const_in, 16)
            for n, src in enumerate((a_re, a_im)):
                for half in range(2):
                    act.dma_start(lam[:, n, NS * half:NS * (half + 1)], src[0]).then_inc(row_in, 16)
            act.dma_start(dt_row[:, 0:1], log_dt[0].rearrange("(g o) -> g o", o=1)).then_inc(row_in, 16)
            at = 0
            for src in (attn_norm[0], ffn_norm[0], b_glu[0]):
                n = src.shape[0] // P
                act.dma_start(vec_rows[at:at + n, :], src.rearrange("(k p) -> k p", p=P)).then_inc(vec_in, 16)
                at += n
            for n, src in enumerate((pos_k[0], pos_v[0])):
                act.dma_start(vec_rows[at:at + 16, :], src.rearrange("(k j) d -> k (j d)", j=2)).then_inc(vec_in, 16)
                at += 16
            def square(t):
                nc.scalar.activation(xs[:, t, :], xt[:, t, :], ACT.Square, accum_out=stat[:, 4 * t:4 * t + 1]
                                     ).then_inc(sumsq, 1)

            def squares(n, t):
                for b in range(4):
                    act.wait_ge(x1_done, 8 * (n - 2) + 4 * t + b + 1)
                    nc.scalar.activation(xs2[:, t, 512 * b:512 * (b + 1)], xr[:, t, 512 * b:512 * (b + 1)], ACT.Square,
                                         accum_out=stat[:, 4 * t + b:4 * t + b + 1]).then_inc(sumsq, 1)

            def load_table(function):
                nc.scalar.activation(stat[:, 14:15], vec[:, 0:1], function)

            act.wait_ge(x_in[0], 16)
            square(0)
            act.wait_ge(row_in, 80)
            nc.scalar.activation(dt_row[:, 1:2], dt_row[:, 0:1], ACT.Exp).then_inc(dt_done, 1)
            act.wait_ge(x_in[1], 16)
            square(1)
            act.wait_ge(ang_done, 1)
            nc.scalar.activation(mag[:], rnd[:, 0, :], ACT.Exp)
            nc.scalar.activation(ssm_rows[:, 6, :], rnd[:, 0, :], ACT.Exp, scale=float(STEP)).then_inc(mag_done, 1)

            def root(n, t0=0, t1=TT):
                act.wait_ge(std, n)
                nc.scalar.activation(stat[:, 10 + t0:10 + t1], stat[:, 8 + t0:8 + t1], ACT.Sqrt).then_inc(rstd, 1)

            act.wait_ge(vec_ps, 1)
            copy(vec[:], ps[:, 7, 0:NVEC]).then_inc(vec_done, 1)
            root(1)

            def cut_hi(phase, i, q):
                first, _, form = STREAM[phase]
                n = 4 * (first + i) + q
                if phase == "glu":
                    act.wait_ge(glu_in["AB"[q // 2]], 32 * (i + 1))
                elif q % 2 == 0:
                    past = first - (GLU_BODIES if first > GLU_0 else 0)
                    act.wait_ge(raw_in["AB"[q // 2]], 16 * (past + i + 1))
                if form == "rows":
                    whole = not (isinstance(i, int) and i == 0 and q < 2)
                    if phase == "out":
                        act.wait_ge(glu_done, (4 * i + q + 1 if isinstance(i, int) and i < 2 else UT) + PAIR_CREDIT)
                        src = proj[:, ds(4 * i + q, 1), :]
                    else:
                        act.wait_ge(ff_done, (D_FF // P if whole else 2) + PAIR_CREDIT)
                        src = ff[:, ds(4 * i + q, 1), :]
                    copy(act_hi[:, q:q + 1, :], src).then_inc(act_cut, 1)
                act.wait_ge(mm_done, n - 2 + 1 + MM_CREDIT if not isinstance(n, int) or n >= 2 else MM_CREDIT)
                copy(part_tile(w_hi, form, q), raw_tile(form, q)).then_inc(hi_done, 1)

            def run(phase, use):
                first, bodies, form = STREAM[phase]

                def body(i, last):
                    for q in range(4):
                        if q < 2:
                            cut_hi(phase, i, q + 2)
                        elif not last:
                            cut_hi(phase, i + 1, q - 2)
                        elif NEXT[phase]:
                            cut_hi(NEXT[phase], 0, q - 2)
                        use(i, q)

                with act.Fori(0, bodies - 1) as i:
                    body(i, False)
                body(bodies - 1, True)

            cut_hi("in", 0, 0)
            cut_hi("in", 0, 1)
            act.wait_ge(red_done, 1)
            nc.scalar.activation(sin_cos[:], sin_cos[:], ACT.Sin).then_inc(trig_done, 1)

            def norm_hi(v):
                for k in range(KT):
                    copy(h_hi[:, k, :].rearrange("p (t c) -> p t c", t=TT), flipped(k), scale=vec[:, v + k:v + k + 1]
                         ).then_inc(hh_done, 1)

            act.wait_ge(norm_ps, 1)
            act.wait_ge(vec_done, 1)
            norm_hi(V_ATTN)
            act.wait_ge(gatew_in, 16)
            copy(gate_hi[:], gate_raw[:]).then_inc(gate_hi_done, 1)

            def keep_proj(i, q):
                n = 4 * i + q
                act.wait_ge(mm_done, n + 1 + MM_CREDIT)
                copy(proj[:, ds(n, 1), :], ps[:, q:q + 1, 0:SEQ]).then_inc(proj_done, 1)

            def keep_nsa(unit):
                act.wait_ge(otr_ps, unit + 1)
                tile, tq = UT + 2 * (unit // 2), unit % 2
                copy(proj[:, tile:tile + 2, P * tq:P * (tq + 1)],
                     ps[:, 7, 0:2 * P].rearrange("p (n c) -> p n c", n=2)).then_inc(nsa_done, 1)

            def proj_body(i, last=False):
                for q in range(4):
                    if q < 2:
                        cut_hi("in", i, q + 2)
                    elif not last:
                        cut_hi("in", i + 1, q - 2)
                    keep_proj(i, q)

            def keep_u(i, q):
                n = 4 * i + q
                act.wait_ge(mm_done, n + 1 + MM_CREDIT)
                copy(proj[:, n, :].rearrange("p (s c) -> p c s", s=STEP),
                     ps[:, q, 0:SEQ].rearrange("p (c s) -> p c s", s=STEP)).then_inc(proj_done, 1)

            cut_hi("in", 0, 2)
            keep_u(0, 0)
            act.wait_ge(cols_ps, 1)
            copy(ssm_cols[:], ps[:, 6, 0:7 * GROUPS].rearrange("p (n g) -> p n g", n=7)).then_inc(cols_done, 1)
            act.wait_ge(bias_ps, 1)
            copy(bias_sb[:], ps[0:HEADS, 5, 0:SPAN]).then_inc(bias_copied, 1)
            act.wait_ge(dcol_ps, 1)
            copy(dcol[:], ps[:, 4, 0:GROUPS]).then_inc(dcol_done, 1)
            cut_hi("in", 0, 3)
            keep_u(0, 1)
            act.wait_ge(gatet_ps, 1)
            nc.scalar.activation(gate_t[:], ps[0:NGATE, 7, 0:SEQ], ACT.Sigmoid).then_inc(gatet_done, 1)
            cut_hi("in", 1, 0)
            keep_u(0, 2)
            act.wait_ge(gate_ps, 1)
            copy(gates[:], ps[:, 7, SEQ:SEQ + TT * NGATE].rearrange("p (t n) -> p t n", t=TT)).then_inc(gate_done, 1)
            cut_hi("in", 1, 1)
            keep_u(0, 3)
            cut_hi("in", 1, 2)
            act.wait_ge(bc_ps, 1)
            copy(bs[:].rearrange("p g h -> p h g"), ps[:, 4:6, :].rearrange("p b (h g) -> p (b h) g", g=GROUPS)
                 ).then_inc(bc_done, 1)
            copy(cs[:].rearrange("p (t g) h -> p t (g h)", t=UT),
                 ps[:, 6:8, :].rearrange("p b (t c) -> p (b t) c", c=P)).then_inc(bc_done, 1)
            keep_u(1, 0)
            cut_hi("in", 1, 3)
            keep_u(1, 1)
            cut_hi("in", 2, 0)
            act.wait_ge(bcw_ps, 1)
            for n, t in enumerate((sw, cw)):
                copy(t[:].rearrange("p g h -> p (g h)"), ps[:, 4 + 2 * n:6 + 2 * n, :].rearrange("p b c -> p (b c)")
                     ).then_inc(bcw_done, 1)
            keep_u(1, 2)
            cut_hi("in", 2, 1)
            keep_u(1, 3)
            proj_body(2)

            def ssm_body(j, last):
                i = 3 + j
                for a in range(2):
                    it = 2 * j + a
                    act.wait_ge(ssm_a_ps, it + 1)
                    copy(msb[:].rearrange("p g h -> p (g h)"), ps[:, 6, 0:P]).then_inc(m_copied, 1)
                    copy(wt[:].rearrange("p g c -> p (g c)"), ps[:, 4:6, :].rearrange("p b c -> p (b c)")
                         ).then_inc(wt_done, 1)
                    act.wait_ge(s_ps, it + 1)
                    copy(ssb[:], ps[:, 6, P:P + G8 * NCH]).then_inc(s_done, 1)
                    act.wait_ge(toep_ps, it + 1)
                    for b in range(2):
                        copy(tp[:, :, :, 4 * b:4 * b + 4],
                             ps[:, 4 + b, :].rearrange("p (t g h) -> p g h t", t=4, g=G8)).then_inc(toep_done, 1)
                    for q in (2 * a, 2 * a + 1):
                        if q < 2:
                            cut_hi("in", i, q + 2)
                        elif not last:
                            cut_hi("in", i + 1, q - 2)
                        keep_proj(i, q)
                    act.wait_ge(y_ps, it + 1)
                    copy(proj[:, ds(it, 1), :], ps[:, 7:8, 256:512]).then_inc(y_done, 1)

            act.wait_ge(tables_done, 1)
            with act.Fori(0, 3) as j:
                ssm_body(j, False)
            ssm_body(3, True)

            act.wait_ge(y_in, 16 * UT)
            nc.scalar.activation(yg[:].rearrange("p t (c s) -> p t s c", s=STEP),
                                 proj[:, 0:UT, :].rearrange("p t (s c) -> p t s c", s=STEP),
                                 ACT.Gelu_apprx_tanh).then_inc(gelu_done, 1)
            act.wait_ge(gelu_done, 1)
            copy(y_hi[:], yg[:]).then_inc(yhi_done, 1)
            act.wait_ge(hid_ps, 1)
            nc.scalar.activation(hid_rows[:].rearrange("p n c -> p (n c)"), ps[0:NKV * NCMP, 0, 0:2 * P],
                                 ACT.Gelu_apprx_tanh).then_inc(hidrows_done, 1)
            act.wait_ge(hidt_ps, 1)
            copy(hid[:], ps[:, 2, 0:P].rearrange("p (n c) -> p n c", n=2)[:, :, 0:NKV * NCMP]).then_inc(hid_done, 1)
            act.wait_ge(kvc_ps, 1)
            copy(kct[:].rearrange("p g n -> p (g n)"), ps[0:DH, 1, 0:NKV * NCMP]).then_inc(kvc_done, 1)
            copy(vc[:].rearrange("p g d -> p (g d)"), ps[0:NCMP, 1, 128:128 + NKV * DH]).then_inc(kvc_done, 1)

            act.wait_ge(ylo_done, 1)
            cut_hi("glu", 0, 0)
            for at in range(STEPS):
                unit, n, gp, gl, tq, keys, ncm = parts_of(at)
                act.wait_ge(max_done, at + 1)
                for r in range(R):
                    nc.scalar.activation(pr[:, n, r, 0:keys], lg[:, n, r, 0:keys], ACT.Exp,
                                         bias=nmax[:, n, r:r + 1], accum_out=den[:, unit % 2, n, r:r + 1]
                                         ).then_inc(prob_done, 1)
                if n == 0:
                    act.wait_ge(maxc_done, unit + 1)
                    for r in range(R):
                        nc.scalar.activation(prc[:, r, 0:ncm], lgc[:, r, 0:ncm], ACT.Exp,
                                             bias=nmax[:, 2, r:r + 1], accum_out=den[:, unit % 2, 2, r:r + 1]
                                             ).then_inc(probc_done, 1)
                if at < STEPS - 1:
                    cut_hi("glu", (at + 1) // 4, (at + 1) % 4)
                else:
                    cut_hi("out", 0, 0)
                if at % 8 == 0:
                    act.wait_ge(vt_ps, gp + 1)
                    copy(vtok[:].rearrange("p n b c -> p (n b c)"), ps[:, 4, :]).then_inc(vtok_done, 1)
                act.wait_ge(pt_ps, at + 1)
                copy(pts[:, :, 0:tq + 1, :],
                     ps[:, 4:6, :].rearrange("p b (r s c) -> p (b r) s c", r=2, c=P)[:, :, 0:tq + 1, :]
                     ).then_inc(pt_done, 1)
                if n == 1:
                    if unit >= 2:
                        act.wait_ge(glu_done, unit - 1 + PAIR_CREDIT)
                    bias = V_BGLU + UT + unit
                    nc.scalar.activation(pair[:, unit % 2, :], ps[:, 1, 0:SEQ], ACT.Exp, scale=-1.0,
                                         bias=vec[:, bias:bias + 1]).then_inc(pair_act, 1)
                    act.wait_ge(ptc_ps, unit + 1)
                    copy(ptc[0:ncm].rearrange("p r c -> p (r c)"), ps[0:ncm, 6, :]).then_inc(ptc_done, 1)
                else:
                    if unit >= 2:
                        act.wait_ge(glu_done, unit - 1 + PAIR_CREDIT)
                    bias = V_BGLU + unit
                    nc.scalar.activation(a_sb[:, unit % 2, :], ps[:, 0, 0:SEQ], ACT.Identity,
                                         bias=vec[:, bias:bias + 1]).then_inc(a_act, 1)
                    if unit > 0:
                        keep_nsa(unit - 1)
            keep_nsa(STEPS // 2 - 1)

            cut_hi("out", 0, 1)
            run("out", lambda i, q: None)
            load_table(ACT.Sqrt)
            for t in range(TT):
                squares(2, t)
                root(2 + t, t, t + 1)
            cut_hi("ffn", 0, 0)
            cut_hi("ffn", 0, 1)
            load_table(ACT.Silu)
            act.wait_ge(norm_ps, 2)
            norm_hi(V_FFN)

            def silu(i, q):
                if q < 2:
                    act.wait_ge(mm_done, 4 * (FFN_0 + i) + q + 1 + MM_CREDIT)
                    act.wait_ge(ff_done, 2 * i + q - 1 + PAIR_CREDIT)
                    nc.scalar.activation(pair[:, q:q + 1, :], ps[:, q:q + 1, 0:SEQ], ACT.Silu).then_inc(pair_act, 1)

            run("ffn", silu)
            run("down", lambda i, q: None)

            load_table(ACT.Sqrt)
            for t in range(TT):
                squares(3, t)
                root(4 + t, t, t + 1)
            act.wait_ge(scales_done, 4)
            act.wait_ge(gained, 1)
            c = slice(D_MODEL // 2, D_MODEL)
            copy(ynorm[:, 0, c], ynorm[:, 0, c], scale=stat[:, 12:13]).then_inc(fin_act, 1)

        @block.vector
        def _(dve):
            step = Steps(dve, dve_step)

            def tt(o, a, b, op):
                return nc.vector.tensor_tensor(o, a, b, op)

            def tsc(o, a, s1, op0, s2=None, op1=None):
                return nc.vector.tensor_scalar(o, a, s1, s2, op0, op1) if op1 else nc.vector.tensor_scalar(
                    o, a, s1, None, op0)

            def stt(o, a, s, b, op0, op1):
                return nc.vector.scalar_tensor_tensor(out=o, in0=a, scalar=s, in1=b, op0=op0, op1=op1)

            nc.vector.sem_inc(lo_done, LO_CREDIT)
            nc.vector.sem_inc(glu_done, PAIR_CREDIT)
            nc.vector.sem_inc(ff_done, PAIR_CREDIT)
            nc.vector.memset(tab_rows[BUCKETS:BUCKETS + 1, :], MASK).then_inc(tab_ready, 1)
            dve.wait_ge(row_in, 80)
            dve.wait_ge(dt_done, 1)
            step.then(tsc(lam[:, 0, :], lam[:, 0, :], -1e-4, ALU.min))
            tsc(rnd[:, 0, :], lam[:, 0, :], dt_row[:, 1:2], ALU.mult).then_inc(ang_done, 1)
            step.then(tsc(ang[:, 0, :], lam[:, 1, :], dt_row[:, 1:2], ALU.mult))
            step.then(tsc(ang[:, 1, :], ang[:, 0, :], float(STEP), ALU.mult))
            def mean_first():
                dve.wait_ge(sumsq, TT)
                tsc(stat[:, 8:8 + TT], stat[:, 0:4 * TT:4], 1.0 / D_MODEL, ALU.mult, EPS, ALU.add).then_inc(std, 1)
                dve.wait_ge(rstd, 1)
                nc.vector.reciprocal(stat[:, 12:12 + TT], stat[:, 10:10 + TT]).then_inc(scales_done, 1)
                dve.wait_ge(scales_done, 1)

            def mean_square(n, t):
                dve.wait_ge(sumsq, TT + 8 * (n - 2) + 4 * (t + 1))
                total = stat[:, 8 + t:9 + t]
                step.then(nc.vector.reduce_sum(total, stat[:, 4 * t:4 * t + 4], AX_X))
                tsc(total, total, 1.0 / D_MODEL, ALU.mult, EPS, ALU.add).then_inc(std, 1)

            def inverse(n, t):
                dve.wait_ge(rstd, 2 * n - 2 + t)
                nc.vector.reciprocal(stat[:, 12 + t:13 + t], stat[:, 10 + t:11 + t]).then_inc(scales_done, 1)
                dve.wait_ge(scales_done, 2 * n - 2 + t)

            def scale_rows(dst, src, t):
                tsc(dst[:, t, :], src[:, t, :], stat[:, 12 + t:13 + t], ALU.mult).then_inc(xs_done, 1)

            mean_first()
            for t in range(TT):
                scale_rows(xs, xt, t)
            dve.wait_ge(mag_done, 1)
            step.then(tsc(rnd[:], ang[:], float(1 / (2 * np.pi)), ALU.mult, MAGIC, ALU.add))
            step.then(tsc(rnd[:], rnd[:], MAGIC, ALU.subtract))
            for k, piece in enumerate((TWO_PI_1, TWO_PI_2, TWO_PI_3)):
                step.then(stt(red[:], rnd[:], -piece, (red if k else ang)[:], ALU.mult, ALU.add))
            step.then(tsc(sin_cos[:, :, 0, :], red[:], -PI_IN, ALU.max, PI_IN, ALU.min))
            step.then(stt(sin_cos[:, :, 1, :], sin_cos[:, :, 0, :], -1.0, sin_cos[:, :, 0, :], ALU.mult, ALU.min))
            tsc(sin_cos[:, :, 1, :], sin_cos[:, :, 1, :], PI / 2, ALU.add).then_inc(red_done, 1)

            def cut_lo(phase, i, q):
                first, _, form = STREAM[phase]
                n = 4 * (first + i) + q
                if form == "rows":
                    dve.wait_ge(act_cut, (4 * OUT_BODIES if phase == "down" else 0) + 4 * i + q + 1)
                    src = (proj if phase == "out" else ff)[:, ds(4 * i + q, 1), :]
                    tt(act_lo[:, q:q + 1, :], src, act_hi[:, q:q + 1, :].bitcast(F32), ALU.subtract)
                dve.wait_ge(hi_done, n + 1)
                tt(part_tile(w_lo, form, q), raw_tile(form, q), part_tile(w_hi, form, q).bitcast(F32), ALU.subtract
                   ).then_inc(lo_done, 1)

            def run(phase, use):
                first, bodies, form = STREAM[phase]

                def body(i, last):
                    for q in range(4):
                        if q < 2:
                            cut_lo(phase, i, q + 2)
                        elif not last:
                            cut_lo(phase, i + 1, q - 2)
                        use(i, q)
                        if last and q >= 2 and NEXT[phase]:
                            cut_lo(NEXT[phase], 0, q - 2)

                with dve.Fori(0, bodies - 1) as i:
                    body(i, False)
                body(bodies - 1, True)

            def columns():
                dve.wait_ge(trig_done, 1)
                step(tt(ssm_rows[:, 0, :], mag[:], sin_cos[:, 0, 1, :], ALU.mult))
                step(tt(ssm_rows[:, 1, :], mag[:], sin_cos[:, 0, 0, :], ALU.mult))
                step(nc.vector.tensor_copy(ssm_rows[:, 4, :], sin_cos[:, 1, 1, :]))
                step(nc.vector.tensor_copy(ssm_rows[:, 5, :], sin_cos[:, 1, 0, :]))
                step(tt(ang[:, 0, :], lam[:, 0, :], lam[:, 0, :], ALU.mult))
                step.then(tt(ang[:, 1, :], lam[:, 1, :], lam[:, 1, :], ALU.mult))
                step(tsc(red[:, 0, :], ssm_rows[:, 0, :], -1.0, ALU.add))
                step.then(tt(red[:, 1, :], ang[:, 0, :], ang[:, 1, :], ALU.add))
                step(nc.vector.reciprocal(red[:, 1, :], red[:, 1, :]))
                step(tt(rnd[:, 0, :], red[:, 0, :], lam[:, 0, :], ALU.mult))
                step(tt(rnd[:, 1, :], ssm_rows[:, 1, :], lam[:, 1, :], ALU.mult))
                step(tt(ang[:, 0, :], ssm_rows[:, 1, :], lam[:, 0, :], ALU.mult))
                step.then(tt(ang[:, 1, :], red[:, 0, :], lam[:, 1, :], ALU.mult))
                step(tt(rnd[:, 0, :], rnd[:, 0, :], rnd[:, 1, :], ALU.add))
                step.then(tt(ang[:, 0, :], ang[:, 0, :], ang[:, 1, :], ALU.subtract))
                step(tt(ssm_rows[:, 2, :], rnd[:, 0, :], red[:, 1, :], ALU.mult))
                tt(ssm_rows[:, 3, :], ang[:, 0, :], red[:, 1, :], ALU.mult).then_inc(rows_done, 1)
                step.then(nc.vector.memset(d_wide[:], 0.0))
                dve.wait_ge(d_in, 16)
                nc.vector.tensor_copy(d_wide[:, :, STEP - 1], d_rows[:]).then_inc(wide_done, 1)

            cut_lo("in", 0, 0)
            cut_lo("in", 0, 1)

            def norm_lo(v, n):
                for k in range(KT):
                    dve.wait_ge(hh_done, KT * n + k // 4 * 4 + 4)
                    stt(h_lo[:, k, :].rearrange("p (t c) -> p t c", t=TT), flipped(k), vec[:, v + k:v + k + 1],
                        h_hi[:, k, :].bitcast(F32).rearrange("p (t c) -> p t c", t=TT), ALU.mult, ALU.subtract
                        ).then_inc(hl_done, 1)

            norm_lo(V_ATTN, 0)
            columns()
            dve.wait_ge(gate_hi_done, 1)
            tt(gate_lo[:], gate_raw[:], gate_hi[:].bitcast(F32), ALU.subtract).then_inc(gate_split, 1)

            for n in range(4):
                cut_lo("in", (2 + n) // 4, (2 + n) % 4)
            for n in range(3):
                cut_lo("in", 1 + (2 + n) // 4, (2 + n) % 4)
            dve.wait_ge(bcw_done, 2)
            dve.wait_ge(cols_done, 1)
            f_re = ssm_cols[:, 2, :].unsqueeze(2).broadcast_to([P, GROUPS, H])
            f_im = ssm_cols[:, 3, :].unsqueeze(2).broadcast_to([P, GROUPS, H])
            t1 = pb[:].rearrange("p g h s -> p (g h s)").rearrange("p (g h) -> p g h", h=H)
            t2 = pt[:].rearrange("p g h s -> p (g h s)").rearrange("p (g h) -> p g h", h=H)
            step(tt(t1, f_re, bs[:], ALU.mult))
            step.then(tt(t2, f_im, sw[:], ALU.mult))
            step(tt(bb[:], t1, t2, ALU.subtract))
            cut_lo("in", 2, 1)
            step.wait()
            step(tt(t1, f_re, sw[:], ALU.mult))
            step.then(tt(t2, f_im, bs[:], ALU.mult))
            tt(bbw[:], t1, t2, ALU.add).then_inc(bbw_done, 1)
            cut_lo("in", 2, 2)
            dve.wait_ge(pow_done, 1)
            for k in range(STEP):
                step(nc.vector.tensor_copy(inp_re[:, k, :], pow_re[:, STEP - 1 - k, :]))
                step(nc.vector.tensor_copy(inp_im[:, k, :], pow_im[:, STEP - 1 - k, :]))
            cut_lo("in", 2, 3)

            def inputs(i):
                g = ds(G8 * i, G8)
                shape = [P, G8, H, STEP]
                p_re = inp_re[:, :, g].rearrange("p k g -> p g k").unsqueeze(2).broadcast_to(shape)
                p_im = inp_im[:, :, g].rearrange("p k g -> p g k").unsqueeze(2).broadcast_to(shape)
                step(tt(pb[:], p_re, bb[:, g, :].unsqueeze(3).broadcast_to(shape), ALU.mult))
                step.then(tt(pt[:], p_im, bbw[:, g, :].unsqueeze(3).broadcast_to(shape), ALU.mult))
                tt(pb[:], pb[:], pt[:], ALU.subtract).then_inc(pb_done, 1)

            dve.wait_ge(bbw_done, 1)
            step.wait()
            inputs(0)
            cut_lo("in", 3, 0)
            dve.wait_ge(tables_done, 1)
            dve.wait_ge(dcol_done, 1)
            dve.wait_ge(delay_in, 48)
            step(tt(dmat[:], dcol[:].unsqueeze(2).broadcast_to([P, GROUPS, H]),
                    own_rows[:].unsqueeze(1).broadcast_to([P, GROUPS, H]), ALU.mult))
            cut_lo("in", 3, 1)
            step.then(nc.vector.memset(xp[:, :, 0:1], 0.0))

            def recurrence(j, a, last):
                i = 2 * j + a
                g = ds(G8 * i, G8)
                dve.wait_ge(m_copied, i + 1)
                tt(msb[:], msb[:], dmat[:, g, :], ALU.add).then_inc(m_done, 1)
                if not (last and a == 1):
                    dve.wait_ge(ssm_a_ps, i + 1)
                    inputs(i + 1)
                step.then(nc.vector.tensor_copy(decay[:], ssm_cols[:, 6, g].unsqueeze(2).broadcast_to([P, G8, NCH])))
                step(nc.vector.memset(decay[:, :, 0:1], 0.0))
                ps3 = ps[:, 7, 0:G8 * NCH].rearrange("p (g c) -> p g c", g=G8)
                dve.wait_ge(s_done, i + 1)
                step(tt(v1[:], rot_c[:, g, :], ssb[:].rearrange("p (g c) -> p g c", g=G8), ALU.mult))
                dve.wait_ge(swap_ps, i + 1)
                step.then(tt(v2[:], rot_s[:, g, :], ps3, ALU.mult))
                step.then(tt(v1[:], v1[:], v2[:], ALU.add))
                nc.vector.tensor_tensor_scan(zs[:], decay[:].rearrange("p g c -> p (g c)"),
                                             v1[:].rearrange("p g c -> p (g c)"), 0.0, ALU.mult, ALU.add
                                             ).then_inc(z_done, 1)
                dve.wait_ge(z_done, i + 1)
                step(tt(v1[:], rot_c[:, g, :], zs[:].rearrange("p (g c) -> p g c", g=G8), ALU.mult))
                if a == 0:
                    cut_lo("in", 3 + j, 2)
                elif not last:
                    cut_lo("in", 4 + j, 0)
                dve.wait_ge(zswap_ps, i + 1)
                step.then(tt(v2[:], rot_s[:, g, :], ps3, ALU.mult))
                tt(xp[:, :, 1:NCH], v1[:, :, 0:NCH - 1], v2[:, :, 0:NCH - 1], ALU.subtract).then_inc(xp_done, 1)
                if a == 0:
                    cut_lo("in", 3 + j, 3)
                elif not last:
                    cut_lo("in", 4 + j, 1)

            per = 2 * (2 + 2 + 3 + 2)
            n0 = step.n
            with dve.Fori(0, 3) as j:
                step.n = n0 + per * j
                recurrence(j, 0, False)
                recurrence(j, 1, False)
            step.n = n0 + per * 3
            recurrence(3, 0, True)
            recurrence(3, 1, True)

            step.wait()
            dve.wait_ge(xp_done, UT)
            dve.wait_ge(proj_done, 20 + PROJ_CREDIT)
            for n in range(2):
                for half in range(2):
                    for j in range(2):
                        rows = slice(DH * j, DH * (j + 1))
                        v = proj[DH * half:DH * (half + 1), 16 + 2 * n:18 + 2 * n, :]
                        tokens = bass.AP(v.tensor, v.offset + j, [v.ap[0], [SEQ, 2], [2, 16], [CMP_STRIDE, NCMP]])
                        pos = vec[rows, V_POS + 16 * n:V_POS + 16 * (n + 1)]
                        last = tt(kk[rows, n, :, half::2, :].rearrange("p k t i -> p t k i"), tokens,
                                  pos.unsqueeze(1).unsqueeze(3).broadcast_to([DH, 2, 16, NCMP]), ALU.add)
            last.then_inc(kk_done, 1)

            step.then(tsc(vec[:, V_BGLU + UT:V_POS], vec[:, V_BGLU + UT:V_POS], -1.0, ALU.mult))

            def logits(at):
                unit, n, gp, gl, tq, keys, ncm = parts_of(at)
                heads = slice(R * (unit // 2), R * (unit // 2 + 1))
                dve.wait_ge(sc_ps, at + 1)
                if at >= 2:
                    dve.wait_ge(prob_done, R * (at - 1))
                tt(lg[:, n, :, 0:keys], ps[:, 2:4, :].rearrange("p b (r s) -> p (b r) s", r=2)[:, :, 0:keys],
                   bt[:, heads, SEQ - keys:SEQ], ALU.add).then_inc(lg_done, 1)
                dve.wait_ge(lg_done, at + 1)
                step.then(nc.vector.reduce_max(nmax[:, n, :], lg[:, n, :, 0:keys], AX_X))
                tsc(nmax[:, n, :], nmax[:, n, :], -1.0, ALU.mult).then_inc(max_done, 1)
                if n == 0:
                    first = SEQ - keys + CMP_BLOCK - 1
                    dve.wait_ge(scc_ps, unit + 1)
                    if unit > 0:
                        dve.wait_ge(probc_done, R * unit)
                    step.then(tt(lgc[:, :, 0:ncm], ps[:, 6, 0:R * 16].rearrange("p (r s) -> p r s", r=R)[:, :, 0:ncm],
                                 bt[:, heads, first:SEQ:CMP_STRIDE], ALU.add))
                    step.then(nc.vector.reduce_max(nmax[:, 2, :], lgc[:, :, 0:ncm], AX_X))
                    tsc(nmax[:, 2, :], nmax[:, 2, :], -1.0, ALU.mult, -0.1 * MASK, ALU.min).then_inc(maxc_done, 1)

            def weigh(unit):
                group, tq = unit // 2, unit % 2
                d = den[:, unit % 2]
                step.then(tsc(d, d, 1e-30, ALU.max))
                step.then(nc.vector.reciprocal(d, d))
                gate = gates[:, tq, 3 * R * group:3 * R * (group + 1)].rearrange("p (r n) -> p n r", n=3)
                step(tt(wgt[:, 0:2], gate[:, 1:3], d[:, 0:2], ALU.mult))
                step.then(tt(wgt[:, 2:3], gate[:, 0:1], d[:, 2:3], ALU.mult))

            def combine(unit):
                dve.wait_ge(o_ps, unit + 1)
                step(tt(ot[:, 0:2], ps[:, 7, :].rearrange("p (n r d) -> p n r d", n=2, r=R),
                        wgt[:, 0:2].unsqueeze(3).broadcast_to([P, 2, R, DH]), ALU.mult))
                step.then(tt(ot[:, 2], ps[:, 6, P:P + R * DH].rearrange("p (r d) -> p r d", r=R),
                             wgt[:, 2].unsqueeze(2).broadcast_to([P, R, DH]), ALU.mult))
                step.then(tt(ot[:, 0], ot[:, 0], ot[:, 1], ALU.add))
                tt(ot[:, 0], ot[:, 0], ot[:, 2], ALU.add).then_inc(ot_done, 1)

            def keys_of(gp):
                for b in range(2):
                    tsc(qs[:, b::2, :], proj[DH * b:DH * (b + 1), UT + 4 * gp:UT + 4 * gp + 4, :], DH ** -0.5, ALU.mult)
                for n in range(2):
                    for gl in range(2):
                        nc.vector.tensor_copy(kt[:, n, gl, :], proj[DH * gl:DH * (gl + 1), 20 + 4 * n + gp, :])
                    last = nc.vector.tensor_copy(vt[:, n, :], proj[:, 22 + 4 * n + gp, :])
                last.then_inc(qk_done, 1)

            def product(unit):
                dve.wait_ge(a_act, unit + 1)
                dve.wait_ge(pair_act, unit + 1)
                gate = pair[:, unit % 2, :]
                step.then(tsc(gate, gate, 1.0, ALU.add))
                step.then(nc.vector.reciprocal(gate, gate))
                tt(proj[:, unit, :], a_sb[:, unit % 2, :], gate, ALU.mult).then_inc(glu_done, 1)

            def compressed_keys(gp):
                nc.vector.tensor_copy(kcg[:], kct[:, 2 * gp:2 * gp + 2, :]).then_inc(kcg_done, 1)

            def compressed_values(gp):
                nc.vector.tensor_copy(vcg[:], vc[:, 2 * gp:2 * gp + 2, :]).then_inc(vcg_done, 1)

            dve.wait_ge(proj_done, 4 * IN_BODIES + PROJ_CREDIT)
            keys_of(0)
            dve.wait_ge(yhi_done, 1)
            tt(y_lo[:], yg[:], y_hi[:].bitcast(F32), ALU.subtract).then_inc(ylo_done, 1)
            dve.wait_ge(bt_in, 16)
            dve.wait_ge(kvc_done, 2)
            compressed_keys(0)
            compressed_values(0)
            cut_lo("glu", 0, 0)
            logits(0)
            for at in range(STEPS):
                unit, n = at // 2, at % 2
                if at == 7:
                    keys_of(1)
                    compressed_keys(1)
                if at < STEPS - 1:
                    logits(at + 1)
                if n == 0 and unit > 0:
                    weigh(unit - 1)
                    combine(unit - 1)
                    product(unit - 1)
                if at == 8:
                    compressed_values(1)
                if at < STEPS - 1:
                    cut_lo("glu", (at + 1) // 4, (at + 1) % 4)
                else:
                    cut_lo("out", 0, 0)
            weigh(STEPS // 2 - 1)
            product(STEPS // 2 - 1)
            combine(STEPS // 2 - 1)

            def add_residual(n, t, b0=0, b1=4):
                phase = {2: "out", 3: "down"}[n]
                if t == 0:
                    dve.wait_ge(t0_done, n - 1)
                else:
                    dve.wait_ge(mm_done, 4 * (STREAM[phase][0] + STREAM[phase][1]) + MM_CREDIT)
                for b in range(b0, b1):
                    tt(xr[:, t, 512 * b:512 * (b + 1)], ps[:, 2 * b + t, :], xr[:, t, 512 * b:512 * (b + 1)],
                       ALU.add).then_inc(x1_done, 1)

            cut_lo("out", 0, 1)
            run("out", lambda i, q: None)
            dve.wait_ge(xr_in, 32)

            def add_residuals(n):
                add_residual(n, 0)
                add_residual(n, 1, 0, 2)
                mean_square(n, 0)
                add_residual(n, 1, 2, 4)
                inverse(n, 0)

            add_residuals(2)
            scale_rows(xs2, xr, 0)
            mean_square(2, 1)
            inverse(2, 1)
            scale_rows(xs2, xr, 1)
            cut_lo("ffn", 0, 0)
            cut_lo("ffn", 0, 1)
            norm_lo(V_FFN, 1)

            def swiglu(i, q):
                if q >= 2:
                    j = 2 * i + q - 2
                    dve.wait_ge(pair_act, UT + j + 1)
                    dve.wait_ge(mm_done, 4 * (FFN_0 + i) + q + 1 + MM_CREDIT)
                    tt(ff[:, ds(j, 1), :], ps[:, q:q + 1, 0:SEQ], pair[:, q - 2:q - 1, :], ALU.mult
                       ).then_inc(ff_done, 1)

            run("ffn", swiglu)
            run("down", lambda i, q: None)
            dve.wait_ge(gain_in, 16)
            add_residuals(3)

            def finish(t, b):
                c = slice(D_MODEL // 2 * b, D_MODEL // 2 * (b + 1))
                stt(ynorm[:, t, c], xr[:, t, c], stat[:, 12 + t:13 + t], gain[:, c], ALU.mult, ALU.mult
                    ).then_inc(fin_dve, 1)

            finish(0, 0)
            mean_square(3, 1)
            inverse(3, 1)
            finish(1, 0)
            finish(1, 1)

        @block.tensor
        def _(pe):
            def mm(o, a, b, start=True, stop=True):
                return nc.tensor.matmul(o, a, b, start=start, stop=stop)

            def flip(o, a):
                k = a.shape[0]
                return nc.tensor.transpose(o, a, ident[0:k, 0:k])

            nc.tensor.sem_inc(mm_done, MM_CREDIT)
            pe.wait_ge(const_in, 16)
            pe.wait_ge(vec_in, 80)
            flip(ps[:, 7, 0:NVEC], vec_rows[:]).then_inc(vec_ps, 1)
            def norm_flip(src, n):
                for t in range(TT):
                    pe.wait_ge(xs_done, TT * n + t + 1)
                    for k in range(KT):
                        last = flip(ps[:, k // 4 * 2 + t, P * (k % 4):P * (k % 4 + 1)],
                                    src[:, t, P * k:P * (k + 1)])
                last.then_inc(norm_ps, 1)

            pe.wait_ge(vec_done, 1)
            norm_flip(xs, 0)

            def column_tile(form, q, x_hi, x_lo, k0=0, k1=KT, bank=None, parts=None):
                hi, lo = part_tile(w_hi, form, q), part_tile(w_lo, form, q)
                o = ps[:, q if bank is None else bank, 0:SEQ]
                kn = UT if form == "glu" else KT
                for k in range(k0, min(k1, kn)):
                    if parts is not None:
                        pe.wait_ge(hl_done, parts + max(k + 1, 4))
                    mm(o, hi[:, k, :], x_hi[:, k, :], start=(k == 0), stop=False)
                    mm(o, hi[:, k, :], x_lo[:, k, :], start=False, stop=False)
                    last = mm(o, lo[:, k, :], x_hi[:, k, :], start=False, stop=(k == kn - 1))
                if k1 >= kn:
                    last.then_inc(mm_done, 1)

            def cut(phase, i, q):
                pe.wait_ge(lo_done, 4 * (STREAM[phase][0] + i) + q + 1 + LO_CREDIT)

            def proj_tile(i, q, k0=0, k1=KT):
                if k0 == 0:
                    cut("in", i, q)
                    pe.wait_ge(proj_done, 4 * i + q - 3 + PROJ_CREDIT)
                column_tile("cols", q, h_hi, h_lo, k0, k1)

            cut("in", 0, 0)
            pe.wait_ge(proj_done, PROJ_CREDIT)
            column_tile("cols", 0, h_hi, h_lo, parts=0)
            proj_tile(0, 1)
            pe.wait_ge(rows_done, 1)
            for n in range(7):
                last = flip(ps[:, 6, GROUPS * n:GROUPS * (n + 1)], ssm_rows[:, n, :])
            last.then_inc(cols_ps, 1)
            pe.wait_ge(tab_ready, 1)
            pe.wait_ge(tab_in, 32)
            mm(ps[0:HEADS, 5, 0:SPAN], tab_rows[:], hot[:]).then_inc(bias_ps, 1)
            pe.wait_ge(wide_done, 1)
            flip(ps[:, 4, 0:GROUPS], d_wide[:].rearrange("g h s -> g (h s)")).then_inc(dcol_ps, 1)
            pe.wait_ge(gate_split, 1)
            for k in range(KT):
                o = ps[0:NGATE, 7, 0:SEQ]
                mm(o, gate_hi[:, k, :], h_hi[:, k, :], start=(k == 0), stop=False)
                mm(o, gate_hi[:, k, :], h_lo[:, k, :], start=False, stop=False)
                last = mm(o, gate_lo[:, k, :], h_hi[:, k, :], start=False, stop=(k == KT - 1))
            last.then_inc(gatet_ps, 1)
            proj_tile(0, 2)
            pe.wait_ge(gatet_done, 1)
            for t in range(TT):
                last = flip(ps[:, 7, SEQ + NGATE * t:SEQ + NGATE * (t + 1)], gate_t[:, P * t:P * (t + 1)])
            last.then_inc(gate_ps, 1)
            proj_tile(0, 3)
            pe.wait_ge(b_in, 32)
            pe.wait_ge(cn_done, 1)
            pe.wait_ge(cols_done, 1)
            pe.wait_ge(bias_copied, 1)
            pe.wait_ge(dcol_done, 1)
            pe.wait_ge(gate_done, 1)
            for h in range(H):
                flip(ps[:, 4 + h // 8, GROUPS * (h % 8):GROUPS * (h % 8 + 1)],
                     b_rows[:, :, :, h].rearrange("g n p -> g (n p)"))
            for t in range(UT):
                last = flip(ps[:, 6 + t // 4, P * (t % 4):P * (t % 4 + 1)], cn[:, t, :])
            last.then_inc(bc_ps, 1)
            proj_tile(1, 0)
            proj_tile(1, 1)
            pe.wait_ge(bc_done, 2)
            pe.wait_ge(delay_in, 48)
            for n, t in enumerate((bs, cs)):
                for b in range(2):
                    flat = t[:].rearrange("p g h -> p (g h)")
                    last = mm(ps[:, 4 + 2 * n + b, :], swap[:], flat[:, 512 * b:512 * (b + 1)])
            last.then_inc(bcw_ps, 1)
            proj_tile(1, 2)
            proj_tile(1, 3)
            for q in range(4):
                proj_tile(2, q)
            pe.wait_ge(bcw_done, 2)
            pe.wait_ge(u_in, 16 * UT)

            with pe.Fori(0, 4) as j:
                for a in range(2):
                    i = 2 * j + a
                    pe.wait_ge(pb_done, i + 1)
                    for g in range(G8):
                        flip(ps[:, 4 + g // 4, P * (g % 4):P * (g % 4 + 1)], pb[:, g].rearrange("p h s -> p (h s)"))
                    for g in range(G8):
                        last = mm(ps[:, 6, H * g:H * (g + 1)], pb[:, g].rearrange("p h s -> p (h s)"),
                                  cs[:, ds(G8 * i + g, 1), :])
                    last.then_inc(ssm_a_ps, 1)
                    proj_tile(3 + j, 2 * a, 0, KT // 2)
                    pe.wait_ge(m_copied, i + 1)
                    pe.wait_ge(wt_done, i + 1)
                    for g in range(G8):
                        last = mm(ps[:, 6, P + NCH * g:P + NCH * (g + 1)], wt[:, g, :], uc[:, ds(i, 1), g, :])
                    last.then_inc(s_ps, 1)
                    pe.wait_ge(m_done, i + 1)
                    for t in range(STEP):
                        last = mm(ps[:, 4 + t // 4, P * (t % 4):P * (t % 4 + 1)], delay[:, t, :],
                                  msb[:].rearrange("p g h -> p (g h)"))
                    last.then_inc(toep_ps, 1)
                    proj_tile(3 + j, 2 * a, KT // 2, KT)
                    pe.wait_ge(s_done, i + 1)
                    mm(ps[:, 7, 0:G8 * NCH], swap[:], ssb[:]).then_inc(swap_ps, 1)
                    proj_tile(3 + j, 2 * a + 1, 0, KT // 2)
                    pe.wait_ge(z_done, i + 1)
                    mm(ps[:, 7, 0:G8 * NCH], swap[:], zs[:]).then_inc(zswap_ps, 1)
                    proj_tile(3 + j, 2 * a + 1, KT // 2, KT)
                    pe.wait_ge(xp_done, i + 1)
                    pe.wait_ge(toep_done, 2 * (i + 1))
                    pe.wait_ge(ca_done, i + 1)
                    for g in range(G8):
                        o = ps[:, 7, 256 + NCH * g:256 + NCH * (g + 1)]
                        mm(o, tp[:, g].rearrange("p h t -> p (h t)"), uc[:, ds(i, 1), g, :], stop=False)
                        last = mm(o, ca[:, g].rearrange("p h t -> p (h t)"), xp[:, g, :], start=False)
                    last.then_inc(y_ps, 1)
            pe.wait_ge(y_done, UT)
            pe.wait_ge(proj_done, 4 * IN_BODIES + PROJ_CREDIT)

            pe.wait_ge(cmp_in, 32)
            pe.wait_ge(w2_in, 32)
            pe.wait_ge(kk_done, 1)
            for n in range(2):
                for k in range(16):
                    last = mm(ps[0:NKV * NCMP, 0, P * n:P * (n + 1)], kk[:, n, k].rearrange("p g i -> p (g i)"),
                              w1[n][:, k, :], start=(k == 0), stop=(k == 15))
            last.then_inc(hid_ps, 1)
            pe.wait_ge(hidrows_done, 1)
            for n in range(2):
                last = flip(ps[:, 2, 64 * n:64 * n + NKV * NCMP], hid_rows[:, n, :])
            last.then_inc(hidt_ps, 1)
            pe.wait_ge(hid_done, 1)
            mm(ps[0:DH, 1, 0:NKV * NCMP], w2[:, 0, :], hid[:, 0, :])
            for g in range(NKV):
                last = mm(ps[0:NCMP, 1, 128 + DH * g:128 + DH * (g + 1)], hid[:, 1, NCMP * g:NCMP * (g + 1)],
                          w2[:, 1, :])
            last.then_inc(kvc_ps, 1)
            pe.wait_ge(kvc_done, 2)
            def scores(at):
                unit, n, gp, gl, tq, keys, ncm = parts_of(at)
                pe.wait_ge(qk_done, gp + 1)
                if at > 0:
                    pe.wait_ge(lg_done, at)
                for r in range(R):
                    last = mm(ps[:, 2 + r // 2, 256 * (r % 2):256 * (r % 2) + keys],
                              qs[:, R * gl + r, P * tq:P * (tq + 1)], kt[:, n, gl, 0:keys])
                last.then_inc(sc_ps, 1)
                if n == 0:
                    pe.wait_ge(kcg_done, gp + 1)
                    if unit > 1:
                        pe.wait_ge(ot_done, unit - 1)
                    for r in range(R):
                        last = mm(ps[:, 6, 16 * r:16 * r + ncm], qs[:, R * gl + r, P * tq:P * (tq + 1)],
                                  kcg[:, gl, 0:ncm])
                    last.then_inc(scc_ps, 1)

            def values(at):
                unit, n, gp, gl, tq, keys, ncm = parts_of(at)
                pe.wait_ge(pt_done, at + 1)
                if n == 0 and unit > 0:
                    pe.wait_ge(nsa_done, unit)
                for r in range(R):
                    for k in range(tq + 1):
                        last = mm(ps[:, 7, 256 * n + DH * r:256 * n + DH * (r + 1)], pts[:, r, k, :],
                                  vtok[:, n, k, DH * gl:DH * (gl + 1)], start=(k == 0), stop=(k == tq))
                if n == 1:
                    pe.wait_ge(ptc_done, unit + 1)
                    pe.wait_ge(vcg_done, gp + 1)
                    for r in range(R):
                        last = mm(ps[:, 6, P + DH * r:P + DH * (r + 1)], ptc[0:ncm, r, :], vcg[0:ncm, gl, :])
                    last.then_inc(o_ps, 1)

            def outputs(unit):
                pe.wait_ge(ot_done, unit + 1)
                for n in range(2):
                    last = flip(ps[:, 7, P * n:P * (n + 1)], ot[:, 0, 2 * n:2 * n + 2, :].rearrange("p r d -> p (r d)"))
                last.then_inc(otr_ps, 1)

            scores(0)
            for at in range(STEPS):
                unit, n, gp, gl, tq, keys, ncm = parts_of(at)
                if at < STEPS - 1 and at != 7:
                    scores(at + 1)
                if at > 0:
                    values(at - 1)
                if at % 8 == 0:
                    for m in range(2):
                        for k in range(TT):
                            last = flip(ps[:, 4, P * (2 * m + k):P * (2 * m + k + 1)], vt[:, m, P * k:P * (k + 1)])
                    last.then_inc(vt_ps, 1)
                cut("glu", at // 4, at % 4)
                if at == 0:
                    pe.wait_ge(ylo_done, 1)
                if unit > 0:
                    pe.wait_ge((a_act, pair_act)[n], unit)
                column_tile("glu", at % 4, y_hi, y_lo, bank=n)
                if at == 7:
                    scores(at + 1)
                if at % 8 == 0:
                    pe.wait_ge(vtok_done, gp + 1)
                pe.wait_ge(prob_done, R * (at + 1))
                for r in range(R):
                    for k in range(tq + 1):
                        last = flip(ps[:, 4 + r // 2, 256 * (r % 2) + P * k:256 * (r % 2) + P * (k + 1)],
                                    pr[:, n, r, P * k:P * (k + 1)])
                last.then_inc(pt_ps, 1)
                if n == 1:
                    pe.wait_ge(probc_done, R * (unit + 1))
                    if at < STEPS - 1:
                        pe.wait_ge(maxc_done, unit + 2)
                    for r in range(R):
                        last = flip(ps[0:ncm, 6, P * r:P * (r + 1)], prc[:, r, 0:ncm])
                    last.then_inc(ptc_ps, 1)
                elif unit > 0:
                    outputs(unit - 1)
            values(STEPS - 1)
            outputs(STEPS // 2 - 1)

            def row_phase(phase):
                _, bodies, form = STREAM[phase]

                passes = ((act_hi, w_hi), (act_hi, w_lo), (act_lo, w_hi))

                def token_tile(q, t, first=False, final=False):
                    for n, (a, w) in enumerate(passes):
                        for b in range(4):
                            last = mm(ps[:, 2 * b + t, :], a[:, q, P * t:P * (t + 1)],
                                      w[:, q % 2, 512 * b:512 * (b + 1)],
                                      start=(first and n == 0), stop=(final and n == 2))
                    return last

                def tile(i, q, first=False):
                    cut(phase, i, q)
                    for t in range(TT):
                        last = token_tile(q, t, first)
                    last.then_inc(mm_done, 1)

                for q in range(4):
                    tile(0, q, first=(q == 0))
                with pe.Fori(1, bodies - 1) as i:
                    for q in range(4):
                        tile(i, q)
                for q in range(3):
                    tile(bodies - 1, q)
                cut(phase, bodies - 1, 3)
                token_tile(3, 0, final=True).then_inc(t0_done, 1)
                token_tile(3, 1, final=True).then_inc(mm_done, 1)

            pe.wait_ge(glu_done, UT + PAIR_CREDIT)
            pe.wait_ge(nsa_done, 8)
            row_phase("out")
            norm_flip(xs2, 1)

            def ffn_tile(i, q, parts=None):
                cut("ffn", i, q)
                pe.wait_ge(ff_done, 2 * i + q % 2 - 1 + PAIR_CREDIT)
                column_tile("cols", q, h_hi, h_lo, parts=parts)

            for q in range(4):
                ffn_tile(0, q, KT if q == 0 else None)
            with pe.Fori(1, FFN_BODIES) as i:
                for q in range(4):
                    ffn_tile(i, q)
            pe.wait_ge(ff_done, D_FF // P + PAIR_CREDIT)
            row_phase("down")


_INS = ["x", "rpb_table", "attn_norm", "ffn_norm", "final_norm", "w_in", "ssm_a_re", "ssm_a_im", "ssm_log_dt",
        "ssm_b_re", "ssm_b_im", "ssm_c_re", "ssm_c_im", "ssm_d", "w_glu", "b_glu", "cmp_pos_k", "cmp_w1_k", "cmp_w2_k",
        "cmp_pos_v", "cmp_w1_v", "cmp_w2_v", "w_out", "w_ffn_gate", "w_ffn_up", "w_ffn_down"]


def selector_rows():
    rows = np.zeros((P, P * STEP + P + H), np.float32)
    h, s = np.divmod(np.arange(P), STEP)
    for t in range(STEP):
        to = s <= t
        rows[np.arange(P)[to] + STEP - 1 - t, P * t + np.arange(P)[to]] = 1
    k = np.arange(P)
    rows[k[NS:], P * STEP + k[NS:] - NS] = 1
    rows[k[:NS], P * STEP + k[:NS] + NS] = -1
    rows[k, P * (STEP + 1) + h] = 1
    return rows


def bucket_rows():
    dist = SEQ - 1 - np.arange(SPAN)
    n = np.maximum(dist, 1).astype(np.float32)
    exact = BUCKETS // 2
    large = exact + (np.log(n / np.float32(exact)) / np.float32(np.log(1024 / exact)) * np.float32(exact)
                     ).astype(np.int32)
    bucket = np.where(dist < exact, np.maximum(dist, 0), np.minimum(large, BUCKETS - 1))
    rows = np.zeros((BUCKETS + 1, SPAN), np.float32)
    valid = dist >= 0
    rows[bucket[valid], np.arange(SPAN)[valid]] = 1
    rows[BUCKETS, ~valid] = 1
    return rows


_CONST = [("selectors", selector_rows), ("onehot", bucket_rows)]


def kernel(**inputs):
    import concourse.bacc as _bacc
    from concourse.bass_utils import run_bass_kernel_spmd as _run

    nc = _bacc.Bacc("TRN2", target_bir_lowering=False, num_devices=1)
    arrays, args = {}, []
    given = [(name, np.ascontiguousarray(inputs[name])) for name in _INS]
    given += [(name, rows()) for name, rows in _CONST]
    for name, a in given:
        arrays[f"in_{name}_dram"] = a
        args.append(nc.dram_tensor(f"in_{name}_dram", a.shape, mybir.dt.from_np(a.dtype), kind="ExternalInput").ap())
    args.append(nc.dram_tensor("out_0_dram", (1, SEQ, D_MODEL), F32, kind="ExternalOutput").ap())
    build(nc, *args)
    r = _run(nc, [arrays], core_ids=[0])
    return r.results[0]["out_0_dram"]
```
